# Optimizing a Trainium2 kernel written in Bass

```python
import math
import jax
import jax.numpy as jnp
from jax import lax
import numpy as np
import jax, jax.numpy as jnp

D_MODEL = 1024
BATCH = 1
SEQ = 512
DEPTH = 1

CHUNK = 64
EPS = 1e-6
NEG_BIG = -1e30
HG_HEADS = 8
HG_DK = 128
HG_DV = 128
HG_QK = HG_HEADS * HG_DK
HG_W = HG_HEADS * HG_DV
ML_HEADS = 4
ML_DQK = 128
ML_DV = 256
ML_CONV = 4
ML_QK = ML_HEADS * ML_DQK
ML_W = ML_HEADS * ML_DV
MB_HEADS = 16
MB_P = 64
MB_GROUPS = 4
MB_N = 128
MB_CONV = 4
MB_W = MB_HEADS * MB_P
MB_CONV_DIM = MB_W + 2 * MB_GROUPS * MB_N
D_FF = 2816
FFN_CONV = 3
N_BRANCH = 3
IN_SPLITS = (HG_QK, HG_QK, HG_W, HG_W,
             2 * ML_QK, ML_W, 2 * ML_HEADS, ML_W,
             MB_W, MB_CONV_DIM, MB_HEADS,
             N_BRANCH * D_MODEL)
N_IN = sum(IN_SPLITS)


def rmsnorm(x, g):
    xf = x.astype(jnp.float32)
    y = xf * lax.rsqrt(jnp.mean(xf * xf, axis=-1, keepdims=True) + EPS)
    return (y * g.astype(jnp.float32)).astype(x.dtype)

def causal_dwconv(u, w, b):
    K = w.shape[0]
    S = u.shape[1]
    up = jnp.pad(u, ((0, 0), (K - 1, 0), (0, 0)))
    return sum(up[:, k:k + S] * w[k] for k in range(K)) + b

def to_chunks(t):
    B, S = t.shape[:2]
    t = t.astype(jnp.float32).reshape(B, S // CHUNK, CHUNK, *t.shape[2:])
    return jnp.moveaxis(t, 1, 0)

def from_chunks(t):
    t = jnp.moveaxis(t, 0, 1)
    return t.reshape(t.shape[0], -1, *t.shape[3:])

def causal_tri():
    return jnp.tril(jnp.ones((CHUNK, CHUNK), dtype=bool))

def hgrn2_scan(q, log_f, v):
    B, _, H, dk = q.shape
    dv = v.shape[-1]
    k = -jnp.expm1(log_f)
    tri = causal_tri()

    def step(state, inp):
        qc, lfc, kc, vc = inp
        b = jnp.cumsum(lfc, axis=1)
        diff = b[:, :, None] - b[:, None, :]
        decay = jnp.exp(jnp.where(tri[None, :, :, None, None], diff, NEG_BIG))
        attn = jnp.einsum('bthd,btshd->bhts', qc, decay * kc[:, None])
        o_intra = jnp.einsum('bhts,bshv->bthv', attn, vc)
        o_inter = jnp.einsum('bthd,bhdv->bthv', qc * jnp.exp(b), state)
        b_last = b[:, -1]
        k_dec = kc * jnp.exp(b_last[:, None] - b)
        state = jnp.exp(b_last)[..., None] * state + jnp.einsum('bshd,bshv->bhdv', k_dec, vc)
        return state, o_intra + o_inter

    s0 = jnp.zeros((B, H, dk, dv), jnp.float32)
    _, o = lax.scan(step, s0, (to_chunks(q), to_chunks(log_f), to_chunks(k), to_chunks(v)))
    return from_chunks(o)

def mlstm_scan(q, k, v, i_pre, log_f):
    B, _, H, dk = q.shape
    dv = v.shape[-1]
    tri = causal_tri()

    def step(carry, inp):
        C, n, m = carry
        qc, kc, vc, ic, fc = inp
        bh = jnp.moveaxis(jnp.cumsum(fc, axis=1), 1, 2)
        ih = jnp.moveaxis(ic, 1, 2)
        logD = jnp.where(tri, bh[..., :, None] - bh[..., None, :] + ih[..., None, :], NEG_BIG)
        log_inter = bh + m[..., None]
        m_t = jnp.maximum(jnp.max(logD, axis=-1), log_inter)
        s = jnp.einsum('bthd,bshd->bhts', qc, kc) * jnp.exp(logD - m_t[..., None])
        inter_w = jnp.exp(log_inter - m_t)
        inter_wt = jnp.swapaxes(inter_w, 1, 2)[..., None]
        num = jnp.einsum('bhts,bshv->bthv', s, vc) + jnp.einsum('bthd,bhdv->bthv', qc, C) * inter_wt
        den = jnp.sum(s, axis=-1) + jnp.einsum('bthd,bhd->bht', qc, n) * inter_w
        denom = jnp.maximum(jnp.abs(den), jnp.exp(-m_t))
        h = num / jnp.swapaxes(denom, 1, 2)[..., None]
        b_last = bh[..., -1]
        log_w = b_last[..., None] - bh + ih
        m_new = jnp.maximum(b_last + m, jnp.max(log_w, axis=-1))
        w = jnp.swapaxes(jnp.exp(log_w - m_new[..., None]), 1, 2)[..., None]
        dstate = jnp.exp(b_last + m - m_new)
        C = dstate[..., None, None] * C + jnp.einsum('bshd,bshv->bhdv', kc * w, vc)
        n = dstate[..., None] * n + jnp.sum(kc * w, axis=1)
        return (C, n, m_new), h

    c0 = (jnp.zeros((B, H, dk, dv), jnp.float32), jnp.zeros((B, H, dk), jnp.float32),
          jnp.zeros((B, H), jnp.float32))
    _, h = lax.scan(step, c0, (to_chunks(q), to_chunks(k), to_chunks(v), to_chunks(i_pre), to_chunks(log_f)))
    return from_chunks(h)

def ssd_scan(x, dt, A, Bm, Cm):
    B, _, H, P = x.shape
    N = Bm.shape[-1]
    hpg = H // Bm.shape[2]
    tri = causal_tri()
    A = A.astype(jnp.float32)

    def step(state, inp):
        xc, dtc, Bc, Cc = inp
        cum = jnp.moveaxis(jnp.cumsum(dtc * A, axis=1), 1, 2)
        L = jnp.exp(jnp.where(tri, cum[..., :, None] - cum[..., None, :], NEG_BIG))
        CB = jnp.repeat(jnp.einsum('btgn,bsgn->bgts', Cc, Bc), hpg, axis=1)
        xdt = xc * dtc[..., None]
        y_intra = jnp.einsum('bhts,bshp->bthp', CB * L, xdt)
        Ch = jnp.repeat(Cc, hpg, axis=2)
        y_inter = jnp.einsum('bthn,bhpn->bthp', Ch, state) * jnp.swapaxes(jnp.exp(cum), 1, 2)[..., None]
        dec = jnp.swapaxes(jnp.exp(cum[..., -1:] - cum), 1, 2)[..., None]
        Bh = jnp.repeat(Bc, hpg, axis=2)
        state = jnp.exp(cum[..., -1])[..., None, None] * state + jnp.einsum('bshn,bshp->bhpn', Bh * dec, xdt)
        return state, y_intra + y_inter

    s0 = jnp.zeros((B, H, P, N), jnp.float32)
    _, y = lax.scan(step, s0, (to_chunks(x), to_chunks(dt), to_chunks(Bm), to_chunks(Cm)))
    return from_chunks(y)

def first_inputs(seed: int = 0) -> dict:
    key = jax.random.key(seed)
    ks = jax.random.split(key, 32)
    f32 = jnp.float32

    def nrm(k, shape, scale):
        return jax.random.normal(k, shape, f32) * scale

    def gain(k, shape):
        return 1.0 + 0.05 * jax.random.normal(k, shape, f32)

    dt0 = jnp.exp(jax.random.uniform(ks[12], (DEPTH, MB_HEADS), f32, math.log(1e-3), math.log(1e-1)))
    ml_f_bias = jnp.linspace(3.0, 6.0, ML_HEADS, dtype=f32)[None] + nrm(ks[7], (DEPTH, ML_HEADS), 0.1)
    ml_i_bias = nrm(ks[8], (DEPTH, ML_HEADS), 0.1)
    return {
        "x": jax.random.normal(ks[0], (BATCH, SEQ, D_MODEL), f32),
        "norm1_g": gain(ks[1], (DEPTH, D_MODEL)),
        "w_in": nrm(ks[2], (DEPTH, D_MODEL, N_IN), D_MODEL ** -0.5),
        "hg_lb_logits": nrm(ks[3], (DEPTH, HG_QK), 0.1),
        "hg_norm_g": gain(ks[4], (DEPTH, HG_DV)),
        "ml_conv_w": nrm(ks[5], (DEPTH, ML_CONV, 2 * ML_QK), ML_CONV ** -0.5),
        "ml_conv_b": nrm(ks[6], (DEPTH, 2 * ML_QK), 0.02),
        "ml_gate_b": jnp.concatenate([ml_i_bias, ml_f_bias], axis=-1),
        "ml_norm_g": gain(ks[9], (DEPTH, ML_DV)),
        "mb_conv_w": nrm(ks[10], (DEPTH, MB_CONV, MB_CONV_DIM), MB_CONV ** -0.5),
        "mb_conv_b": nrm(ks[11], (DEPTH, MB_CONV_DIM), 0.02),
        "mb_dt_bias": dt0 + jnp.log(-jnp.expm1(-dt0)),
        "mb_a_log": jnp.log(jax.random.uniform(ks[13], (DEPTH, MB_HEADS), f32, 1.0, 16.0)),
        "mb_d": gain(ks[14], (DEPTH, MB_HEADS)),
        "mb_norm_g": gain(ks[15], (DEPTH, MB_W)),
        "w_br_hg": nrm(ks[16], (DEPTH, HG_W, D_MODEL), HG_W ** -0.5),
        "w_br_ml": nrm(ks[17], (DEPTH, ML_W, D_MODEL), ML_W ** -0.5),
        "w_br_mb": nrm(ks[18], (DEPTH, MB_W, D_MODEL), MB_W ** -0.5),
        "w_out": nrm(ks[19], (DEPTH, D_MODEL, D_MODEL), D_MODEL ** -0.5),
        "norm2_g": gain(ks[20], (DEPTH, D_MODEL)),
        "w_up": nrm(ks[21], (DEPTH, D_MODEL, 2 * D_FF), D_MODEL ** -0.5),
        "ffn_conv_w": nrm(ks[22], (DEPTH, FFN_CONV, 2 * D_FF), FFN_CONV ** -0.5),
        "ffn_conv_b": nrm(ks[23], (DEPTH, 2 * D_FF), 0.02),
        "w_down": nrm(ks[24], (DEPTH, D_FF, D_MODEL), D_FF ** -0.5),
        "final_g": gain(ks[25], (D_MODEL,)),
    }

def first_block(x, norm1_g, w_in, hg_lb_logits, hg_norm_g, ml_conv_w, ml_conv_b, ml_gate_b, ml_norm_g,
              mb_conv_w, mb_conv_b, mb_dt_bias, mb_a_log, mb_d, mb_norm_g, w_br_hg, w_br_ml, w_br_mb,
              w_out, norm2_g, w_up, ffn_conv_w, ffn_conv_b, w_down, final_g):
    B, S, _ = x.shape
    f32 = jnp.float32
    lb_p = jax.nn.softmax(hg_lb_logits.astype(f32), axis=0)
    lbs = jnp.cumsum(lb_p, axis=0) - lb_p[0]
    split_at = [int(c) for c in np.cumsum(IN_SPLITS)[:-1]]

    for l in range(DEPTH):
        h = rmsnorm(x, norm1_g[l])
        (hg_q, hg_f, hg_i, hg_g, ml_qk, ml_v, ml_if, ml_o,
         mb_z, mb_xbc, mb_dt, gate_pre) = jnp.split(h @ w_in[l], split_at, axis=-1)

        lb = lbs[l]
        log_f = jnp.log(lb + (1.0 - lb) * jax.nn.sigmoid(hg_f.astype(f32)))
        o_hg = hgrn2_scan(jax.nn.silu(hg_q).reshape(B, S, HG_HEADS, HG_DK),
                          log_f.reshape(B, S, HG_HEADS, HG_DK),
                          hg_i.reshape(B, S, HG_HEADS, HG_DV))
        y_hg = (rmsnorm(o_hg, hg_norm_g[l]).reshape(B, S, HG_W)
                * jax.nn.silu(hg_g.astype(f32))).astype(x.dtype)

        qk = jax.nn.silu(causal_dwconv(ml_qk, ml_conv_w[l], ml_conv_b[l]))
        q_m, k_m = jnp.split(qk, 2, axis=-1)
        gb = ml_gate_b[l]
        i_pre = ml_if[..., :ML_HEADS] + gb[:ML_HEADS]
        log_f_m = jax.nn.log_sigmoid((ml_if[..., ML_HEADS:] + gb[ML_HEADS:]).astype(f32))
        h_ml = mlstm_scan(q_m.reshape(B, S, ML_HEADS, ML_DQK),
                          k_m.reshape(B, S, ML_HEADS, ML_DQK) * (ML_DQK ** -0.5),
                          ml_v.reshape(B, S, ML_HEADS, ML_DV), i_pre, log_f_m)
        y_ml = (rmsnorm(h_ml, ml_norm_g[l]).reshape(B, S, ML_W)
                * jax.nn.sigmoid(ml_o.astype(f32))).astype(x.dtype)

        xbc = jax.nn.silu(causal_dwconv(mb_xbc, mb_conv_w[l], mb_conv_b[l]))
        xs, Bm, Cm = jnp.split(xbc, [MB_W, MB_W + MB_GROUPS * MB_N], axis=-1)
        xs = xs.reshape(B, S, MB_HEADS, MB_P)
        dt = jax.nn.softplus((mb_dt + mb_dt_bias[l]).astype(f32))
        A = -jnp.exp(mb_a_log[l].astype(f32))
        y_ssd = ssd_scan(xs, dt, A, Bm.reshape(B, S, MB_GROUPS, MB_N), Cm.reshape(B, S, MB_GROUPS, MB_N))
        y_ssd = y_ssd + mb_d[l].astype(f32)[:, None] * xs
        yz = (y_ssd.reshape(B, S, MB_W) * jax.nn.silu(mb_z.astype(f32))).reshape(B, S, MB_GROUPS, MB_W // MB_GROUPS)
        y_mb = rmsnorm(yz, mb_norm_g[l].reshape(MB_GROUPS, MB_W // MB_GROUPS)).reshape(B, S, MB_W).astype(x.dtype)

        gates = jax.nn.sigmoid(gate_pre).reshape(B, S, N_BRANCH, D_MODEL)
        mixed = (gates[:, :, 0] * (y_hg @ w_br_hg[l])
                 + gates[:, :, 1] * (y_ml @ w_br_ml[l])
                 + gates[:, :, 2] * (y_mb @ w_br_mb[l]))
        x = x + mixed @ w_out[l]

        u = causal_dwconv(rmsnorm(x, norm2_g[l]) @ w_up[l], ffn_conv_w[l], ffn_conv_b[l])
        u_g, u_v = jnp.split(u, 2, axis=-1)
        x = x + (jax.nn.silu(u_g) * u_v) @ w_down[l]

    return rmsnorm(x, final_g)


MIX_WIDTH = D_MODEL
CONV_WIDTH = MIX_WIDTH // 2
ATTN_HEADS = 8
HEAD_DIM = (MIX_WIDTH - CONV_WIDTH) // ATTN_HEADS
ATTN_WIDTH = ATTN_HEADS * HEAD_DIM
CONV_K = 3
DILATED_CONFIGS = ((128, 1), (512, 4), (2048, 16))
Q_BLOCK = 128
NUM_BUCKETS = 32
MAX_DISTANCE = 1024
NEG = -1e30


def rmsnorm_2(x, w):
    xf = x.astype(jnp.float32)
    y = xf * lax.rsqrt(jnp.mean(xf * xf, axis=-1, keepdims=True) + EPS)
    return (y * w.astype(jnp.float32)).astype(x.dtype)

def t5_bucket(rel):
    half_b = NUM_BUCKETS // 2
    max_exact = half_b // 2
    ret = jnp.where(rel > 0, half_b, 0)
    n = jnp.abs(rel)
    nf = jnp.maximum(n, 1).astype(jnp.float32)
    large = max_exact + (jnp.log(nf / max_exact) / math.log(MAX_DISTANCE / max_exact)
                         * (half_b - max_exact)).astype(jnp.int32)
    large = jnp.minimum(large, half_b - 1)
    return ret + jnp.where(n < max_exact, n, large)

def dilated_window_attention(q, k, v, rel_bias, window, dilation):
    b, s, nh, dh = q.shape
    half = window // (2 * dilation)
    length = s // dilation
    n_blk = -(-length // Q_BLOCK)
    padded = n_blk * Q_BLOCK
    kb_len = Q_BLOCK + 2 * half
    bd = b * dilation

    def to_residue(t):
        t = t.reshape(b, length, dilation, nh, dh)
        return t.transpose(0, 2, 3, 1, 4).reshape(bd, nh, length, dh)

    qr = jnp.pad(to_residue(q), ((0, 0), (0, 0), (0, padded - length), (0, 0)))
    qr = qr.reshape(bd, nh, n_blk, Q_BLOCK, dh)
    pad_kv = ((0, 0), (0, 0), (half, padded - length + half), (0, 0))
    kr = jnp.pad(to_residue(k), pad_kv)
    vr = jnp.pad(to_residue(v), pad_kv)

    key_idx = jnp.arange(n_blk)[:, None] * Q_BLOCK + jnp.arange(kb_len)[None, :]
    kblk = kr[:, :, key_idx]
    vblk = vr[:, :, key_idx]

    logits = jnp.einsum('bhnqd,bhnkd->bhnqk', qr, kblk,
                        preferred_element_type=jnp.float32) * (dh ** -0.5)

    rel = jnp.arange(kb_len)[None, :] - half - jnp.arange(Q_BLOCK)[:, None]
    band = jnp.abs(rel) <= half
    buckets = t5_bucket(jnp.clip(rel, -half, half) * dilation)
    bias = rel_bias[buckets].astype(jnp.float32).transpose(2, 0, 1)
    key_pos = key_idx - half
    key_ok = (key_pos >= 0) & (key_pos < length)
    mask = band[None, :, :] & key_ok[:, None, :]
    logits = jnp.where(mask[None, None], logits + bias[None, :, None], NEG)

    m = jnp.max(logits, axis=-1, keepdims=True)
    p = jnp.exp(logits - m)
    denom = jnp.sum(p, axis=-1, keepdims=True)
    o = jnp.einsum('bhnqk,bhnkd->bhnqd', p, vblk.astype(jnp.float32)) / denom
    lse = (m + jnp.log(denom))[..., 0]

    o = o.reshape(bd, nh, padded, dh)[:, :, :length]
    o = o.reshape(b, dilation, nh, length, dh).transpose(0, 3, 1, 2, 4).reshape(b, s, nh, dh)
    lse = lse.reshape(bd, nh, padded)[:, :, :length]
    lse = lse.reshape(b, dilation, nh, length).transpose(0, 3, 1, 2).reshape(b, s, nh)
    return o, lse

def short_gated_conv(u, gate_b, gate_c, conv_w, conv_b):
    pad = (CONV_K - 1) // 2
    z = lax.conv_general_dilated(gate_c * u, conv_w[:, None, :].astype(u.dtype),
                                 window_strides=(1,), padding=((pad, pad),),
                                 dimension_numbers=('NWC', 'WIO', 'NWC'),
                                 feature_group_count=CONV_WIDTH)
    return gate_b * (z + conv_b.astype(u.dtype))

def second_inputs(seed: int = 0) -> dict:
    key = jax.random.key(seed)
    ks = jax.random.split(key, 9)
    proj_cols = 4 * CONV_WIDTH + 4 * ATTN_WIDTH
    x = jax.random.normal(ks[0], (BATCH, SEQ, D_MODEL), jnp.float32)
    norm_w = 1.0 + 0.05 * jax.random.normal(ks[1], (D_MODEL,), jnp.float32)
    w_in = jax.random.normal(ks[2], (D_MODEL, proj_cols), jnp.float32) * D_MODEL ** -0.5
    conv_w = jax.random.normal(ks[3], (CONV_K, CONV_WIDTH), jnp.float32) * CONV_K ** -0.5
    conv_b = 0.01 * jax.random.normal(ks[4], (CONV_WIDTH,), jnp.float32)
    q_norm_w = 1.0 + 0.05 * jax.random.normal(ks[5], (HEAD_DIM,), jnp.float32)
    k_norm_w = 1.0 + 0.05 * jax.random.normal(ks[6], (HEAD_DIM,), jnp.float32)
    rel_bias = 0.5 * jax.random.normal(ks[7], (NUM_BUCKETS, ATTN_HEADS), jnp.float32)
    w_out = jax.random.normal(ks[8], (MIX_WIDTH, D_MODEL), jnp.float32) * MIX_WIDTH ** -0.5
    return {"x": x, "norm_w": norm_w, "w_in": w_in, "conv_w": conv_w, "conv_b": conv_b,
            "q_norm_w": q_norm_w, "k_norm_w": k_norm_w, "rel_bias": rel_bias, "w_out": w_out}

def second_block(x, norm_w, w_in, conv_w, conv_b, q_norm_w, k_norm_w, rel_bias, w_out):
    b, s, _ = x.shape
    for _layer in range(DEPTH):
        h = rmsnorm_2(x, norm_w)
        proj = jnp.einsum('bsd,de->bse', h, w_in)
        c, a = CONV_WIDTH, ATTN_WIDTH
        splits = [c, 2 * c, 3 * c, 4 * c, 4 * c + a, 4 * c + 2 * a, 4 * c + 3 * a]
        u, g_b, g_c, z_conv, q, k, v, z_attn = jnp.split(proj, splits, axis=-1)

        y_conv = short_gated_conv(u, g_b, g_c, conv_w, conv_b) * jax.nn.silu(z_conv)

        q = rmsnorm_2(q.reshape(b, s, ATTN_HEADS, HEAD_DIM), q_norm_w)
        k = rmsnorm_2(k.reshape(b, s, ATTN_HEADS, HEAD_DIM), k_norm_w)
        v = v.reshape(b, s, ATTN_HEADS, HEAD_DIM)
        outs, lses = [], []
        for window, dilation in DILATED_CONFIGS:
            o_i, lse_i = dilated_window_attention(q, k, v, rel_bias, window, dilation)
            outs.append(o_i)
            lses.append(lse_i)
        mix = jax.nn.softmax(jnp.stack(lses, axis=0), axis=0)
        o = jnp.einsum('gbsh,gbshd->bshd', mix, jnp.stack(outs, axis=0))
        y_attn = o.reshape(b, s, ATTN_WIDTH).astype(x.dtype) * jax.nn.silu(z_attn)

        y = jnp.concatenate([y_conv, y_attn], axis=-1)
        x = x + jnp.einsum('bse,ed->bsd', y, w_out)
    return x


def setup_inputs(seed=0):
    out = dict(first_inputs(seed))
    for name, value in second_inputs(seed + 1).items():
        if name != "x":
            out[name + "_2"] = value
    return out


def reference(
    x, norm1_g, w_in, hg_lb_logits, hg_norm_g, ml_conv_w, ml_conv_b, ml_gate_b, ml_norm_g,
    mb_conv_w, mb_conv_b, mb_dt_bias, mb_a_log, mb_d, mb_norm_g, w_br_hg, w_br_ml, w_br_mb,
    w_out, norm2_g, w_up, ffn_conv_w, ffn_conv_b, w_down, final_g, norm_w_2, w_in_2, conv_w_2,
    conv_b_2, q_norm_w_2, k_norm_w_2, rel_bias_2, w_out_2,
):
    x = first_block(
        x, norm1_g, w_in, hg_lb_logits, hg_norm_g, ml_conv_w, ml_conv_b, ml_gate_b, ml_norm_g,
        mb_conv_w, mb_conv_b, mb_dt_bias, mb_a_log, mb_d, mb_norm_g, w_br_hg, w_br_ml, w_br_mb,
        w_out, norm2_g, w_up, ffn_conv_w, ffn_conv_b, w_down, final_g,
    )
    return second_block(
        x, norm_w_2, w_in_2, conv_w_2, conv_b_2, q_norm_w_2, k_norm_w_2, rel_bias_2, w_out_2,
    )


_drawn_inputs = setup_inputs


def setup_inputs(seed=0):
    import zlib

    import numpy as np

    out = dict(_drawn_inputs(seed))
    spreads = {}
    factors = {'hg_norm_g': 3.139,
     'ml_conv_b': 8.0,
     'ml_norm_g': 3.362,
     'mb_conv_b': 3.597,
     'ffn_conv_b': 3.73,
     'conv_b_2': 8.0,
     'q_norm_w_2': 8.0,
     'k_norm_w_2': 8.0,
     'rel_bias_2': 2.771}
    for name, (base, spread) in spreads.items():
        noise = np.random.default_rng([zlib.crc32(name.encode()), seed]).standard_normal(out[name].shape)
        drawn = base * np.exp(spread * noise) if base else spread * noise
        out[name] = jnp.asarray(drawn.astype(out[name].dtype))
    for name, factor in factors.items():
        out[name] = (out[name] * factor).astype(out[name].dtype)
    return out
```

```python
from contextlib import ExitStack

import numpy as np

import concourse.bass as bass
from concourse import mybir

P = 128
T = 512
NB = T // P
D = 1024
KT = D // P
F32 = mybir.dt.float32
F32R = mybir.dt.float32r
U32 = mybir.dt.uint32
ALU = mybir.AluOpType
ACT = mybir.ActivationFunctionType
AX_X = mybir.AxisListType.X
EPS = 1e-6
NEG = -1e30

HG_HEADS, ML_HEADS, MB_GROUPS, MB_HEADS = 8, 4, 4, 16
D_FF = 2816
NF = D_FF // P
AT_HEADS, AT_DH = 8, 64

C_HGQ, C_HGF, C_HGI, C_HGG = 0, 1024, 2048, 3072
C_MLQ, C_MLK, C_MLV, C_MLIF, C_MLO = 4096, 4608, 5120, 6144, 6152
C_MBZ, C_MBX, C_MBDT, C_GATE = 7176, 8200, 10248, 10264

J_SMALL = 0
J_HG = 1
J_ML0 = J_HG + 4 * HG_HEADS
J_G0 = J_ML0 + 6
J_ML1 = J_G0 + 16
J_MB0 = J_ML1 + 18
J_G1 = J_MB0 + 6
J_MB1 = J_G1 + 16
J_G2 = J_MB1 + 18
J_O = J_G2 + 16
J_UP = J_O + 8
J_DN = J_UP + 2 * NF
DN_CHUNKS = (8, 8, 6)
J_CV = J_DN + 24
J_AT = J_CV + 16
J_O2 = J_AT + 16
N_SLABS = J_O2 + 8
DN_SHIFT = 16

K_ID, K_NID, K_ONES, K_BD, K_SELI, K_NSELF, K_CLAMP = (P * i for i in range(7))
K_LMASK = 7 * P
K_HGMASK = K_LMASK + 7 * P
K_RMASK = K_HGMASK + T
K_SIGN = K_RMASK + T
N_CONST = K_SIGN + 1

_PAR = [("norm1", 8), ("norm2", 8), ("final", 8), ("normw2", 8), ("lb", 8), ("hgg", 1), ("mlcw", 32), ("mlcb", 8),
        ("mlg", 2), ("mbcw", 64), ("mbcb", 16), ("mbg", 8), ("mbd", 8), ("fcw", 132), ("fcb", 44), ("cw2", 12),
        ("cb2", 4), ("qn", 1), ("kn", 1), ("rowb", 1), ("alog", 1), ("rel", 8)]
PAR = {}
N_PAR = 0
for _n, _w in _PAR:
    PAR[_n] = N_PAR
    N_PAR += _w

ROW_DT, ROW_I, ROW_F = 0, 32, 64
W_BIAS = 896
W_LINE = 1024


def ml_slab(u):
    return J_ML0 if u == 0 else J_ML1 + 6 * (u - 1)


def mb_slab(g):
    return J_MB0 if g == 0 else J_MB1 + 6 * (g - 1)


def lin(c, it, k):
    return c if it is None else it * k + c


def wait(eng, sem, n):
    if not isinstance(n, int) or n > 0:
        eng.wait_ge(sem, n)


def tiles_before(part, n):
    return {0: [[], [], [], []], 4: [[0], [1], [2], [3]], 6: [[0], [1, 2], [3], [4, 5]]}[n][part]


def build(nc, slabs, x, par_d, const_d, onehot_d, bias_scratch, out):
    with ExitStack() as ctx:
        start = -(-nc.sbuf_base // 64) * 64

        def arena(at):
            pos = [at]

            def take(name, shape, dt=F32):
                n = 4
                for s in shape[1:]:
                    n *= s
                pos[0] = -(-pos[0] // 64) * 64
                t = nc.alloc_sbuf_tensor_at(name, shape, dt, offset=pos[0])
                pos[0] += n
                assert pos[0] <= nc.sbuf_usable_end, (name, pos[0])
                return t
            return take, pos

        sb, sb_pos = arena(start)
        raw = sb("raw", [P, 4, KT, P])
        wh = sb("wh", [P, 2, KT, P], F32R)
        wl = sb("wl", [P, 2, KT, P], F32R)
        xT = sb("xT", [P, KT, T])
        hh = sb("hh", [P, KT, T], F32R)
        hl = sb("hl", [P, KT, T], F32R)
        con = sb("con", [P, N_CONST])
        par = sb("par", [P, N_PAR])
        zero = sb("zero", [P, 1])
        tick = sb("tick", [P, 1])
        lbc = sb("lbc", [P, 8])
        lbt = sb("lbt", [P, 3, 8])
        sb_pos[0] = -(-sb_pos[0] // 64) * 64
        y_at = sb_pos[0]
        yh = sb("yh", [P, KT, T], F32R)
        yl = sb("yl", [P, KT, T], F32R)
        area = sb_pos[0]

        mx, mx_pos = arena(area)
        mixed = mx("mixed", [P, KT, T])
        unit = [mx(f"unit{i}", [P, 6, T]) for i in range(2)]
        cum = mx("cum", [P, T])
        rnm = mx("rnm", [P, T])
        acol = mx("acol", [P, NB, ML_HEADS])
        dtc = mx("dtc", [P, NB, MB_HEADS])
        ncc = mx("ncc", [P, NB, MB_HEADS])
        totb = mx("totb", [P, NB, MB_HEADS])
        dend = mx("dend", [P, 6, MB_HEADS])
        scratch = mx_pos[0]

        psum = [ctx.enter_context(nc.psum_tensor(f"bank{i}", [P, T], F32)) for i in range(8)]
        acc = psum[:2]
        b2, b3, b4, b5, b6, b7 = psum[2:]

        names = """params_in x_in onehot_in slab_hi slab_split slab_used acc_free0 acc_free1 zero_set
            pro_tr pro_xT nrm_sq nrm_ss nrm_rs nrm_h nrm_hi nrm_lo lb_step
            wb_mm wb_ev wb_out wb_in row_step row_act row_mm row_ev row_a row_done rnm_done
            conv_step
            hg_silu hg_e hg_l hg_lf hg_b hg_f hg_k hg_d hg_ex hg_eb hg_x hg_tr hg_v hg_kt hg_lv hg_z hg_at hg_stp
            hg_s hg_o hg_sq hg_ss hg_rs hg_y hg_hi hg_lo
            ml_silu ml_tanh ml_nm ml_tr ml_v ml_dx ml_ex ml_qk ml_pt ml_num ml_nm2 ml_em ml_h ml_dn ml_sq ml_ss
            ml_rs ml_y ml_hi ml_lo
            mb_silu mb_tr mb_xd mb_cb mb_nm mb_dx mb_ex mb_pt mb_ym mb_y mb_sq mb_ss mb_rs mb_hi mb_lo
            g_acc o_hi o_lo up_c up_s1 up_sg up_a up_hi up_lo
            cv_in cv_p cv_y cv_hi cv_lo
            at_silu at_sq at_ss at_tr at_rs at_v at_n at_s at_l at_mx at_ex at_sum at_p at_pt at_pe at_o at_y
            at_hi at_lo kz_set out_tr out_ev out_dma0 out_dma1""".split()
        S = {n: ctx.enter_context(nc.semaphore(n)) for n in names}
        slab_in = [ctx.enter_context(nc.semaphore(f"slab_in{i}")) for i in range(4)]
        acc_free = [S["acc_free0"], S["acc_free1"]]

        def cc(k, n=P):
            return con[:, k:k + n]

        ident, nident, ones, clampm = cc(K_ID), cc(K_NID), cc(K_ONES), cc(K_CLAMP)

        def pc(name, i=0):
            if isinstance(i, int):
                return par[:, PAR[name] + i:PAR[name] + i + 1]
            return par[:, bass.ds(i + PAR[name], 1)]

        def tile_of(buf, f):
            if isinstance(f, int):
                return buf[:, f, :]
            return buf[:, bass.ds(f, 1), :].rearrange("p a t -> p (a t)")

        def blk(ap, b, n=1):
            return ap[:, b * P:(b + n) * P]

        def stage(at=scratch):
            return arena(at)[0]

        pr = stage()
        xs = pr("xs", [P, NB, D])
        oneh = pr("oneh", [P, W_LINE])
        wrow = [pr(f"wrow{i}", [P, W_LINE]) for i in range(2)]
        nr = stage(area)
        sqn = [nr(f"sqn{i}", [P, T]) for i in range(2)]
        rsn = nr("rsn", [P, T])
        htn = [nr(f"htn{i}", [P, T]) for i in range(2)]
        ro = stage()
        rz, r1, r2, r3, r4, r5, ra = (ro(f"row{i}", [P, T]) for i in range(7))
        rdg = ro("rdg", [P, NB, MB_HEADS])
        rac = ro("rac", [P, 1])

        hg = stage()
        e0, e1, lf, bb, kk, eb, k1, q1, at_ = (hg(f"hg{i}", [P, T]) for i in range(9))
        dd = [hg(f"hgd{i}", [P, T]) for i in range(2)]
        ex = [hg(f"hgx{i}", [P, T]) for i in range(2)]
        zz = [hg(f"hgz{i}", [P, T]) for i in range(2)]
        hm = stage(area)
        sqh, rsh, yth, vt = (hm(f"hgm{i}", [P, T]) for i in range(4))
        kt_ = hm("hgkt", [P, 3 * P])
        st_ = hm("hgst", [P, 3 * P])

        ml = stage()
        m_e = ml("m_e", [P, 1280])
        m_p = ml("m_p", [P, 1280])
        m_v = ml("m_v", [P, NB, 2 * P])
        m_em, m_dn, m_rd, m_rs = (ml(f"m_{i}", [P, T]) for i in range(4))
        m_h = ml("m_h", [P, 2, T])
        m_sq = ml("m_sq", [P, 2, T])
        mb = stage()
        s_e = mb("s_e", [P, 1280])
        s_p = [mb(f"s_p{i}", [P, 1280]) for i in range(2)]
        s_x = mb("s_x", [P, NB, 4, 64])
        s_y = mb("s_y", [P, 2, T])
        s_sq = mb("s_sq", [P, 2, T])
        s_rs = mb("s_rs", [P, T])
        gs = stage()
        tg = [gs(f"tg{i}", [P, T]) for i in range(2)]
        tm = gs("tm", [P, T])

        fl = stage(y_at)("fl", [P, NF, T], F32R)
        ff = stage(max(y_at + NF * 4 * T, area + 5 * 4 * T))
        fh = ff("fh", [P, NF, T], F32R)
        f_g = [ff(f"f_g{i}", [P, T]) for i in range(2)]
        f_v = [ff(f"f_v{i}", [P, T]) for i in range(2)]
        f_s = [ff(f"f_s{i}", [P, T]) for i in range(2)]

        sec = stage(area + 5 * 4 * T)
        wb = sec("wb", [P, AT_HEADS, W_BIAS])
        au = [sec(f"au{i}", [P, 4, T]) for i in range(2)]
        c_u, c_b, c_p, c_y, c_z = cbuf = [sec(f"c_{i}", [P, T]) for i in range(5)]
        a_l, a_q = cbuf[:4], cbuf[4]
        an = stage(area)
        a_rs = an("a_rs", [P, 2, T])
        a_pt = [an(f"a_pt{i}", [P, T]) for i in range(2)]
        a_sq = sec("a_sq", [P, 2, T])
        a_k = [sec(f"a_k{i}", [P, T]) for i in range(2)]
        a_v = sec("a_v", [P, NB, P])
        a_st = sec("a_st", [P, 8, 3])
        a_y = sec("a_y", [P, T])
        os_ = [sec(f"os{i}", [P, T]) for i in range(2)]

        OFF = {0: (512, 384), 2: (896, 128), 1: (1024, 256)}

        block = ctx.enter_context(nc.Block())

        def filled(eng, j0, it=None, k=0):
            eng.wait_ge(acc_free[j0 % 2], lin(j0 // 2 + 1, it, k // 2))

        @block.sync
        def _(sp):
            def load(slot, j, use):
                wait(sp, S["slab_split"], use)
                src = slabs[bass.ds(j, 1)] if not isinstance(j, int) else slabs[j:j + 1]
                sp.dma_start(raw[:, slot:slot + 1].rearrange("p a k f -> p a (k f)"),
                             src.rearrange("a p n -> p a n")).then_inc(slab_in[slot], 16)

            for j in range(4):
                load(j, j, 0)
            with sp.Fori(1, N_SLABS // 4) as it:
                for i in range(4):
                    load(i, it * 4 + i, it * 4 + (i - 3))
            for j in range(N_SLABS // 4 * 4, N_SLABS):
                load(j % 4, j, j - 3)
            for f in range(KT):
                sp.wait_ge(S["out_ev"], f + 1)
                sp.dma_start(out.rearrange("a (b p) d -> p (a b) d", p=P)[:, :, f * P:(f + 1) * P],
                             os_[f % 2][:, :].rearrange("p (b d) -> p b d", b=NB)
                             ).then_inc(S[f"out_dma{f % 2}"], 16)
            sp.wait_ge(S["out_dma0"], 16 * KT // 2)
            sp.wait_ge(S["out_dma1"], 16 * KT // 2)

        @block.gpsimd
        def _(pool):
            nc.gpsimd.memset(zero[:, :], 0.0).then_inc(S["zero_set"], 1)
            pool.wait_ge(S["zero_set"], 1)

            def split(i, j, nth):
                r = raw[:, i].rearrange("p k f -> p (k f)")
                h = wh[:, i % 2].rearrange("p k f -> p (k f)")
                lo = wl[:, i % 2].rearrange("p k f -> p (k f)")
                pool.wait_ge(slab_in[i], nth)
                wait(pool, S["slab_used"], j - 1)
                pool.tensor_tensor(h, r, zero[:, 0:1].broadcast_to([P, KT * P]), ALU.add).then_inc(S["slab_hi"], 1)
                pool.wait_ge(S["slab_hi"], j + 1)
                pool.tensor_tensor(lo, r, h.bitcast(F32), ALU.subtract).then_inc(S["slab_split"], 1)

            for j in range(4):
                split(j, j, 16)
            with pool.Fori(1, N_SLABS // 4) as it:
                for i in range(4):
                    split(i, it * 4 + i, it * 16 + 16)
            for j in range(N_SLABS // 4 * 4, N_SLABS):
                split(j % 4, j, 16 * (j // 4 + 1))

        @block.tensor
        def _(pe):
            mm = pe.matmul

            def project(j0, it=None, k=0, src=(hh, hl), n=KT, base=0, t0=None, first=True, last=True):
                t0 = j0 if t0 is None else t0
                bank, s = acc[t0 % 2], j0 % 2
                pe.wait_ge(S["slab_split"], lin(j0 + 1, it, k))
                if first:
                    wait(pe, acc_free[t0 % 2], lin(t0 // 2, it, k // 2))
                for b in range(n):
                    xh, xl = src[0][:, base + b, :], src[1][:, base + b, :]
                    mm(bank[:, :], wh[:, s, b, :], xh, start=first and b == 0, stop=False)
                    mm(bank[:, :], wh[:, s, b, :], xl, start=False, stop=False)
                    ins = mm(bank[:, :], wl[:, s, b, :], xh, start=False, stop=last and b == n - 1)
                ins.then_inc(S["slab_used"], 1)

            def norm(k):
                for f in range(KT):
                    pe.wait_ge(S["nrm_sq"], 8 * k + f + 1)
                    if f == 0:
                        wait(pe, S["nrm_rs"], 2 * k)
                    mm(b6[:, :], ones, sqn[f % 2][:, :], start=f == 0, stop=f == KT - 1).then_inc(S["nrm_ss"], 1)

            pe.wait_ge(S["params_in"], 32)
            pe.wait_ge(S["x_in"], 16)
            for f in range(KT):
                wait(pe, S["pro_xT"], f - 3)
                for b in range(NB):
                    ins = pe.transpose(blk(psum[2 + f % 4], b), xs[:, b, f * P:(f + 1) * P], ident)
                ins.then_inc(S["pro_tr"], 1)
            norm(0)
            pe.wait_ge(S["onehot_in"], 16)
            pe.wait_ge(S["pro_xT"], 8)
            for h in range(AT_HEADS):
                for c in range(2):
                    n = 2 * h + c
                    wait(pe, S["wb_ev"], n - 1)
                    mm(psum[2 + n % 2][:, :], pc("rel", h).broadcast_to([P, P]), oneh[:, c * T:(c + 1) * T],
                       start=True, stop=True).then_inc(S["wb_mm"], 1)
            pe.wait_ge(S["nrm_lo"], 8)
            project(J_SMALL)
            project(J_HG)
            pe.wait_ge(S["row_a"], 1)
            mm(b4[:, :], cc(K_SELI), rz[:, :], start=True, stop=False)
            mm(b4[:, :], cc(K_NSELF), cum[:, :], start=False, stop=True).then_inc(S["row_mm"], 1)
            project(J_HG + 1)
            pe.wait_ge(S["row_ev"], 1)
            for b in range(NB):
                pe.transpose(blk(b5, b), blk(ra, b), ident)
            for b in range(NB):
                pe.transpose(blk(b6, b), blk(cum, b), ident)
            for b in range(NB):
                ins = pe.transpose(blk(b7, b), blk(r5, b), ident)
            ins.then_inc(S["row_mm"], 1)
            pe.wait_ge(S["row_done"], 4)
            mm(b4[:, 0:NB * MB_HEADS], ones, rdg[:, :, :].rearrange("p b h -> p (b h)"),
               start=True, stop=True).then_inc(S["row_mm"], 1)
            project(J_HG + 2)
            project(J_HG + 3)
            pe.wait_ge(S["row_done"], 11)
            pe.wait_ge(S["rnm_done"], 2)

            def hg_level(l, u, p):
                pe.wait_ge(S["hg_z"], u * 14 + 2 * l)
                pe.wait_ge(S["hg_at"], u * 8 + (l - 1))
                z, bank = zz[l % 2], (b2, b3)[l % 2]
                for b in range(NB):
                    ins = mm(blk(bank, b), blk(z, b), blk(z, b), start=True, stop=True)
                ins.then_inc(S["hg_lv"], 1)

            def hg_part(part, u, p, j0, it):
                U = unit[p]
                if part == 0:
                    filled(pe, j0 + 2, it, 8)
                    wait(pe, S["hg_kt"], u * 1)
                    for b in range(NB):
                        ins = pe.transpose(blk(b4, b), blk(U[:, 2, :], b), ident)
                    ins.then_inc(S["hg_tr"], 1)
                    pe.wait_ge(S["hg_k"], u + 1)
                    pe.wait_ge(S["hg_silu"], u * 2 + 1)
                    wait(pe, S["hg_at"], u * 8)
                    for b in range(NB):
                        ins = mm(blk(b2, b), blk(kk, b), blk(U[:, 0, :], b), start=True, stop=True)
                    ins.then_inc(S["hg_lv"], 1)
                    pe.wait_ge(S["hg_x"], u * 2 + 1)
                    pe.wait_ge(S["hg_v"], u + 1)
                    for b in range(3):
                        ins = pe.transpose(blk(b4, b), blk(k1, b), ident)
                    ins.then_inc(S["hg_tr"], 1)
                elif part == 1:
                    pe.wait_ge(S["hg_kt"], u + 1)
                    wait(pe, S["hg_s"], u * 3)
                    for b in range(3):
                        ins = mm(blk(b5, b), blk(kt_, b), blk(vt, b), start=True, stop=True)
                    ins.then_inc(S["hg_stp"], 1)
                    hg_level(1, u, p)
                    hg_level(2, u, p)
                elif part == 2:
                    for l in (3, 4, 5):
                        hg_level(l, u, p)
                else:
                    hg_level(6, u, p)
                    hg_level(7, u, p)
                    pe.wait_ge(S["hg_at"], u * 8 + 8)
                    pe.wait_ge(S["hg_s"], u * 3 + 3)
                    pe.wait_ge(S["hg_x"], u * 2 + 2)
                    wait(pe, S["hg_y"], u * 2)
                    for b in range(NB):
                        ins = mm(blk(b6, b), blk(vt, b), blk(at_, b), start=True, stop=b == 0)
                        if b:
                            ins = mm(blk(b6, b), blk(st_, b - 1), blk(q1, b), start=False, stop=True)
                    ins.then_inc(S["hg_o"], 1)
                    pe.wait_ge(S["hg_sq"], u + 1)
                    mm(b7[:, :], ones, sqh[:, :], start=True, stop=True).then_inc(S["hg_ss"], 1)

            def ml_part(part, u):
                p = u % 2
                U, j = unit[p], ml_slab(u)
                if part == 0:
                    if u == 0:
                        pe.wait_ge(S["hg_lo"], HG_HEADS)
                        pe.wait_ge(S["hg_hi"], HG_HEADS)
                        filled(pe, J_G0 + 15)
                    wait(pe, S["ml_h"], 2 * u)
                    mm(b5[:, :], ident[:, u:u + 1].broadcast_to([P, P]), rnm[:, :], start=True, stop=True
                       ).then_inc(S["ml_nm"], 1)
                    for v in range(2):
                        filled(pe, j + 2 + v)
                        for b in range(NB):
                            ins = pe.transpose(blk((b6, b7)[v], b), blk(U[:, 2 + v, :], b), ident)
                        ins.then_inc(S["ml_tr"], 1)
                elif part == 1:
                    pe.wait_ge(S["ml_silu"], 2 * u + 2)
                    wait(pe, S["ml_em"], u)
                    wait(pe, S["ml_rs"], 2 * u)
                    q, k = U[:, 0, :], U[:, 1, :]
                    for b in range(NB):
                        ins = mm(blk(b2, b), blk(k, b), blk(q, b), start=True, stop=True)
                    ins.then_inc(S["ml_qk"], 1)
                    mm(b3[:, 0:384], blk(k, 0), blk(q, 1, 3), start=True, stop=True)
                    mm(b3[:, 384:512], blk(k, 2), blk(q, 3), start=True, stop=True).then_inc(S["ml_qk"], 1)
                    mm(b4[:, 0:256], blk(k, 1), blk(q, 2, 2), start=True, stop=True).then_inc(S["ml_qk"], 1)
                elif part == 2:
                    pe.wait_ge(S["ml_pt"], 3 * u + 3)
                    pe.wait_ge(S["ml_v"], 2 * u + 2)
                    pe.wait_ge(S["ml_dx"], 4 * u + 4)
                    pe.wait_ge(S["ml_ex"], 4 * u + 4)
                    for bank, w in ((b6, lambda b: m_v[:, b, 0:P]), (b7, lambda b: m_v[:, b, P:2 * P]),
                                    (b5, lambda b: ones)):
                        mm(bank[:, P:T], w(0), m_p[:, 512:896], start=True, stop=False)
                        mm(bank[:, 2 * P:T], w(1), m_p[:, 1024:1280], start=False, stop=False)
                        mm(bank[:, 3 * P:T], w(2), m_p[:, 896:1024], start=False, stop=False)
                        for b in range(NB):
                            ins = mm(blk(bank, b), w(b), m_p[:, b * P:(b + 1) * P], start=False, stop=b == NB - 1)
                        ins.then_inc(S["ml_num"], 1)
                    mm(b2[:, :], nident[:, ROW_F + u:ROW_F + u + 1].broadcast_to([P, P]), cum[:, :],
                       start=True, stop=False)
                    mm(b2[:, :], ident[:, u:u + 1].broadcast_to([P, P]), rnm[:, :], start=False, stop=True
                       ).then_inc(S["ml_nm2"], 1)
                else:
                    for v in range(2):
                        pe.wait_ge(S["ml_sq"], 2 * u + v + 1)
                        ins = mm(b3[:, :], ones, m_sq[:, v, :], start=v == 0, stop=v == 1)
                    ins.then_inc(S["ml_ss"], 1)

            def mb_head(g, h):
                n = 4 * g + h
                if h == 0:
                    wait(pe, S["mb_rs"], 2 * g)
                if n:
                    pe.wait_ge(S["mb_dx"], 4 * n)
                    pe.wait_ge(S["mb_ex"], 7 * n)
                mm(b5[:, :], ident[:, n:n + 1].broadcast_to([P, P]), cum[:, :], start=True, stop=True
                   ).then_inc(S["mb_nm"], 1)
                pe.wait_ge(S["mb_pt"], 3 * n + 3)
                if h == 0:
                    pe.wait_ge(S["mb_xd"], 2 * g + 2)
                pt = s_p[n % 2]
                rows = slice(64 * (h % 2), 64 * (h % 2) + 64)
                bank = (b6, b7)[h // 2]
                mm(bank[rows, P:T], s_x[:, 0, h, :], pt[:, 512:896], start=True, stop=False)
                mm(bank[rows, 2 * P:T], s_x[:, 1, h, :], pt[:, 1024:1280], start=False, stop=False)
                mm(bank[rows, 3 * P:T], s_x[:, 2, h, :], pt[:, 896:1024], start=False, stop=False)
                for b in range(NB):
                    ins = mm(bank[rows, b * P:(b + 1) * P], s_x[:, b, h, :], pt[:, b * P:(b + 1) * P],
                             start=False, stop=b == NB - 1)
                ins.then_inc(S["mb_ym"], 1)

            def mb_part(part, g):
                p = g % 2
                U = unit[p]
                if part == 0:
                    if g == 0:
                        pe.wait_ge(S["ml_lo"], 2 * ML_HEADS)
                        pe.wait_ge(S["ml_hi"], 2 * ML_HEADS)
                        pe.wait_ge(S["g_acc"], KT)
                    pe.wait_ge(S["mb_silu"], 6 * g + 4)
                    wait(pe, S["mb_y"], 6 * g)
                    for i in range(2):
                        for b in range(2):
                            for v in range(2):
                                ins = pe.transpose(blk((b6, b7)[i], 2 * b + v), blk(U[:, 2 + v, :], 2 * i + b), ident)
                        ins.then_inc(S["mb_tr"], 1)
                    wait(pe, S["mb_pt"], 12 * g)
                    bm, cm = U[:, 0, :], U[:, 1, :]
                    for b in range(NB):
                        mm(blk(b2, b), blk(bm, b), blk(cm, b), start=True, stop=True)
                    mm(b3[:, 0:384], blk(bm, 0), blk(cm, 1, 3), start=True, stop=True)
                    mm(b3[:, 384:512], blk(bm, 2), blk(cm, 3), start=True, stop=True)
                    mm(b4[:, 0:256], blk(bm, 1), blk(cm, 2, 2), start=True, stop=True).then_inc(S["mb_cb"], 1)
                mb_head(g, part)
                if part == 3:
                    pe.wait_ge(S["mb_dx"], 16 * (g + 1))
                    pe.wait_ge(S["mb_ex"], 28 * (g + 1))
                    for v in range(2):
                        pe.wait_ge(S["mb_sq"], 2 * g + v + 1)
                        ins = mm(b5[:, :], ones, s_sq[:, v, :], start=v == 0, stop=v == 1)
                    ins.then_inc(S["mb_ss"], 1)

            def hg_pair(it):
                for p in range(2):
                    for part in range(4):
                        project(J_HG + 4 + 4 * p + part, it, 8)
                        hg_part(part, lin(p, it, 2), p, J_HG + 4 * p, it)

            hg_pair(None)
            with pe.Fori(1, HG_HEADS // 2 - 1) as it:
                hg_pair(it)
            for u in (HG_HEADS - 2, HG_HEADS - 1):
                for part in range(4):
                    for i in tiles_before(part, 4 if u == HG_HEADS - 2 else 6):
                        project((J_HG + 4 * (u + 1) if u == HG_HEADS - 2 else J_ML0) + i)
                    hg_part(part, u, u % 2, J_HG + 4 * u, None)

            def gates(j0, lo_sem, n):
                pe.wait_ge(lo_sem, n)
                with pe.Fori(0, KT // 2) as it:
                    for f in range(2):
                        project(j0 + 2 * f, it, 4)
                        project(j0 + 2 * f + 1, it, 4, src=(yh, yl))

            gates(J_G0, S["hg_lo"], HG_HEADS)
            for u in range(ML_HEADS):
                nxt = ml_slab(u + 1) if u + 1 < ML_HEADS else J_MB0
                for part in range(4):
                    for i in tiles_before(part, 6):
                        project(nxt + i)
                    ml_part(part, u)
            gates(J_G1, S["ml_lo"], 2 * ML_HEADS)
            for g in range(MB_GROUPS):
                for part in range(4):
                    if g + 1 < MB_GROUPS:
                        for i in tiles_before(part, 6):
                            project(mb_slab(g + 1) + i)
                    mb_part(part, g)
            gates(J_G2, S["mb_lo"], 2 * MB_GROUPS)

            pe.wait_ge(S["o_lo"], KT)
            with pe.Fori(0, KT // 4) as it:
                for f in range(4):
                    project(J_O + f, it, 4)
            norm(1)
            pe.wait_ge(S["nrm_lo"], 16)
            with pe.Fori(0, NF // 2) as it:
                for j in range(2):
                    project(J_UP + 2 * j, it, 4)
                    project(J_UP + 2 * j + 1, it, 4)
            pe.wait_ge(S["up_lo"], NF)
            with pe.Fori(0, KT // 4) as it:
                for f in range(4):
                    for c, n in enumerate(DN_CHUNKS):
                        j0, t0 = J_DN + 3 * f + c, J_DN + f
                        s = j0 % 2
                        pe.wait_ge(S["slab_split"], it * 12 + (j0 + 1))
                        if c == 0:
                            pe.wait_ge(acc_free[t0 % 2], it * 2 + t0 // 2)
                        bank = acc[t0 % 2]
                        for b in range(n):
                            xh, xl = fh[:, 8 * c + b, :], fl[:, 8 * c + b, :]
                            end = c == 2 and b == n - 1
                            mm(bank[:, :], wh[:, s, b, :], xh, start=c == 0 and b == 0, stop=False)
                            mm(bank[:, :], wh[:, s, b, :], xl, start=False, stop=False)
                            ins = mm(bank[:, :], wl[:, s, b, :], xh, start=False, stop=end)
                        ins.then_inc(S["slab_used"], 1)
            norm(2)
            norm(3)
            pe.wait_ge(S["nrm_lo"], 24)
            with pe.Fori(0, 4) as it:
                for i in range(4):
                    project(J_CV + i, it, 4, t0=J_CV - DN_SHIFT + i)

            def at_scores(i, t):
                n = 8 * t + i
                wait(pe, S["at_l"], n - 1)
                mm((b5, b6)[i % 2][:, :], blk(a_q, i % 4), a_k[i // 4][:, :], start=True, stop=True
                   ).then_inc(S["at_s"], 1)

            def at_values(i, t):
                n = 8 * t + i
                pe.wait_ge(S["at_p"], n + 1)
                wait(pe, S["at_pt"], n - 1)
                if i < 2:
                    pe.wait_ge(S["at_n"], 3 * t + 3)
                bank = (b2, b3)[i % 2]
                for b in range(NB):
                    ins = pe.transpose(blk(bank, b), blk(a_l[i % 4], b), ident)
                ins.then_inc(S["at_tr"], 1)
                pe.wait_ge(S["at_pt"], n + 1)
                if i == 0:
                    wait(pe, S["at_y"], t)
                hd = i // 4
                rows = slice(64 * hd, 64 * hd + 64)
                for b in range(NB):
                    ins = mm(b7[rows, (i % 4) * P:(i % 4 + 1) * P], a_v[:, b, rows], blk(a_pt[i % 2], b),
                             start=b == 0, stop=b == NB - 1)
                ins.then_inc(S["at_o"], 1)

            def at_part(part, t):
                U, j = au[t % 2], J_AT - DN_SHIFT + 4 * t
                if part == 0:
                    for i in range(2):
                        pe.wait_ge(S["at_sq"], 2 * t + i + 1)
                        wait(pe, S["at_tr"], 8 * t)
                        wait(pe, S["at_pt"], 8 * t)
                        mm((b2, b3)[i][:, :], cc(K_BD), a_sq[:, i, :], start=True, stop=True
                           ).then_inc(S["at_ss"], 1)
                    filled(pe, j + 2)
                    wait(pe, S["at_v"], t)
                    for b in range(NB):
                        ins = pe.transpose(blk(b4, b), blk(U[:, 2, :], b), ident)
                    ins.then_inc(S["at_ss"], 1)
                    pe.wait_ge(S["at_n"], 3 * t + 3)
                at_scores(2 * part, t)
                at_scores(2 * part + 1, t)
                if part:
                    if part == 1:
                        pe.wait_ge(S["at_v"], t + 1)
                    at_values(2 * part - 2, t)
                    at_values(2 * part - 1, t)

            for i in range(4):
                project(J_AT + i, t0=J_AT - DN_SHIFT + i)
            for t in range(4):
                for part in range(4):
                    if t < 3:
                        j = J_AT + 4 * (t + 1) + part
                        project(j, t0=j - DN_SHIFT)
                    at_part(part, t)
                at_values(6, t)
                at_values(7, t)
            pe.wait_ge(S["at_lo"], 4)
            pe.wait_ge(S["cv_lo"], 4)
            with pe.Fori(0, KT // 4) as it:
                for f in range(4):
                    project(J_O2 + f, it, 4, src=(yh, yl), t0=J_O2 - DN_SHIFT + f)
            for f in range(KT):
                filled(pe, J_O2 - DN_SHIFT + f)
                wait(pe, S["out_ev"], f - 3)
                for b in range(NB):
                    ins = pe.transpose(blk(psum[2 + f % 4], b), blk(xT[:, f, :], b), ident)
                ins.then_inc(S["out_tr"], 1)

        @block.scalar
        def _(act):
            A = act.activation

            def silu_tables():
                act.preload_act_table_set("silu_and_others")

            def exp_tables():
                act.preload_act_table_set("natural_log_exp_and_others")

            act.dma_start(con[:, :], const_d).then_inc(S["params_in"], 16)
            act.dma_start(par[:, :], par_d).then_inc(S["params_in"], 16)
            act.dma_start(xs[:, :, :], x.rearrange("a (b p) d -> p (a b) d", p=P)).then_inc(S["x_in"], 16)
            act.dma_start(oneh[:, :], onehot_d).then_inc(S["onehot_in"], 16)
            exp_tables()

            def norm(k):
                for f in range(KT):
                    n = 8 * k + f
                    wait(act, S["nrm_ss"], n - 1)
                    A(sqn[f % 2][:, :], xT[:, f, :], ACT.Square).then_inc(S["nrm_sq"], 1)
                act.wait_ge(S["nrm_ss"], 8 * k + 8)
                if k:
                    act.wait_ge(S["nrm_h"], 8 * k)
                A(rsn[:, :], b6[:, :], ACT.Ln, scale=1.0 / D, bias=EPS).then_inc(S["nrm_rs"], 1)
                act.wait_ge(S["nrm_rs"], 2 * k + 1)
                A(rsn[:, :], rsn[:, :], ACT.Exp, scale=-0.5).then_inc(S["nrm_rs"], 1)

            def norm_hi(k, m):
                for f in range(KT):
                    act.wait_ge(S["nrm_h"], 8 * k + f + 1)
                    A(hh[:, f, :], htn[f % 2][:, :], ACT.Copy).then_inc(S["nrm_hi"], 1)

            for f in range(KT):
                act.wait_ge(S["pro_tr"], f + 1)
                A(xT[:, f, :], psum[2 + f % 4][:, :], ACT.Copy).then_inc(S["pro_xT"], 1)
            act.wait_ge(S["pro_xT"], 8)
            norm(0)
            norm_hi(0, 0)
            act.wait_ge(S["lb_step"], 1)
            A(lbt[:, 1, :], lbt[:, 0, :], ACT.Exp).then_inc(S["lb_step"], 1)
            for n in range(2 * AT_HEADS):
                h, c = n // 2, n % 2
                act.wait_ge(S["wb_mm"], n + 1)
                if c == 0 and h >= 2:
                    act.wait_ge(S["wb_out"], 16 * (h - 1))
                A(wrow[h % 2][:, c * T:(c + 1) * T], psum[2 + n % 2][:, :], ACT.Copy).then_inc(S["wb_ev"], 1)
                if c:
                    act.wait_ge(S["wb_ev"], n + 1)
                    if h:
                        act.wait_ge(S["wb_out"], 16 * h)
                    act.dma_start(bias_scratch[h], wrow[h % 2][:, :]).then_inc(S["wb_out"], 16)
            act.wait_ge(S["row_step"], 2)
            A(r2[:, :], r1[:, :], ACT.Exp).then_inc(S["row_act"], 1)
            A(rac[:, :], pc("alog"), ACT.Exp).then_inc(S["row_act"], 1)

            def copy_out(j0, dst, it=None, k=0, bank=None):
                act.wait_ge(S["slab_used"], lin(j0 + 1, it, k))
                A(dst, acc[j0 % 2][:, :], ACT.Copy).then_inc(acc_free[j0 % 2], 1)

            U0 = unit[0]
            copy_out(J_HG, U0[:, 0, :])
            act.wait_ge(S["row_mm"], 1)
            A(ra[:, :], b4[:, :], ACT.Copy).then_inc(S["row_ev"], 1)
            copy_out(J_HG + 2, U0[:, 2, :])
            copy_out(J_HG + 3, U0[:, 3, :])
            act.wait_ge(S["row_done"], 11)
            act.wait_ge(S["rnm_done"], 2)

            def hg_exps(l, u):
                n, half = P >> (l - 1), P >> l
                d, e = dd[l % 2], ex[l % 2]
                act.wait_ge(S["hg_d"], u * 8 + (l + 1))
                if l == 1:
                    wait(act, S["hg_z"], u * 14)
                elif l == 2:
                    act.wait_ge(S["hg_x"], u * 2 + 1)
                else:
                    act.wait_ge(S["hg_z"], u * 14 + 2 * (l - 2))
                dv = d[:, :].rearrange("p (c n) -> p c n", n=n)
                ev = e[:, :].rearrange("p (c n) -> p c n", n=n)
                A(ev[:, :, half:], dv[:, :, half:], ACT.Exp).then_inc(S["hg_ex"], 1)
                A(ev[:, :, :half], dv[:, :, :half], ACT.Exp, scale=-1.0).then_inc(S["hg_ex"], 1)

            def hg_part(part, u, p, j0, it):
                U = unit[p]
                if part == 0:
                    silu_tables()
                    filled(act, j0, it, 8)
                    A(U[:, 0, :], U[:, 0, :], ACT.Silu).then_inc(S["hg_silu"], 1)
                    filled(act, j0 + 3, it, 8)
                    A(U[:, 3, :], U[:, 3, :], ACT.Silu).then_inc(S["hg_silu"], 1)
                    exp_tables()
                    filled(act, j0 + 1, it, 8)
                    wait(act, S["hg_lf"], u * 1)
                    wait(act, S["hg_k"], u * 1)
                    A(e0[:, :], U[:, 1, :], ACT.Exp, scale=-1.0).then_inc(S["hg_e"], 1)
                    act.wait_ge(S["hg_e"], u + 1)
                    lb = lbc[:, u:u + 1] if isinstance(u, int) else lbc[:, bass.ds(u, 1)]
                    A(e1[:, :], e0[:, :], ACT.Ln, scale=lb, bias=1.0).then_inc(S["hg_l"], 1)
                    act.wait_ge(S["hg_l"], u * 2 + 1)
                    A(e0[:, :], e0[:, :], ACT.Ln, bias=1.0).then_inc(S["hg_l"], 1)
                    act.wait_ge(S["hg_lf"], u + 1)
                    A(e1[:, :], lf[:, :], ACT.Exp).then_inc(S["hg_f"], 1)
                    act.wait_ge(S["hg_d"], u * 8 + 1)
                    wait(act, S["hg_z"], u * 14)
                    A(ex[0][:, :], dd[0][:, :], ACT.Exp).then_inc(S["hg_ex"], 1)
                    act.wait_ge(S["hg_b"], u + 1)
                    wait(act, S["hg_s"], u * 3)
                    wait(act, S["hg_x"], u * 2)
                    A(eb[:, :], bb[:, :], ACT.Exp).then_inc(S["hg_eb"], 1)
                    act.wait_ge(S["hg_tr"], u * 2 + 1)
                    wait(act, S["hg_o"], u * 1)
                    A(vt[:, :], b4[:, :], ACT.Copy).then_inc(S["hg_v"], 1)
                    act.wait_ge(S["hg_tr"], u * 2 + 2)
                    A(kt_[:, :], b4[:, 0:3 * P], ACT.Copy).then_inc(S["hg_kt"], 1)
                    hg_exps(1, u)
                elif part == 1:
                    hg_exps(2, u)
                    hg_exps(3, u)
                elif part == 2:
                    hg_exps(4, u)
                    hg_exps(5, u)
                    hg_exps(6, u)
                else:
                    hg_exps(7, u)
                    act.wait_ge(S["hg_o"], u + 1)
                    wait(act, S["hg_ss"], u * 1)
                    A(sqh[:, :], b6[:, :], ACT.Square).then_inc(S["hg_sq"], 1)
                    act.wait_ge(S["hg_ss"], u + 1)
                    wait(act, S["hg_y"], u * 2)
                    A(rsh[:, :], b7[:, :], ACT.Ln, scale=1.0 / P, bias=EPS).then_inc(S["hg_rs"], 1)
                    act.wait_ge(S["hg_rs"], u * 2 + 1)
                    A(rsh[:, :], rsh[:, :], ACT.Exp, scale=-0.5).then_inc(S["hg_rs"], 1)
                    act.wait_ge(S["hg_y"], u * 2 + 2)
                    A(tile_of(yh, u), yth[:, :], ACT.Copy).then_inc(S["hg_hi"], 1)

            def fill_hg(i, j0, dst, it):
                if i != 1:
                    copy_out(j0 + i, dst[:, i, :], it, 8)

            def fill_ml(i, j0, dst):
                if i >= 2:
                    copy_out(j0 + i, dst[:, i, :])

            def fill_mb(i, j0, dst):
                if i >= 4:
                    copy_out(j0 + i, dst[:, i, :])

            def ml_part(part, u):
                p = u % 2
                U, j = unit[p], ml_slab(u)
                if part == 0:
                    silu_tables()
                    for i in range(2):
                        filled(act, j + i)
                        A(U[:, i, :], U[:, i, :], ACT.Silu).then_inc(S["ml_silu"], 1)
                    for i in range(2):
                        filled(act, j + 4 + i)
                        A(U[:, 4 + i, :], U[:, 4 + i, :], ACT.Tanh, scale=0.5).then_inc(S["ml_tanh"], 1)
                    exp_tables()
                    if u == 0:
                        act.wait_ge(S["hg_lo"], HG_HEADS)
                        act.wait_ge(S["hg_hi"], HG_HEADS)
                        filled(act, J_G0 + 15)
                    act.wait_ge(S["ml_dx"], 4 * u + 4)
                    wait(act, S["ml_pt"], 3 * u)
                    for b in (0, 2, 1):
                        o, n = OFF[b]
                        A(m_e[:, o:o + n], b5[:, (b + 1) * P:T], ACT.Exp, bias=acol[:, b, u:u + 1]
                          ).then_inc(S["ml_ex"], 1)
                    for v in range(2):
                        act.wait_ge(S["ml_tr"], 2 * u + v + 1)
                        wait(act, S["ml_num"], 3 * u)
                        A(m_v[:, :, v * P:(v + 1) * P], (b6, b7)[v][:, :].rearrange("p (b d) -> p b d", b=NB),
                          ACT.Copy).then_inc(S["ml_v"], 1)
                    A(m_e[:, 0:T], m_e[:, 0:T], ACT.Exp).then_inc(S["ml_ex"], 1)
                elif part == 2:
                    act.wait_ge(S["ml_nm2"], u + 1)
                    wait(act, S["ml_dn"], 3 * u)
                    A(m_em[:, :], b2[:, :], ACT.Exp).then_inc(S["ml_em"], 1)
                elif part == 3:
                    for v in range(2):
                        act.wait_ge(S["ml_h"], 2 * u + v + 1)
                        wait(act, S["ml_ss"], u)
                        A(m_sq[:, v, :], m_h[:, v, :], ACT.Square).then_inc(S["ml_sq"], 1)
                    act.wait_ge(S["ml_ss"], u + 1)
                    wait(act, S["ml_y"], 4 * u)
                    A(m_rs[:, :], b3[:, :], ACT.Ln, scale=1.0 / 256, bias=EPS).then_inc(S["ml_rs"], 1)
                    act.wait_ge(S["ml_rs"], 2 * u + 1)
                    A(m_rs[:, :], m_rs[:, :], ACT.Exp, scale=-0.5).then_inc(S["ml_rs"], 1)
                    for v in range(2):
                        act.wait_ge(S["ml_y"], 4 * u + 2 * v + 2)
                        if u == 0:
                            act.wait_ge(S["slab_used"], J_ML1)
                        A(yh[:, 2 * u + v, :], m_h[:, v, :], ACT.Copy, scale=0.5).then_inc(S["ml_hi"], 1)

            def mb_head(g, h):
                n = 4 * g + h
                act.wait_ge(S["mb_dx"], 4 * n + 4)
                wait(act, S["mb_pt"], 3 * n)
                if n == 0:
                    act.wait_ge(S["ml_lo"], 2 * ML_HEADS)
                    act.wait_ge(S["g_acc"], KT)
                for k, (b, i) in enumerate(((0, 1), (0, 2), (0, 3), (2, 3), (1, 2), (1, 3))):
                    o = OFF[b][0] + (i - b - 1) * P
                    A(s_e[:, o:o + P], blk(b5, i), ACT.Exp, bias=dend[:, k, n:n + 1]).then_inc(S["mb_ex"], 1)
                A(s_e[:, 0:T], s_e[:, 0:T], ACT.Exp).then_inc(S["mb_ex"], 1)

            def mb_part(part, g):
                U, j = unit[g % 2], mb_slab(g)
                if part == 0:
                    silu_tables()
                    for i in range(6):
                        filled(act, j + i)
                        A(U[:, i, :], U[:, i, :], ACT.Silu).then_inc(S["mb_silu"], 1)
                    exp_tables()
                mb_head(g, part)
                if part == 3:
                    for v in range(2):
                        act.wait_ge(S["mb_y"], 6 * g + 2 * v + 2)
                        wait(act, S["mb_ss"], g)
                        A(s_sq[:, v, :], s_y[:, v, :], ACT.Square).then_inc(S["mb_sq"], 1)
                    act.wait_ge(S["mb_ss"], g + 1)
                    wait(act, S["mb_y"], 6 * g)
                    A(s_rs[:, :], b5[:, :], ACT.Ln, scale=1.0 / 256, bias=EPS).then_inc(S["mb_rs"], 1)
                    act.wait_ge(S["mb_rs"], 2 * g + 1)
                    A(s_rs[:, :], s_rs[:, :], ACT.Exp, scale=-0.5).then_inc(S["mb_rs"], 1)
                    for v in range(2):
                        act.wait_ge(S["mb_y"], 6 * g + 4 + v + 1)
                        if g == 0:
                            act.wait_ge(S["slab_used"], J_MB1)
                        A(yh[:, 2 * g + v, :], s_y[:, v, :], ACT.Copy).then_inc(S["mb_hi"], 1)

            def hg_pair(it):
                for p in range(2):
                    for part in range(4):
                        hg_part(part, lin(p, it, 2), p, J_HG + 4 * p, it)
                        if part == 0:
                            wait(act, S["hg_lo"], lin(p, it, 2))
                        fill_hg(part, J_HG + 4 + 4 * p, unit[1 - p], it)

            hg_pair(None)
            with act.Fori(1, HG_HEADS // 2 - 1) as it:
                hg_pair(it)
            for u in (HG_HEADS - 2, HG_HEADS - 1):
                for part in range(4):
                    hg_part(part, u, u % 2, J_HG + 4 * u, None)
                    if part == 0:
                        act.wait_ge(S["hg_lo"], u)
                    if u == HG_HEADS - 2:
                        fill_hg(part, J_HG + 4 * (u + 1), unit[1 - u % 2], None)
                    else:
                        for i in tiles_before(part, 6):
                            fill_ml(i, J_ML0, unit[0])

            def gates(b, j0):
                silu_tables()
                if b == 0:
                    act.wait_ge(S["hg_lo"], HG_HEADS)
                elif b == 1:
                    act.wait_ge(S["ml_lo"], 2 * ML_HEADS)
                else:
                    act.wait_ge(S["mb_lo"], 2 * MB_GROUPS)
                with act.Fori(0, KT // 2) as it:
                    for f in range(2):
                        act.wait_ge(S["slab_used"], it * 4 + (j0 + 2 * f + 1))
                        filled(act, j0 + 2 * f - 3, it, 4)
                        A(tg[f][:, :], acc[j0 % 2][:, :], ACT.Tanh, scale=0.5).then_inc(acc_free[j0 % 2], 1)

            gates(0, J_G0)
            for u in range(ML_HEADS):
                last = u + 1 == ML_HEADS
                for part in range(4):
                    ml_part(part, u)
                    if part == 0:
                        wait(act, S["ml_lo"], 2 * u)
                    for i in tiles_before(part, 6):
                        if last:
                            fill_mb(i, J_MB0, unit[0])
                        else:
                            fill_ml(i, ml_slab(u + 1), unit[1 - u % 2])
            gates(1, J_G1)
            for g in range(MB_GROUPS):
                for part in range(4):
                    mb_part(part, g)
                    if g + 1 < MB_GROUPS:
                        if part == 0:
                            wait(act, S["mb_lo"], 2 * g)
                        for i in tiles_before(part, 6):
                            fill_mb(i, mb_slab(g + 1), unit[1 - g % 2])
            gates(2, J_G2)
            act.wait_ge(S["slab_used"], J_O)
            for f in range(KT):
                act.wait_ge(S["g_acc"], KT + f + 1)
                A(hh[:, f, :], mixed[:, f, :], ACT.Copy, scale=0.5).then_inc(S["o_hi"], 1)

            exp_tables()
            act.wait_ge(S["o_lo"], KT)
            for f in range(KT):
                filled(act, J_O + f)
            norm(1)
            norm_hi(1, 1)
            silu_tables()
            with act.Fori(0, NF // 2) as it:
                for p in range(2):
                    j = it * 2 + p
                    act.wait_ge(S["slab_used"], it * 4 + (J_UP + 2 * p + 1))
                    A(f_g[p][:, :], acc[J_UP % 2][:, :], ACT.Identity, scale=pc("fcw", it * 6 + (3 * p + 2)),
                      bias=pc("fcb", j)).then_inc(S["up_c"], 1)
                    act.wait_ge(S["slab_used"], it * 4 + (J_UP + 2 * p + 2))
                    A(f_v[p][:, :], acc[1 - J_UP % 2][:, :], ACT.Identity,
                      scale=pc("fcw", it * 6 + (3 * NF + 3 * p + 2)), bias=pc("fcb", j + NF)
                      ).then_inc(S["up_c"], 1)
                    filled(act, J_UP + 2 * p, it, 4)
                    A(f_s[p][:, :], f_g[p][:, :], ACT.Silu).then_inc(S["up_sg"], 1)
                    act.wait_ge(S["up_a"], j + 1)
                    A(tile_of(fh, j), f_s[p][:, :], ACT.Copy).then_inc(S["up_hi"], 1)
            exp_tables()
            for f in range(KT):
                filled(act, J_DN + f)
            act.wait_ge(S["wb_out"], 16 * AT_HEADS)
            skew = bass.AP(tensor=bias_scratch.tensor, offset=P - 1,
                           ap=[[W_LINE - 1, P], [P * W_LINE, AT_HEADS], [1, W_BIAS]])
            act.dma_start(wb[:, :, :], skew).then_inc(S["wb_in"], 16)
            norm(2)
            act.wait_ge(S["nrm_h"], 24)
            norm(3)
            norm_hi(3, 2)
            silu_tables()
            def conv_tile(it):
                j = J_CV
                t0 = J_CV - DN_SHIFT
                wait(act, S["cv_y"], it * 5)
                for i, dst in ((0, c_u), (1, c_b)):
                    act.wait_ge(S["slab_used"], it * 4 + (j + i + 1))
                    A(dst[:, :], acc[(t0 + i) % 2][:, :], ACT.Copy).then_inc(acc_free[(t0 + i) % 2], 1)
                act.wait_ge(S["slab_used"], it * 4 + (j + 4))
                A(c_z[:, :], acc[(t0 + 3) % 2][:, :], ACT.Silu).then_inc(acc_free[(t0 + 3) % 2], 1)
                act.wait_ge(S["cv_y"], it * 5 + 5)
                A(tile_of(yh, it), c_y[:, :], ACT.Copy).then_inc(S["cv_hi"], 1)

            conv_tile(0)
            with act.Fori(1, 4) as it:
                conv_tile(it)

            def fill_at(i, t):
                j = J_AT + 4 * t + i
                act.wait_ge(S["slab_used"], j + 1)
                A(au[t % 2][:, i, :], acc[(j - DN_SHIFT) % 2][:, :], ACT.Copy
                  ).then_inc(acc_free[(j - DN_SHIFT) % 2], 1)

            for i in range(4):
                fill_at(i, 0)

            def at_part(part, t):
                U, j = au[t % 2], J_AT - DN_SHIFT + 4 * t
                if part == 0:
                    silu_tables()
                    filled(act, j + 3)
                    A(U[:, 3, :], U[:, 3, :], ACT.Silu).then_inc(S["at_silu"], 1)
                    exp_tables()
                    for i in range(2):
                        wait(act, S["at_ss"], 3 * t)
                        A(a_sq[:, i, :], U[:, i, :], ACT.Square).then_inc(S["at_sq"], 1)
                    for i in range(2):
                        act.wait_ge(S["at_ss"], 3 * t + i + 1)
                        wait(act, S["at_n"], 3 * t)
                        A(a_rs[:, i, :], (b2, b3)[i][:, :], ACT.Ln, scale=1.0 / AT_DH, bias=EPS
                          ).then_inc(S["at_rs"], 1)
                        act.wait_ge(S["at_rs"], 4 * t + 2 * i + 1)
                        A(a_rs[:, i, :], a_rs[:, i, :], ACT.Exp, scale=-0.5).then_inc(S["at_rs"], 1)
                    act.wait_ge(S["at_ss"], 3 * t + 3)
                    wait(act, S["at_o"], 8 * t)
                    A(a_v[:, :, :].rearrange("p b d -> p (b d)"), b4[:, :], ACT.Copy).then_inc(S["at_v"], 1)
                for i in (2 * part, 2 * part + 1):
                    n = 8 * t + i
                    act.wait_ge(S["at_mx"], n + 1)
                    A(a_l[i % 4][:, :], a_l[i % 4][:, :], ACT.Exp, bias=a_st[:, i, 0:1],
                      accum_out=a_st[:, i, 1:2]).then_inc(S["at_ex"], 1)
                if part:
                    at_copy(2 * part - 2, t)
                    at_copy(2 * part - 1, t)

            def at_copy(i, t):
                n = 8 * t + i
                act.wait_ge(S["at_tr"], n + 1)
                wait(act, S["at_o"], n - 1)
                A(a_pt[i % 2][:, :], (b2, b3)[i % 2][:, :], ACT.Copy).then_inc(S["at_pt"], 1)

            for t in range(4):
                for part in range(4):
                    at_part(part, t)
                    if t < 3:
                        if part == 0:
                            wait(act, S["at_lo"], t)
                        fill_at(part, t + 1)
                at_copy(6, t)
                at_copy(7, t)
                act.wait_ge(S["at_y"], t + 1)
                A(yh[:, 4 + t, :], a_y[:, :], ACT.Copy).then_inc(S["at_hi"], 1)
            for f in range(KT):
                act.wait_ge(S["out_tr"], f + 1)
                if f >= 2:
                    act.wait_ge(S[f"out_dma{f % 2}"], 16 * (f // 2))
                A(os_[f % 2][:, :], psum[2 + f % 4][:, :], ACT.Copy).then_inc(S["out_ev"], 1)

        @block.vector
        def _(dve):
            TT, TS, STT = dve.tensor_tensor, dve.tensor_scalar, dve.scalar_tensor_tensor

            def norm_scale(k, m, gain, keep=False):
                dve.wait_ge(S["nrm_rs"], 2 * k + 2)
                for f in range(KT):
                    if keep:
                        STT(xT[:, f, :], xT[:, f, :], pc(gain, f), rsn[:, :], ALU.mult, ALU.mult
                            ).then_inc(S["nrm_h"], 1)
                        continue
                    if f >= 2:
                        dve.wait_ge(S["nrm_hi"], 8 * m + f - 1)
                        dve.wait_ge(S["nrm_lo"], 8 * m + f - 1)
                    STT(htn[f % 2][:, :], xT[:, f, :], pc(gain, f), rsn[:, :], ALU.mult, ALU.mult
                        ).then_inc(S["nrm_h"], 1)
                    if f:
                        lo(k, m, f - 1)
                if not keep:
                    lo(k, m, KT - 1)

            def lo(k, m, f):
                dve.wait_ge(S["nrm_h"], 8 * k + f + 1)
                dve.wait_ge(S["nrm_hi"], 8 * m + f + 1)
                TT(hl[:, f, :], htn[f % 2][:, :], hh[:, f, :].bitcast(F32), ALU.subtract).then_inc(S["nrm_lo"], 1)

            dve.wait_ge(S["zero_set"], 1)
            dve.wait_ge(S["params_in"], 32)
            lg = par[:, PAR["lb"]:PAR["lb"] + 8]
            TT(lbt[:, 0, :], lg, lg, ALU.subtract).then_inc(S["lb_step"], 1)
            norm_scale(0, 0, "norm1")
            dve.wait_ge(S["lb_step"], 2)
            dve.reciprocal(lbt[:, 2, :], lbt[:, 1, :]).then_inc(S["lb_step"], 1)
            dve.wait_ge(S["lb_step"], 3)
            TT(lbt[:, 0, :], lbt[:, 1, :], lbt[:, 2, :], ALU.mult).then_inc(S["lb_step"], 1)
            dve.wait_ge(S["lb_step"], 4)
            TT(lbc[:, :], lbt[:, 0, :], lbt[:, 0, :], ALU.subtract).then_inc(S["lb_step"], 1)

            step = [0]

            def row(ins):
                step[0] += 1
                ins.then_inc(S["row_step"], 1)
                dve.wait_ge(S["row_step"], step[0])

            sign = cc(K_SIGN, 1)
            dve.wait_ge(S["slab_used"], 1)
            dve.wait_ge(S["wb_out"], 16 * AT_HEADS)
            dve.wait_ge(S["nrm_lo"], 8)
            STT(rz[:, :], acc[0][:, :], pc("rowb"), sign.broadcast_to([P, T]), ALU.add, ALU.mult
                ).then_inc(acc_free[0], 1)
            dve.wait_ge(acc_free[0], 1)
            row(TS(r3[:, :], rz[:, :], 0.0, None, ALU.max))
            row(STT(r1[:, :], rz[:, :], -1.0, rz[:, :], ALU.mult, ALU.min))
            dve.wait_ge(S["row_act"], 2)
            row(TS(r4[:, :], r2[:, :], 2.0, None, ALU.add))
            row(dve.reciprocal(r5[:, :], r4[:, :]))
            row(TT(r4[:, :], r2[:, :], r5[:, :], ALU.mult))
            row(TT(r2[:, :], r4[:, :], r4[:, :], ALU.mult))
            row(TS(r1[:, :], r2[:, :], 1.0 / 17, None, ALU.mult))
            for k in (15, 13, 11, 9, 7, 5, 3):
                row(STT(r1[:, :], r1[:, :], 1.0 / k, r2[:, :], ALU.add, ALU.mult))
            row(STT(r1[:, :], r1[:, :], 1.0, r4[:, :], ALU.add, ALU.mult))
            row(STT(r5[:, :], r1[:, :], 2.0, r3[:, :], ALU.mult, ALU.add))
            row(TS(rac[:, :], rac[:, :], -1.0, None, ALU.mult))
            row(TS(r4[:, :], r5[:, :], rac[:, 0:1], None, ALU.mult))
            dve.tensor_tensor_scan(cum[:, :], cc(K_RMASK, T), r4[:, :], 0.0, ALU.mult, ALU.add
                                   ).then_inc(S["row_a"], 1)
            dve.wait_ge(S["row_a"], 1)
            for b in range(NB):
                TS(rdg[:, b, :], ident[:, 0:MB_HEADS], cum[:, b * P + P - 1:b * P + P], None, ALU.mult
                   ).then_inc(S["row_done"], 1)
            def clamp_f(j0, dst, it=None):
                dve.wait_ge(S["slab_used"], lin(j0 + 1, it, 8))
                TS(dst, acc[j0 % 2][:, :], -40.0, None, ALU.max).then_inc(acc_free[j0 % 2], 1)

            clamp_f(J_HG + 1, unit[0][:, 1, :])
            dve.wait_ge(S["row_ev"], 1)
            dve.tensor_tensor_scan(rnm[:, :], ra[:, :], ra[:, :], 0.0, ALU.max, ALU.max).then_inc(S["rnm_done"], 1)
            dve.wait_ge(S["rnm_done"], 1)
            TS(rnm[:, :], rnm[:, :], -1.0, None, ALU.mult).then_inc(S["rnm_done"], 1)
            dve.wait_ge(S["row_mm"], 2)

            def cols(bank, n):
                return bank[:, :].rearrange("p (b r) -> p b r", b=NB)[:, :, 0:n]

            dve.tensor_copy(acol[:, :, :], cols(b5, ML_HEADS)).then_inc(S["row_done"], 1)
            TS(ncc[:, :, :], cols(b6, MB_HEADS), -1.0, None, ALU.mult).then_inc(S["row_done"], 1)
            dve.tensor_copy(dtc[:, :, :], cols(b7, MB_HEADS)).then_inc(S["row_done"], 1)
            dve.wait_ge(S["row_mm"], 3)
            dve.tensor_copy(totb[:, :, :], b4[:, 0:NB * MB_HEADS].rearrange("p (b h) -> p b h", b=NB)
                            ).then_inc(S["row_done"], 1)
            dve.wait_ge(S["row_done"], 8)
            TT(dend[:, 0, :], totb[:, 0, :], ncc[:, 0, :], ALU.add).then_inc(S["row_step"], 1)
            TT(dend[:, 3, :], totb[:, 2, :], ncc[:, 2, :], ALU.add).then_inc(S["row_step"], 1)
            TT(dend[:, 4, :], totb[:, 1, :], ncc[:, 1, :], ALU.add).then_inc(S["row_step"], 1)
            dve.wait_ge(S["row_step"], step[0] + 3)
            TT(dend[:, 1, :], dend[:, 0, :], totb[:, 1, :], ALU.add).then_inc(S["row_done"], 1)
            TT(dend[:, 5, :], dend[:, 4, :], totb[:, 2, :], ALU.add).then_inc(S["row_done"], 1)
            dve.wait_ge(S["row_done"], 10)
            TT(dend[:, 2, :], dend[:, 1, :], totb[:, 2, :], ALU.add).then_inc(S["row_done"], 1)
            dve.wait_ge(S["row_done"], 11)

            convs = [0]

            def conv4(j0, dst, w, b, i):
                bank = acc[j0 % 2]
                dve.wait_ge(S["slab_used"], j0 + 1)
                TS(dst, bank[:, :], pc(w, 4 * i + 3), pc(b, i), ALU.mult, ALU.add).then_inc(S["conv_step"], 1)
                for k in (2, 1, 0):
                    convs[0] += 1
                    dve.wait_ge(S["conv_step"], convs[0])
                    s = 3 - k
                    ins = STT(dst[:, s:], bank[:, 0:T - s], pc(w, 4 * i + k), dst[:, s:], ALU.mult, ALU.add)
                    ins.then_inc(S["conv_step"] if k else acc_free[j0 % 2], 1)

            def hg_diff(l, u):
                dve.wait_ge(S["hg_b"], u + 1)
                if l == 0:
                    wait(dve, S["hg_ex"], u * 15)
                    v = bb[:, :].rearrange("p (c n) -> p c n", n=P)
                    o = dd[0][:, :].rearrange("p (c n) -> p c n", n=P)
                    TT(o, v[:, :, P - 1:P].broadcast_to([P, NB, P]), v, ALU.subtract).then_inc(S["hg_d"], 1)
                    return
                n, half = P >> (l - 1), P >> l
                wait(dve, S["hg_ex"], u * 15 if l == 1 else u * 15 + (1 + 2 * (l - 2)))
                v = bb[:, :].rearrange("p (c n) -> p c n", n=n)
                o = dd[l % 2][:, :].rearrange("p (c n) -> p c n", n=n)
                TT(o, v, v[:, :, half - 1:half].broadcast_to([P, T // n, n]), ALU.subtract).then_inc(S["hg_d"], 1)

            def hg_scale(l, u, p):
                n, half = P >> (l - 1), P >> l
                dve.wait_ge(S["hg_ex"], u * 15 + (1 + 2 * l))
                wait(dve, S["hg_lv"], u * 8 + (l - 1))
                def v(ap):
                    return ap.rearrange("p (c n) -> p c n", n=n)
                q, k, e, z = v(unit[p][:, 0, :]), v(kk[:, :]), v(ex[l % 2][:, :]), v(zz[l % 2][:, :])
                TT(z[:, :, half:], q[:, :, half:], e[:, :, half:], ALU.mult).then_inc(S["hg_z"], 1)
                TT(z[:, :, :half], k[:, :, :half], e[:, :, :half], ALU.mult).then_inc(S["hg_z"], 1)

            def hg_merge(l, u):
                dve.wait_ge(S["hg_lv"], u * 8 + (l + 1))
                dve.wait_ge(S["hg_at"], u * 8 + l)
                dve.tensor_copy(tick[:, :], zero[:, :])
                mask = cc(K_LMASK + (l - 1) * P).bitcast(U32).unsqueeze(1).broadcast_to([P, NB, P])
                dve.copy_predicated(at_[:, :].rearrange("p (b t) -> p b t", b=NB), mask,
                                    (b2, b3)[l % 2][:, :].rearrange("p (b t) -> p b t", b=NB)
                                    ).then_inc(S["hg_at"], 1)

            def hg_part(part, u, p):
                U = unit[p]
                if part == 0:
                    dve.wait_ge(S["hg_l"], u * 2 + 2)
                    wait(dve, S["hg_f"], u * 1)
                    wait(dve, S["hg_b"], u * 1)
                    TT(lf[:, :], e1[:, :], e0[:, :], ALU.subtract).then_inc(S["hg_lf"], 1)
                    dve.wait_ge(S["hg_lf"], u + 1)
                    wait(dve, S["hg_eb"], u * 1)
                    wait(dve, S["hg_d"], u * 8)
                    dve.tensor_tensor_scan(bb[:, :], cc(K_HGMASK, T), lf[:, :], 0.0, ALU.mult, ALU.add
                                           ).then_inc(S["hg_b"], 1)
                    dve.wait_ge(S["hg_f"], u + 1)
                    wait(dve, S["hg_lv"], u * 8)
                    wait(dve, S["hg_z"], u * 14)
                    TS(kk[:, :], e1[:, :], -1.0, 1.0, ALU.mult, ALU.add).then_inc(S["hg_k"], 1)
                    hg_diff(0, u)
                    hg_diff(1, u)
                    dve.wait_ge(S["hg_k"], u + 1)
                    dve.wait_ge(S["hg_ex"], u * 15 + 1)
                    wait(dve, S["hg_tr"], u * 2)
                    TT(k1[:, :], kk[:, :], ex[0][:, :], ALU.mult).then_inc(S["hg_x"], 1)
                    dve.wait_ge(S["hg_eb"], u + 1)
                    dve.wait_ge(S["hg_silu"], u * 2 + 1)
                    wait(dve, S["hg_o"], u * 1)
                    TT(q1[:, :], U[:, 0, :], eb[:, :], ALU.mult).then_inc(S["hg_x"], 1)
                    dve.wait_ge(S["hg_lv"], u * 8 + 1)
                    TT(at_[:, :].rearrange("p (b t) -> p b t", b=NB), b2[:, :].rearrange("p (b t) -> p b t", b=NB),
                       ident.unsqueeze(1).broadcast_to([P, NB, P]), ALU.mult).then_inc(S["hg_at"], 1)
                    hg_scale(1, u, p)
                elif part == 1:
                    hg_diff(2, u)
                    hg_scale(2, u, p)
                    hg_diff(3, u)
                    hg_merge(1, u)
                    hg_scale(3, u, p)
                    dve.wait_ge(S["hg_stp"], u + 1)
                    wait(dve, S["hg_o"], u * 1)
                    dve.tensor_copy(blk(st_, 0), blk(b5, 0)).then_inc(S["hg_s"], 1)
                    for b in (1, 2):
                        dve.wait_ge(S["hg_s"], u * 3 + b)
                        STT(blk(st_, b), blk(st_, b - 1), eb[:, b * P + P - 1:b * P + P], blk(b5, b),
                            ALU.mult, ALU.add).then_inc(S["hg_s"], 1)
                    hg_merge(2, u)
                elif part == 2:
                    hg_diff(4, u)
                    hg_scale(4, u, p)
                    hg_diff(5, u)
                    hg_merge(3, u)
                    hg_scale(5, u, p)
                    hg_diff(6, u)
                    hg_merge(4, u)
                    hg_scale(6, u, p)
                    hg_merge(5, u)
                else:
                    hg_diff(7, u)
                    hg_scale(7, u, p)
                    hg_merge(6, u)
                    hg_merge(7, u)
                    dve.wait_ge(S["hg_rs"], u * 2 + 2)
                    wait(dve, S["hg_hi"], u * 1)
                    wait(dve, S["hg_lo"], u * 1)
                    STT(yth[:, :], b6[:, :], pc("hgg"), rsh[:, :], ALU.mult, ALU.mult).then_inc(S["hg_y"], 1)
                    dve.wait_ge(S["hg_y"], u * 2 + 1)
                    dve.wait_ge(S["hg_silu"], u * 2 + 2)
                    TT(yth[:, :], yth[:, :], U[:, 3, :], ALU.mult).then_inc(S["hg_y"], 1)
                    dve.wait_ge(S["hg_hi"], u + 1)
                    dve.wait_ge(S["hg_y"], u * 2 + 2)
                    TT(tile_of(yl, u), yth[:, :], tile_of(yh, u).bitcast(F32), ALU.subtract
                       ).then_inc(S["hg_lo"], 1)

            def hg_pair(it):
                for p in range(2):
                    for part in range(4):
                        hg_part(part, lin(p, it, 2), p)
                        if part == 1:
                            clamp_f(J_HG + 4 + 4 * p + 1, unit[1 - p][:, 1, :], it)

            hg_pair(None)
            with dve.Fori(1, HG_HEADS // 2 - 1) as it:
                hg_pair(it)
            for u in (HG_HEADS - 2, HG_HEADS - 1):
                for part in range(4):
                    hg_part(part, u, u % 2)
                    if u == HG_HEADS - 2:
                        if part == 1:
                            clamp_f(J_HG + 4 * (u + 1) + 1, unit[1 - u % 2][:, 1, :])
                    else:
                        for i in tiles_before(part, 6):
                            if i < 2:
                                conv4(J_ML0 + i, unit[0][:, i, :], "mlcw", "mlcb", 4 * i)

            def gates(b, j0):
                with dve.Fori(0, KT // 2) as it:
                    for f in range(2):
                        dve.wait_ge(S["slab_used"], it * 4 + (j0 + 2 * f + 2))
                        filled(dve, j0 + 2 * f, it, 4)
                        fo = it * 2 + f
                        dst = tile_of(mixed, fo) if b == 0 else tm[:, :]
                        if b:
                            wait(dve, S["g_acc"], it * 2 + (KT * (b - 1) + f))
                        STT(dst, tg[f][:, :], 1.0, acc[1 - j0 % 2][:, :], ALU.add, ALU.mult
                            ).then_inc(acc_free[1 - j0 % 2], 1)
                        if b:
                            filled(dve, j0 + 2 * f + 1, it, 4)
                            TT(tile_of(mixed, fo), tile_of(mixed, fo), tm[:, :], ALU.add).then_inc(S["g_acc"], 1)

            def ml_part(part, u):
                p = u % 2
                U = unit[p]
                if part == 0:
                    dve.wait_ge(S["ml_nm"], u + 1)
                    wait(dve, S["ml_pt"], 3 * u)
                    for b in range(NB):
                        STT(m_e[:, b * P:(b + 1) * P], blk(b5, b), acol[:, b, u:u + 1], clampm, ALU.add, ALU.min
                            ).then_inc(S["ml_dx"], 1)
                elif part == 1:
                    dve.wait_ge(S["ml_ex"], 4 * u + 4)
                    wait(dve, S["ml_num"], 3 * u)
                    for i, (bank, a, n) in enumerate(((b2, 0, 512), (b3, 512, 512), (b4, 1024, 256))):
                        dve.wait_ge(S["ml_qk"], 3 * u + i + 1)
                        STT(m_p[:, a:a + n], bank[:, 0:n], P ** -0.5, m_e[:, a:a + n], ALU.mult, ALU.mult
                            ).then_inc(S["ml_pt"], 1)
                elif part == 2:
                    dve.wait_ge(S["ml_num"], 3 * u + 3)
                    dve.wait_ge(S["ml_em"], u + 1)
                    wait(dve, S["ml_dn"], 3 * u)
                    STT(m_dn[:, :], b5[:, :], -1.0, m_em[:, :], ALU.mult, ALU.max).then_inc(S["ml_dn"], 1)
                    dve.wait_ge(S["ml_dn"], 3 * u + 1)
                    TT(m_dn[:, :], m_dn[:, :], b5[:, :], ALU.max).then_inc(S["ml_dn"], 1)
                    dve.wait_ge(S["ml_dn"], 3 * u + 2)
                    wait(dve, S["ml_h"], 2 * u)
                    dve.reciprocal(m_rd[:, :], m_dn[:, :]).then_inc(S["ml_dn"], 1)
                    dve.wait_ge(S["ml_dn"], 3 * u + 3)
                    wait(dve, S["ml_hi"], 2 * u)
                    wait(dve, S["ml_lo"], 2 * u)
                    for v in range(2):
                        TT(m_h[:, v, :], (b6, b7)[v][:, :], m_rd[:, :], ALU.mult).then_inc(S["ml_h"], 1)
                else:
                    dve.wait_ge(S["ml_rs"], 2 * u + 2)
                    dve.wait_ge(S["ml_sq"], 2 * u + 2)
                    dve.wait_ge(S["ml_tanh"], 2 * u + 2)
                    for v in range(2):
                        STT(m_h[:, v, :], m_h[:, v, :], pc("mlg", v), m_rs[:, :], ALU.mult, ALU.mult
                            ).then_inc(S["ml_y"], 1)
                        dve.wait_ge(S["ml_y"], 4 * u + 2 * v + 1)
                        STT(m_h[:, v, :], U[:, 4 + v, :], 1.0, m_h[:, v, :], ALU.add, ALU.mult
                            ).then_inc(S["ml_y"], 1)
                    for v in range(2):
                        dve.wait_ge(S["ml_hi"], 2 * u + v + 1)
                        dve.wait_ge(S["ml_y"], 4 * u + 4)
                        STT(yl[:, 2 * u + v, :], m_h[:, v, :], 0.5, yh[:, 2 * u + v, :].bitcast(F32),
                            ALU.mult, ALU.subtract).then_inc(S["ml_lo"], 1)

            def mb_head(g, h):
                n = 4 * g + h
                dve.wait_ge(S["mb_nm"], n + 1)
                wait(dve, S["mb_pt"], 3 * n)
                for b in range(NB):
                    STT(s_e[:, b * P:(b + 1) * P], blk(b5, b), ncc[:, b, n:n + 1], clampm, ALU.add, ALU.min
                        ).then_inc(S["mb_dx"], 1)
                dve.wait_ge(S["mb_ex"], 7 * n + 7)
                wait(dve, S["mb_ym"], n - 1)
                if h == 0:
                    dve.wait_ge(S["mb_cb"], g + 1)
                for bank, a, m in ((b2, 0, 512), (b3, 512, 512), (b4, 1024, 256)):
                    TT(s_p[n % 2][:, a:a + m], s_e[:, a:a + m], bank[:, 0:m], ALU.mult).then_inc(S["mb_pt"], 1)

            def mb_part(part, g):
                U = unit[g % 2]
                if part == 0:
                    wait(dve, S["mb_ym"], 4 * g)
                    for i in range(2):
                        dve.wait_ge(S["mb_tr"], 2 * g + i + 1)
                        TT(s_x[:, 2 * i:2 * i + 2], (b6, b7)[i][:, :].rearrange("p (b h d) -> p b h d", b=2, h=4),
                           dtc[:, 2 * i:2 * i + 2, 4 * g:4 * g + 4].unsqueeze(3).broadcast_to([P, 2, 4, 64]), ALU.mult
                           ).then_inc(S["mb_xd"], 1)
                mb_head(g, part)
                if part == 3:
                    wait(dve, S["mb_hi"], 2 * g)
                    wait(dve, S["mb_lo"], 2 * g)
                    dve.wait_ge(S["mb_ym"], 4 * g + 4)
                    dve.wait_ge(S["mb_silu"], 6 * g + 6)
                    for v in range(2):
                        STT(s_y[:, v, :], U[:, 2 + v, :], pc("mbd", 2 * g + v), (b6, b7)[v][:, :],
                            ALU.mult, ALU.add).then_inc(S["mb_y"], 1)
                        dve.wait_ge(S["mb_y"], 6 * g + 2 * v + 1)
                        TT(s_y[:, v, :], s_y[:, v, :], U[:, 4 + v, :], ALU.mult).then_inc(S["mb_y"], 1)
                    dve.wait_ge(S["mb_rs"], 2 * g + 2)
                    dve.wait_ge(S["mb_sq"], 2 * g + 2)
                    for v in range(2):
                        STT(s_y[:, v, :], s_y[:, v, :], pc("mbg", 2 * g + v), s_rs[:, :], ALU.mult, ALU.mult
                            ).then_inc(S["mb_y"], 1)
                    for v in range(2):
                        dve.wait_ge(S["mb_hi"], 2 * g + v + 1)
                        dve.wait_ge(S["mb_y"], 6 * g + 4 + v + 1)
                        TT(yl[:, 2 * g + v, :], s_y[:, v, :], yh[:, 2 * g + v, :].bitcast(F32), ALU.subtract
                           ).then_inc(S["mb_lo"], 1)

            gates(0, J_G0)
            for u in range(ML_HEADS):
                last = u + 1 == ML_HEADS
                for part in range(4):
                    ml_part(part, u)
                    for i in tiles_before(part, 6):
                        if last and i < 4:
                            conv4(J_MB0 + i, unit[0][:, i, :], "mbcw", "mbcb", (8, 12, 0, 1)[i])
                        elif not last and i < 2:
                            conv4(ml_slab(u + 1) + i, unit[1 - u % 2][:, i, :], "mlcw", "mlcb", 4 * i + u + 1)
            gates(1, J_G1)
            for g in range(MB_GROUPS):
                for part in range(4):
                    mb_part(part, g)
                    if g + 1 < MB_GROUPS:
                        for i in tiles_before(part, 6):
                            if i < 4:
                                conv4(mb_slab(g + 1) + i, unit[1 - g % 2][:, i, :], "mbcw", "mbcb",
                                      (8 + g + 1, 12 + g + 1, 2 * g + 2, 2 * g + 3)[i])
            gates(2, J_G2)
            for f in range(KT):
                dve.wait_ge(S["o_hi"], f + 1)
                STT(hl[:, f, :], mixed[:, f, :], 0.5, hh[:, f, :].bitcast(F32), ALU.mult, ALU.subtract
                    ).then_inc(S["o_lo"], 1)

            def add_residual(j0, used, it, per):
                for f in range(4):
                    t = j0 + f
                    dve.wait_ge(S["slab_used"], it * per + used(f))
                    fo = it * 4 + f
                    TT(tile_of(xT, fo), tile_of(xT, fo), acc[t % 2][:, :], ALU.add).then_inc(acc_free[t % 2], 1)

            with dve.Fori(0, KT // 4) as it:
                add_residual(J_O, lambda f: J_O + f + 1, it, 4)
            norm_scale(1, 1, "norm2")
            with dve.Fori(0, NF // 2) as it:
                for p in range(2):
                    j = it * 2 + p
                    for v, buf in ((0, f_g), (1, f_v)):
                        bank = acc[(J_UP + v) % 2]
                        w0 = it * 6 + (3 * NF * v + 3 * p)
                        d = buf[p]
                        dve.wait_ge(S["up_c"], it * 4 + (2 * p + v + 1))
                        STT(d[:, 1:], bank[:, 0:T - 1], pc("fcw", w0 + 1), d[:, 1:], ALU.mult, ALU.add
                            ).then_inc(S["up_s1"], 1)
                        dve.wait_ge(S["up_s1"], it * 4 + (2 * p + v + 1))
                        STT(d[:, 2:], bank[:, 0:T - 2], pc("fcw", w0), d[:, 2:], ALU.mult, ALU.add
                            ).then_inc(acc_free[(J_UP + v) % 2], 1)
                    dve.wait_ge(S["up_sg"], j + 1)
                    filled(dve, J_UP + 2 * p + 1, it, 4)
                    TT(f_s[p][:, :], f_s[p][:, :], f_v[p][:, :], ALU.mult).then_inc(S["up_a"], 1)
                    dve.wait_ge(S["up_hi"], j + 1)
                    TT(tile_of(fl, j), f_s[p][:, :], tile_of(fh, j).bitcast(F32), ALU.subtract
                       ).then_inc(S["up_lo"], 1)
            with dve.Fori(0, KT // 4) as it:
                add_residual(J_DN, lambda f: J_DN + 3 * f + 3, it, 12)
            norm_scale(2, None, "final", keep=True)
            norm_scale(3, 2, "normw2")
            def conv_tile(it):
                t0 = J_CV - DN_SHIFT
                filled(dve, t0, it, 4)
                dve.wait_ge(S["slab_used"], it * 4 + (J_CV + 3))
                TT(c_p[:, :], c_u[:, :], acc[(t0 + 2) % 2][:, :], ALU.mult).then_inc(acc_free[(t0 + 2) % 2], 1)
                filled(dve, t0 + 2, it, 4)
                wait(dve, S["cv_hi"], it * 1)
                wait(dve, S["cv_lo"], it * 1)
                n = it * 5
                TS(c_y[:, :], c_p[:, :], pc("cw2", it * 3 + 1), pc("cb2", it * 1), ALU.mult, ALU.add
                   ).then_inc(S["cv_y"], 1)
                dve.wait_ge(S["cv_y"], n + 1)
                STT(c_y[:, 1:], c_p[:, 0:T - 1], pc("cw2", it * 3), c_y[:, 1:], ALU.mult, ALU.add
                    ).then_inc(S["cv_y"], 1)
                dve.wait_ge(S["cv_y"], n + 2)
                STT(c_y[:, 0:T - 1], c_p[:, 1:], pc("cw2", it * 3 + 2), c_y[:, 0:T - 1], ALU.mult, ALU.add
                    ).then_inc(S["cv_y"], 1)
                filled(dve, t0 + 1, it, 4)
                dve.wait_ge(S["cv_y"], n + 3)
                TT(c_y[:, :], c_y[:, :], c_b[:, :], ALU.mult).then_inc(S["cv_y"], 1)
                filled(dve, t0 + 3, it, 4)
                dve.wait_ge(S["cv_y"], n + 4)
                TT(c_y[:, :], c_y[:, :], c_z[:, :], ALU.mult).then_inc(S["cv_y"], 1)
                dve.wait_ge(S["cv_hi"], it + 1)
                TT(tile_of(yl, it), c_y[:, :], tile_of(yh, it).bitcast(F32), ALU.subtract).then_inc(S["cv_lo"], 1)

            conv_tile(0)
            with dve.Fori(1, 4) as it:
                conv_tile(it)

            dve.memset(a_k[0][64:P, :], 0.0).then_inc(S["kz_set"], 1)
            dve.memset(a_k[1][0:64, :], 0.0).then_inc(S["kz_set"], 1)
            dve.wait_ge(S["kz_set"], 2)
            dve.wait_ge(S["wb_in"], 16)
            dve.wait_ge(S["cv_lo"], 4)

            def at_part(part, t):
                U, j = au[t % 2], J_AT - DN_SHIFT + 4 * t
                if part == 0:
                    wait(dve, S["at_s"], 8 * t)
                    dve.wait_ge(S["at_rs"], 4 * t + 2)
                    STT(a_q[:, :], U[:, 0, :], pc("qn"), a_rs[:, 0, :], ALU.mult, ALU.mult).then_inc(S["at_n"], 1)
                    dve.wait_ge(S["at_rs"], 4 * t + 4)
                    for h in range(2):
                        r = slice(64 * h, 64 * h + 64)
                        STT(a_k[h][r, :], U[r, 1, :], par[r, PAR["kn"]:PAR["kn"] + 1], a_rs[r, 1, :],
                            ALU.mult, ALU.mult).then_inc(S["at_n"], 1)
                for i in (2 * part, 2 * part + 1):
                    n = 8 * t + i
                    head, qb = 2 * t + i // 4, i % 4
                    lg_ = a_l[i % 4]
                    dve.wait_ge(S["at_s"], n + 1)
                    wait(dve, S["at_tr"], n - 3)
                    STT(lg_[:, :], (b5, b6)[i % 2][:, :], AT_DH ** -0.5,
                        wb[:, head, (3 - qb) * P:(3 - qb) * P + T], ALU.mult, ALU.add).then_inc(S["at_l"], 1)
                    dve.wait_ge(S["at_l"], n + 1)
                    dve.tensor_reduce(a_st[:, i, 0:1], lg_[:, :], AX_X, ALU.max, negate=True
                                      ).then_inc(S["at_mx"], 1)
                for i in (2 * part, 2 * part + 1):
                    n = 8 * t + i
                    dve.wait_ge(S["at_ex"], n + 1)
                    dve.reciprocal(a_st[:, i, 2:3], a_st[:, i, 1:2]).then_inc(S["at_sum"], 1)
                    dve.wait_ge(S["at_sum"], n + 1)
                    TS(a_l[i % 4][:, :], a_l[i % 4][:, :], a_st[:, i, 2:3], None, ALU.mult).then_inc(S["at_p"], 1)

            for t in range(4):
                for part in range(4):
                    at_part(part, t)
                dve.wait_ge(S["at_o"], 8 * t + 8)
                dve.wait_ge(S["at_silu"], t + 1)
                wait(dve, S["at_hi"], t)
                wait(dve, S["at_lo"], t)
                TT(a_y[:, :], b7[:, :], au[t % 2][:, 3, :], ALU.mult).then_inc(S["at_y"], 1)
                dve.wait_ge(S["at_hi"], t + 1)
                dve.wait_ge(S["at_y"], t + 1)
                TT(yl[:, 4 + t, :], a_y[:, :], yh[:, 4 + t, :].bitcast(F32), ALU.subtract).then_inc(S["at_lo"], 1)
            with dve.Fori(0, KT // 4) as it:
                for f in range(4):
                    t = J_O2 - DN_SHIFT + f
                    dve.wait_ge(S["slab_used"], it * 4 + (J_O2 + f + 1))
                    fo = it * 4 + f
                    TT(tile_of(xT, fo), tile_of(xT, fo), acc[t % 2][:, :], ALU.add).then_inc(acc_free[t % 2], 1)


def bucket(rel):
    n = np.abs(rel)
    nf = np.maximum(n, 1).astype(np.float32)
    large = 8 + (np.log(nf / np.float32(8)) / np.float32(np.log(128.0)) * np.float32(8)).astype(np.int32)
    return np.where(rel > 0, 16, 0) + np.where(n < 8, n, np.minimum(large, 15))


def constants():
    c = np.zeros((P, N_CONST), np.float32)
    i = np.arange(P)
    eye = np.eye(P, dtype=np.float32)
    c[:, K_ID:K_ID + P] = eye
    c[:, K_NID:K_NID + P] = -eye
    c[:, K_ONES:K_ONES + P] = 1
    c[:, K_BD:K_BD + P] = (i[:, None] // AT_DH) == (i[None] // AT_DH)
    for h in range(ML_HEADS):
        c[ROW_I + h, K_SELI + h] = 1
        c[ROW_F + h, K_NSELF + h] = -1
    c[:, K_CLAMP:K_CLAMP + P] = np.where(i[:, None] <= i[None], 0.0, NEG)
    for l in range(1, 8):
        n, half = P >> (l - 1), P >> l
        s, t = i[:, None], i[None]
        c[:, K_LMASK + (l - 1) * P:K_LMASK + l * P] = (s // n == t // n) & (s % n < half) & (t % n >= half)
    start = np.where(np.arange(T) % P == 0, 0.0, 1.0)
    c[:, K_HGMASK:K_HGMASK + T] = start
    c[:, K_RMASK:K_RMASK + T] = 1
    c[:ROW_I, K_RMASK:K_RMASK + T] = start
    c[:, K_SIGN] = 1
    c[ROW_F:ROW_F + 32, K_SIGN] = -1
    hot = np.zeros((P, W_LINE), np.float32)
    d = np.arange(1 - T, T)
    hot[bucket(d), np.arange(2 * T - 1)] = 1
    count = (np.abs(d) <= 64) * 1 + ((d % 4 == 0) & (np.abs(d) <= 256)) + (d % 16 == 0)
    hot[32, :2 * T - 1] = np.where(count > 0, np.log(np.maximum(count, 1)), NEG)
    return c, hot


def slabs_of(i):
    w_in, w_up, w_dn, w2 = i["w_in"][0], i["w_up"][0], i["w_down"][0], i["w_in_2"]
    br = (i["w_br_hg"][0], i["w_br_ml"][0], i["w_br_mb"][0])
    a = np.zeros((N_SLABS, P, KT * P), np.float32)

    def put(j, w, c, k0=0, n=KT):
        a[j].reshape(P, KT, P)[:, :n] = w[k0 * P:(k0 + n) * P, c:c + P].reshape(n, P, P).transpose(1, 0, 2)

    small = a[J_SMALL].reshape(P, KT, P)
    for row, c, n in ((ROW_DT, C_MBDT, MB_HEADS), (ROW_I, C_MLIF, ML_HEADS), (ROW_F, C_MLIF + ML_HEADS, ML_HEADS)):
        small[:, :, row:row + n] = w_in[:, c:c + n].reshape(KT, P, n).transpose(1, 0, 2)
    for u in range(HG_HEADS):
        for k, c in enumerate((C_HGQ, C_HGF, C_HGI, C_HGG)):
            put(J_HG + 4 * u + k, w_in, c + P * u)
    for u in range(ML_HEADS):
        for k, c in enumerate((C_MLQ + P * u, C_MLK + P * u, C_MLV + 2 * P * u, C_MLV + 2 * P * u + P,
                               C_MLO + 2 * P * u, C_MLO + 2 * P * u + P)):
            put(ml_slab(u) + k, w_in, c)
    for g in range(MB_GROUPS):
        for k, c in enumerate((C_MBX + 1024 + P * g, C_MBX + 1536 + P * g, C_MBX + 2 * P * g, C_MBX + 2 * P * g + P,
                               C_MBZ + 2 * P * g, C_MBZ + 2 * P * g + P)):
            put(mb_slab(g) + k, w_in, c)
    for b, j in enumerate((J_G0, J_G1, J_G2)):
        for f in range(KT):
            put(j + 2 * f, w_in, C_GATE + D * b + P * f)
            put(j + 2 * f + 1, br[b], P * f)
    for f in range(KT):
        put(J_O + f, i["w_out"][0], P * f)
        put(J_O2 + f, i["w_out_2"], P * f)
        for c, n in enumerate(DN_CHUNKS):
            put(J_DN + 3 * f + c, w_dn, P * f, 8 * c, n)
    for j in range(NF):
        put(J_UP + 2 * j, w_up, P * j)
        put(J_UP + 2 * j + 1, w_up, D_FF + P * j)
    for t in range(4):
        for k in range(4):
            put(J_CV + 4 * t + k, w2, 512 * k + P * t)
            put(J_AT + 4 * t + k, w2, 2048 + 512 * k + P * t)
    return a


def params_of(i):
    a = np.zeros((P, N_PAR), np.float32)

    def put(name, v):
        a[:, PAR[name]:PAR[name] + v.shape[1]] = v

    def cols(v):
        return v.reshape(-1, P).T

    def taps(w):
        return w.reshape(w.shape[0], -1, P).transpose(2, 1, 0).reshape(P, -1)

    put("norm1", cols(i["norm1_g"]))
    put("norm2", cols(i["norm2_g"]))
    put("final", cols(i["final_g"]))
    put("normw2", cols(i["norm_w_2"]))
    put("lb", cols(i["hg_lb_logits"]))
    put("hgg", cols(i["hg_norm_g"]))
    put("mlcw", taps(i["ml_conv_w"][0]))
    put("mlcb", cols(i["ml_conv_b"]))
    put("mlg", cols(i["ml_norm_g"]))
    put("mbcw", taps(i["mb_conv_w"][0]))
    put("mbcb", cols(i["mb_conv_b"]))
    put("mbg", cols(i["mb_norm_g"]))
    put("mbd", cols(np.repeat(i["mb_d"].reshape(-1), 64)))
    put("fcw", taps(i["ffn_conv_w"][0]))
    put("fcb", cols(i["ffn_conv_b"]))
    put("cw2", taps(i["conv_w_2"]))
    put("cb2", cols(i["conv_b_2"]))
    put("qn", cols(np.tile(i["q_norm_w_2"], 2)))
    put("kn", cols(np.tile(i["k_norm_w_2"], 2)))
    a[ROW_DT:ROW_DT + MB_HEADS, PAR["rowb"]] = i["mb_dt_bias"][0]
    a[ROW_I:ROW_I + ML_HEADS, PAR["rowb"]] = i["ml_gate_b"][0, :ML_HEADS]
    a[ROW_F:ROW_F + ML_HEADS, PAR["rowb"]] = i["ml_gate_b"][0, ML_HEADS:]
    a[ROW_DT:ROW_DT + MB_HEADS, PAR["alog"]] = i["mb_a_log"][0]
    a[:32, PAR["rel"]:PAR["rel"] + AT_HEADS] = i["rel_bias_2"]
    a[32, PAR["rel"]:PAR["rel"] + AT_HEADS] = 1
    return a


def kernel(**inputs):
    import concourse.bacc as bacc
    from concourse.bass_utils import run_bass_kernel_spmd

    i = {k: np.asarray(v) for k, v in inputs.items()}
    con, hot = constants()
    arrays = {"slabs": slabs_of(i), "x": np.ascontiguousarray(i["x"]), "params": params_of(i), "consts": con,
              "onehot": hot}
    nc = bacc.Bacc("TRN2", target_bir_lowering=False, num_devices=1)
    ins = [nc.dram_tensor(n, a.shape, F32, kind="ExternalInput").ap() for n, a in arrays.items()]
    bias_scratch = nc.dram_tensor("bias_scratch", (AT_HEADS, P, W_LINE), F32).ap()
    out = nc.dram_tensor("out", (1, T, D), F32, kind="ExternalOutput").ap()
    build(nc, *ins, bias_scratch, out)
    r = run_bass_kernel_spmd(nc, [arrays], core_ids=[0])
    return r.results[0]["out"]
```

```python
from contextlib import ExitStack

import numpy as np

import concourse.bass as bass
from concourse import mybir

P = 128
T = 512
NB = T // P
D = 1024
KT = D // P
F32 = mybir.dt.float32
F32R = mybir.dt.float32r
U32 = mybir.dt.uint32
ALU = mybir.AluOpType
ACT = mybir.ActivationFunctionType
AX_X = mybir.AxisListType.X
EPS = 1e-6
NEG = -1e30

HG_HEADS, ML_HEADS, MB_GROUPS, MB_HEADS = 8, 4, 4, 16
D_FF = 2816
NF = D_FF // P
AT_HEADS, AT_DH = 8, 64

C_HGQ, C_HGF, C_HGI, C_HGG = 0, 1024, 2048, 3072
C_MLQ, C_MLK, C_MLV, C_MLIF, C_MLO = 4096, 4608, 5120, 6144, 6152
C_MBZ, C_MBX, C_MBDT, C_GATE = 7176, 8200, 10248, 10264

HG_F, HG_Q, HG_G, HG_I = range(4)

J_SMALL = 0
J_HG = 1
J_ML0 = J_HG + 4 * HG_HEADS
J_G0 = J_ML0 + 6
J_ML1 = J_G0 + 16
J_MB0 = J_ML1 + 18
J_G1 = J_MB0 + 6
J_MB1 = J_G1 + 16
J_G2 = J_MB1 + 18
J_O = J_G2 + 16
J_UP = J_O + 8
J_DN = J_UP + 2 * NF
DN_CHUNKS = (8, 8, 6)
J_CV = J_DN + 24
J_AT = J_CV + 16
J_O2 = J_AT + 16
N_SLABS = J_O2 + 8
DN_SHIFT = 16

K_ID, K_NID, K_ONES, K_BD, K_SELI, K_NSELF, K_CLAMP = (P * i for i in range(7))
K_LMASK = 7 * P
K_HGMASK = K_LMASK + 7 * P
K_RMASK = K_HGMASK + T
K_SIGN = K_RMASK + T
N_CONST = K_SIGN + 1

_PAR = [("norm1", 8), ("norm2", 8), ("final", 8), ("normw2", 8), ("lb", 8), ("hgg", 1), ("mlcw", 32), ("mlcb", 8),
        ("mlg", 2), ("mbcw", 64), ("mbcb", 16), ("mbg", 8), ("mbd", 8), ("fcw", 132), ("fcb", 44), ("cw2", 12),
        ("cb2", 4), ("qn", 1), ("kn", 1), ("rowb", 1), ("alog", 1), ("rel", 8)]
PAR = {}
N_PAR = 0
for _n, _w in _PAR:
    PAR[_n] = N_PAR
    N_PAR += _w

ROW_DT, ROW_I, ROW_F = 0, 32, 64
W_BIAS = 896
W_LINE = 1024


def ml_slab(u):
    return J_ML0 if u == 0 else J_ML1 + 6 * (u - 1)


def mb_slab(g):
    return J_MB0 if g == 0 else J_MB1 + 6 * (g - 1)


def lin(c, it, k):
    return c if it is None else it * k + c


def wait(eng, sem, n):
    if not isinstance(n, int) or n > 0:
        eng.wait_ge(sem, n)


def tiles_before(part, n):
    return {0: [[], [], [], []], 4: [[0], [1], [2], [3]], 6: [[0], [1, 2], [3], [4, 5]]}[n][part]


def build(nc, slabs, x, par_d, const_d, onehot_d, bias_scratch, out):
    with ExitStack() as ctx:
        start = -(-nc.sbuf_base // 64) * 64

        def arena(at):
            pos = [at]

            def take(name, shape, dt=F32):
                n = 4
                for s in shape[1:]:
                    n *= s
                pos[0] = -(-pos[0] // 64) * 64
                t = nc.alloc_sbuf_tensor_at(name, shape, dt, offset=pos[0])
                pos[0] += n
                assert pos[0] <= nc.sbuf_usable_end, (name, pos[0])
                return t
            return take, pos

        sb, sb_pos = arena(start)
        raw = sb("raw", [P, 4, KT, P])
        wh = sb("wh", [P, 2, KT, P], F32R)
        wl = sb("wl", [P, 2, KT, P], F32R)
        xT = sb("xT", [P, KT, T])
        hh = sb("hh", [P, KT, T], F32R)
        hl = sb("hl", [P, KT, T], F32R)
        con = sb("con", [P, N_CONST])
        par = sb("par", [P, N_PAR])
        zero = sb("zero", [P, 1])
        tick = sb("tick", [P, 1])
        lbc = sb("lbc", [P, 8])
        lbt = sb("lbt", [P, 3, 8])
        sb_pos[0] = -(-sb_pos[0] // 64) * 64
        y_at = sb_pos[0]
        yh = sb("yh", [P, KT, T], F32R)
        yl = sb("yl", [P, KT, T], F32R)
        area = sb_pos[0]

        mx, mx_pos = arena(area)
        mixed = mx("mixed", [P, KT, T])
        unit_at = mx_pos[0]
        unit = [mx(f"unit{i}", [P, 6, T]) for i in range(2)]
        gbuf = arena(unit_at)[0]("gbuf", [P, KT, T])
        cum = mx("cum", [P, T])
        rnm = mx("rnm", [P, T])
        acol = mx("acol", [P, NB, ML_HEADS])
        dtc = mx("dtc", [P, NB, MB_HEADS])
        ncc = mx("ncc", [P, NB, MB_HEADS])
        totb = mx("totb", [P, NB, MB_HEADS])
        dend = mx("dend", [P, 6, MB_HEADS])
        scratch = mx_pos[0]

        psum = [ctx.enter_context(nc.psum_tensor(f"bank{i}", [P, T], F32)) for i in range(8)]
        acc = psum[:2]
        b2, b3, b4, b5, b6, b7 = psum[2:]

        names = """params_in x_in0 x_in1 onehot_in slab_hi slab_split slab_used acc_free0 acc_free1 zero_set
            pro_tr pro_xT nrm_sq nrm_ss nrm_rs nrm_h nrm_hi nrm_lo lb_step
            wb_mm wb_ev wb_out wb_in row_step row_act row_mm row_ev row_a row_done rnm_done
            conv_step
            hg_silu hg_e hg_l hg_lf hg_b hg_f hg_k hg_d hg_ex hg_eb hg_x hg_tr hg_v hg_kt hg_lv hg_z hg_at hg_stp
            hg_s hg_o hg_sq hg_ss hg_rs hg_y hg_hi hg_lo
            ml_silu ml_tanh ml_nm ml_tr ml_v ml_dx ml_ex ml_qk ml_pt ml_num ml_nm2 ml_em ml_h ml_dn ml_sq ml_ss
            ml_rs ml_y ml_hi ml_lo
            mb_silu mb_tr mb_xd mb_cb mb_nm mb_dx mb_ex mb_pt mb_ym mb_y mb_sq mb_ss mb_rs mb_hi mb_lo
            g_tanh g_acc o_hi o_lo up_c up_s1 up_sg up_a up_hi up_lo
            cv_in cv_p cv_y cv_hi cv_lo
            at_silu at_sq at_ss at_tr at_rs at_v at_n at_s at_l at_mx at_ex at_sum at_p at_pt at_pe at_o at_y
            at_hi at_lo kz_set out_tr out_ev out_dma0 out_dma1""".split()
        S = {n: ctx.enter_context(nc.semaphore(n)) for n in names}
        slab_in = [ctx.enter_context(nc.semaphore(f"slab_in{i}")) for i in range(4)]
        acc_free = [S["acc_free0"], S["acc_free1"]]

        def cc(k, n=P):
            return con[:, k:k + n]

        ident, nident, ones, clampm = cc(K_ID), cc(K_NID), cc(K_ONES), cc(K_CLAMP)

        def pc(name, i=0):
            if isinstance(i, int):
                return par[:, PAR[name] + i:PAR[name] + i + 1]
            return par[:, bass.ds(i + PAR[name], 1)]

        def tile_of(buf, f):
            if isinstance(f, int):
                return buf[:, f, :]
            return buf[:, bass.ds(f, 1), :].rearrange("p a t -> p (a t)")

        def blk(ap, b, n=1):
            return ap[:, b * P:(b + n) * P]

        def stage(at=scratch):
            return arena(at)[0]

        pr = stage()
        xs = pr("xs", [P, NB, D])
        nr_at = y_at + NF * 4 * T
        nr, nr_pos = arena(nr_at)
        sqn = [nr(f"sqn{i}", [P, T]) for i in range(2)]
        rsn = nr("rsn", [P, T])
        htn = [nr(f"htn{i}", [P, T]) for i in range(2)]
        ro = stage(y_at)
        rz, r1, r2, r3, r4, r5, ra = (ro(f"row{i}", [P, T]) for i in range(7))
        rdg = ro("rdg", [P, NB, MB_HEADS])
        rac = ro("rac", [P, 1])
        oneh = ro("oneh", [P, W_LINE])
        wrow = ro("wrow", [AT_HEADS, W_LINE])

        hg = stage()
        e0, e1, lf, bb, kk, eb, k1, q1, at_ = (hg(f"hg{i}", [P, T]) for i in range(9))
        dd = [hg(f"hgd{i}", [P, T]) for i in range(2)]
        ex = [hg(f"hgx{i}", [P, T]) for i in range(2)]
        zz = [hg(f"hgz{i}", [P, T]) for i in range(2)]
        hm = stage(area)
        sqh, rsh, yth, vt = (hm(f"hgm{i}", [P, T]) for i in range(4))
        kt_ = hm("hgkt", [P, 3 * P])
        st_ = hm("hgst", [P, 3 * P])

        ml = stage()
        m_e = ml("m_e", [P, 1280])
        m_p = ml("m_p", [P, 1280])
        m_v = ml("m_v", [P, NB, 2 * P])
        m_em, m_dn, m_rd, m_rs = (ml(f"m_{i}", [P, T]) for i in range(4))
        m_h = ml("m_h", [P, 2, T])
        m_sq = ml("m_sq", [P, 2, T])
        mb = stage()
        s_e = mb("s_e", [P, 1280])
        s_p = [mb(f"s_p{i}", [P, 1280]) for i in range(2)]
        s_x = mb("s_x", [P, NB, 4, 64])
        s_y = mb("s_y", [P, 2, T])
        s_sq = mb("s_sq", [P, 2, T])
        s_rs = mb("s_rs", [P, T])
        gs = stage()
        tg = [gs(f"tg{i}", [P, T]) for i in range(2)]
        tm = gs("tm", [P, T])

        nr_end = nr_pos[0]
        fl = stage(y_at)("fl", [P, NF, T], F32R)
        ff = stage(nr_end)
        fh = ff("fh", [P, NF, T], F32R)
        f_g = [ff(f"f_g{i}", [P, T]) for i in range(2)]
        f_v = [ff(f"f_v{i}", [P, T]) for i in range(2)]
        f_s = [ff(f"f_s{i}", [P, T]) for i in range(2)]

        sec = stage(nr_end)
        wb = sec("wb", [P, AT_HEADS, W_BIAS])
        au = [sec(f"au{i}", [P, 4, T]) for i in range(2)]
        c_u, c_b, c_p, c_y, c_z = cbuf = [sec(f"c_{i}", [P, T]) for i in range(5)]
        a_l, a_q = cbuf[:4], cbuf[4]
        an = stage(area)
        a_rs = an("a_rs", [P, 2, T])
        a_pt = [an(f"a_pt{i}", [P, T]) for i in range(2)]
        a_sq = an("a_sq", [P, 2, T])
        a_k = [sec(f"a_k{i}", [P, T]) for i in range(2)]
        a_v = sec("a_v", [P, NB, P])
        a_st = sec("a_st", [P, 8, 3])
        a_y = sqn[0]
        os_ = htn

        OFF = {0: (512, 384), 2: (896, 128), 1: (1024, 256)}

        block = ctx.enter_context(nc.Block())

        def filled(eng, j0, it=None, k=0):
            eng.wait_ge(acc_free[j0 % 2], lin(j0 // 2 + 1, it, k // 2))

        @block.sync
        def _(sp):
            def load(slot, j, use):
                wait(sp, S["slab_split"], use)
                src = slabs[bass.ds(j, 1)] if not isinstance(j, int) else slabs[j:j + 1]
                sp.dma_start(raw[:, slot:slot + 1].rearrange("p a k f -> p a (k f)"),
                             src.rearrange("a p n -> p a n")).then_inc(slab_in[slot], 16)

            for i in range(2):
                c = slice(i * D // 2, (i + 1) * D // 2)
                sp.dma_start(xs[:, :, c], x.rearrange("a (b p) d -> p (a b) d", p=P)[:, :, c]
                             ).then_inc(S[f"x_in{i}"], 16)
            for j in range(4):
                load(j, j, 0)
            with sp.Fori(1, N_SLABS // 4) as it:
                for i in range(4):
                    load(i, it * 4 + i, it * 4 + (i - 3))
            for j in range(N_SLABS // 4 * 4, N_SLABS):
                load(j % 4, j, j - 3)
            for f in range(KT):
                sp.wait_ge(S["out_ev"], f + 1)
                sp.dma_start(out.rearrange("a (b p) d -> p (a b) d", p=P)[:, :, f * P:(f + 1) * P],
                             os_[f % 2][:, :].rearrange("p (b d) -> p b d", b=NB)
                             ).then_inc(S[f"out_dma{f % 2}"], 16)
            sp.wait_ge(S["out_dma0"], 16 * KT // 2)
            sp.wait_ge(S["out_dma1"], 16 * KT // 2)

        @block.gpsimd
        def _(pool):
            nc.gpsimd.memset(zero[:, :], 0.0).then_inc(S["zero_set"], 1)
            pool.wait_ge(S["zero_set"], 1)

            def split(i, j, nth):
                r = raw[:, i].rearrange("p k f -> p (k f)")
                h = wh[:, i % 2].rearrange("p k f -> p (k f)")
                lo = wl[:, i % 2].rearrange("p k f -> p (k f)")
                pool.wait_ge(slab_in[i], nth)
                wait(pool, S["slab_used"], j - 1)
                pool.tensor_tensor(h, r, zero[:, 0:1].broadcast_to([P, KT * P]), ALU.add).then_inc(S["slab_hi"], 1)
                pool.wait_ge(S["slab_hi"], j + 1)
                pool.tensor_tensor(lo, r, h.bitcast(F32), ALU.subtract).then_inc(S["slab_split"], 1)

            for j in range(4):
                split(j, j, 16)
            with pool.Fori(1, N_SLABS // 4) as it:
                for i in range(4):
                    split(i, it * 4 + i, it * 16 + 16)
            for j in range(N_SLABS // 4 * 4, N_SLABS):
                split(j % 4, j, 16 * (j // 4 + 1))

        @block.tensor
        def _(pe):
            mm = pe.matmul

            def project(j0, it=None, k=0, src=(hh, hl), n=KT, base=0, t0=None, first=True, last=True,
                        ready=None):
                t0 = j0 if t0 is None else t0
                bank, s = acc[t0 % 2], j0 % 2
                pe.wait_ge(S["slab_split"], lin(j0 + 1, it, k))
                if first:
                    wait(pe, acc_free[t0 % 2], lin(t0 // 2, it, k // 2))
                for b in range(n):
                    if ready:
                        pe.wait_ge(ready[0], ready[1] + b)
                    xh, xl = src[0][:, base + b, :], src[1][:, base + b, :]
                    mm(bank[:, :], wh[:, s, b, :], xh, start=first and b == 0, stop=False)
                    mm(bank[:, :], wh[:, s, b, :], xl, start=False, stop=False)
                    ins = mm(bank[:, :], wl[:, s, b, :], xh, start=False, stop=last and b == n - 1)
                ins.then_inc(S["slab_used"], 1)

            def norm_sum(k, f):
                pe.wait_ge(S["nrm_sq"], 8 * k + f + 1)
                if f == 0:
                    wait(pe, S["nrm_rs"], 2 * k)
                mm(b6[:, :], ones, sqn[f % 2][:, :], start=f == 0, stop=f == KT - 1).then_inc(S["nrm_ss"], 1)

            def norm(k):
                for f in range(KT):
                    norm_sum(k, f)

            pe.wait_ge(S["params_in"], 32)
            for f in range(KT):
                pe.wait_ge(S[f"x_in{f // 4}"], 16)
                wait(pe, S["pro_xT"], f - 3)
                for b in range(NB):
                    ins = pe.transpose(blk(psum[2 + f % 4], b), xs[:, b, f * P:(f + 1) * P], ident)
                ins.then_inc(S["pro_tr"], 1)
            norm(0)
            pe.wait_ge(S["onehot_in"], 16)
            pe.wait_ge(S["pro_xT"], 8)
            for c, bank in ((0, b7), (1, b5)):
                mm(bank[0:AT_HEADS, :], par[:, PAR["rel"]:PAR["rel"] + AT_HEADS], oneh[:, c * T:(c + 1) * T],
                   start=True, stop=True).then_inc(S["wb_mm"], 1)
            project(J_SMALL, ready=(S["nrm_lo"], 1))
            for i in range(4):
                project(J_HG + i)
            pe.wait_ge(S["row_a"], 1)
            mm(b4[:, :], cc(K_SELI), rz[:, :], start=True, stop=False)
            mm(b4[:, :], cc(K_NSELF), cum[:, :], start=False, stop=True).then_inc(S["row_mm"], 1)
            pe.wait_ge(S["wb_ev"], 2)
            for b in range(NB):
                pe.transpose(blk(b6, b), blk(cum, b), ident)
            for b in range(NB):
                ins = pe.transpose(blk(b7, b), blk(r5, b), ident)
            ins.then_inc(S["row_mm"], 1)
            pe.wait_ge(S["row_done"], 4)
            mm(b5[:, 0:NB * MB_HEADS], ones, rdg[:, :, :].rearrange("p b h -> p (b h)"),
               start=True, stop=True).then_inc(S["row_mm"], 1)
            pe.wait_ge(S["row_ev"], 1)
            for b in range(NB):
                ins = pe.transpose(blk(b3, b), blk(ra, b), ident)
            ins.then_inc(S["row_mm"], 1)

            def hg_level(l, u, p):
                pe.wait_ge(S["hg_z"], u * 14 + 2 * l)
                pe.wait_ge(S["hg_at"], u * 8 + (l - 1))
                z, bank = zz[l % 2], (b2, b3)[l % 2]
                for b in range(NB):
                    ins = mm(blk(bank, b), blk(z, b), blk(z, b), start=True, stop=True)
                ins.then_inc(S["hg_lv"], 1)

            def hg_part(part, u, p, j0, it):
                U = unit[p]
                if part == 0:
                    if not isinstance(u, int) or u:
                        hg_out(u - 1)
                    filled(pe, j0 + 3, it, 8)
                    wait(pe, S["hg_kt"], u * 1)
                    for b in range(NB):
                        ins = pe.transpose(blk(b4, b), blk(U[:, HG_I, :], b), ident)
                    ins.then_inc(S["hg_tr"], 1)
                    pe.wait_ge(S["hg_k"], u + 1)
                    pe.wait_ge(S["hg_silu"], u * 2 + 1)
                    wait(pe, S["hg_at"], u * 8)
                    for b in range(NB):
                        ins = mm(blk(b2, b), blk(kk, b), blk(U[:, HG_Q, :], b), start=True, stop=True)
                    ins.then_inc(S["hg_lv"], 1)
                    pe.wait_ge(S["hg_x"], u * 2 + 1)
                    pe.wait_ge(S["hg_v"], u + 1)
                    for b in range(3):
                        ins = pe.transpose(blk(b4, b), blk(k1, b), ident)
                    ins.then_inc(S["hg_tr"], 1)
                elif part == 1:
                    if not isinstance(u, int) or u:
                        hg_sum(u - 1)
                    pe.wait_ge(S["hg_kt"], u + 1)
                    wait(pe, S["hg_s"], u * 3)
                    for b in range(3):
                        ins = mm(blk(b5, b), blk(kt_, b), blk(vt, b), start=True, stop=True)
                    ins.then_inc(S["hg_stp"], 1)
                    hg_level(1, u, p)
                    hg_level(2, u, p)
                elif part == 2:
                    for l in (3, 4, 5):
                        hg_level(l, u, p)
                else:
                    hg_level(6, u, p)
                    hg_level(7, u, p)

            def hg_out(u):
                pe.wait_ge(S["hg_at"], u * 8 + 8)
                pe.wait_ge(S["hg_s"], u * 3 + 3)
                pe.wait_ge(S["hg_x"], u * 2 + 2)
                wait(pe, S["hg_y"], u * 2)
                for b in range(NB):
                    ins = mm(blk(b6, b), blk(vt, b), blk(at_, b), start=True, stop=b == 0)
                    if b:
                        ins = mm(blk(b6, b), blk(st_, b - 1), blk(q1, b), start=False, stop=True)
                ins.then_inc(S["hg_o"], 1)

            def hg_sum(u):
                pe.wait_ge(S["hg_sq"], u + 1)
                wait(pe, S["hg_rs"], u * 2)
                mm(b7[:, :], ones, sqh[:, :], start=True, stop=True).then_inc(S["hg_ss"], 1)

            def hg_finish(u):
                hg_out(u)
                hg_sum(u)

            def ml_part(part, u):
                p = u % 2
                U, j = unit[p], ml_slab(u)
                if part == 0:
                    if u == 0:
                        pe.wait_ge(S["hg_lo"], HG_HEADS)
                        pe.wait_ge(S["hg_hi"], HG_HEADS)
                        filled(pe, J_G0 + 15)
                    wait(pe, S["ml_h"], 2 * u)
                    mm(b5[:, :], ident[:, u:u + 1].broadcast_to([P, P]), rnm[:, :], start=True, stop=True
                       ).then_inc(S["ml_nm"], 1)
                    for v in range(2):
                        filled(pe, j + 2 + v)
                        for b in range(NB):
                            ins = pe.transpose(blk((b6, b7)[v], b), blk(U[:, 2 + v, :], b), ident)
                        ins.then_inc(S["ml_tr"], 1)
                elif part == 1:
                    pe.wait_ge(S["ml_silu"], 2 * u + 2)
                    wait(pe, S["ml_em"], u)
                    wait(pe, S["ml_rs"], 2 * u)
                    q, k = U[:, 0, :], U[:, 1, :]
                    for b in range(NB):
                        ins = mm(blk(b2, b), blk(k, b), blk(q, b), start=True, stop=True)
                    ins.then_inc(S["ml_qk"], 1)
                    mm(b3[:, 0:384], blk(k, 0), blk(q, 1, 3), start=True, stop=True)
                    mm(b3[:, 384:512], blk(k, 2), blk(q, 3), start=True, stop=True).then_inc(S["ml_qk"], 1)
                    mm(b4[:, 0:256], blk(k, 1), blk(q, 2, 2), start=True, stop=True).then_inc(S["ml_qk"], 1)
                elif part == 2:
                    pe.wait_ge(S["ml_pt"], 3 * u + 3)
                    pe.wait_ge(S["ml_v"], 2 * u + 2)
                    pe.wait_ge(S["ml_dx"], 4 * u + 4)
                    pe.wait_ge(S["ml_ex"], 4 * u + 4)
                    for bank, w in ((b6, lambda b: m_v[:, b, 0:P]), (b7, lambda b: m_v[:, b, P:2 * P]),
                                    (b5, lambda b: ones)):
                        mm(bank[:, P:T], w(0), m_p[:, 512:896], start=True, stop=False)
                        mm(bank[:, 2 * P:T], w(1), m_p[:, 1024:1280], start=False, stop=False)
                        mm(bank[:, 3 * P:T], w(2), m_p[:, 896:1024], start=False, stop=False)
                        for b in range(NB):
                            ins = mm(blk(bank, b), w(b), m_p[:, b * P:(b + 1) * P], start=False, stop=b == NB - 1)
                        ins.then_inc(S["ml_num"], 1)
                    mm(b2[:, :], nident[:, ROW_F + u:ROW_F + u + 1].broadcast_to([P, P]), cum[:, :],
                       start=True, stop=False)
                    mm(b2[:, :], ident[:, u:u + 1].broadcast_to([P, P]), rnm[:, :], start=False, stop=True
                       ).then_inc(S["ml_nm2"], 1)

            def ml_finish(u):
                for v in range(2):
                    pe.wait_ge(S["ml_sq"], 2 * u + v + 1)
                    ins = mm(b3[:, :], ones, m_sq[:, v, :], start=v == 0, stop=v == 1)
                ins.then_inc(S["ml_ss"], 1)

            def mb_bcast(g, h):
                n = 4 * g + h
                if h == 0:
                    wait(pe, S["mb_rs"], 2 * g)
                if n:
                    pe.wait_ge(S["mb_dx"], 4 * n)
                    pe.wait_ge(S["mb_ex"], 7 * n)
                mm(b5[:, :], ident[:, n:n + 1].broadcast_to([P, P]), cum[:, :], start=True, stop=True
                   ).then_inc(S["mb_nm"], 1)

            def mb_values(g, h):
                n = 4 * g + h
                pe.wait_ge(S["mb_pt"], 3 * n + 3)
                if h == 0:
                    pe.wait_ge(S["mb_xd"], 2 * g + 2)
                pt = s_p[n % 2]
                rows = slice(64 * (h % 2), 64 * (h % 2) + 64)
                bank = (b6, b7)[h // 2]
                mm(bank[rows, P:T], s_x[:, 0, h, :], pt[:, 512:896], start=True, stop=False)
                mm(bank[rows, 2 * P:T], s_x[:, 1, h, :], pt[:, 1024:1280], start=False, stop=False)
                mm(bank[rows, 3 * P:T], s_x[:, 2, h, :], pt[:, 896:1024], start=False, stop=False)
                for b in range(NB):
                    ins = mm(bank[rows, b * P:(b + 1) * P], s_x[:, b, h, :], pt[:, b * P:(b + 1) * P],
                             start=False, stop=b == NB - 1)
                ins.then_inc(S["mb_ym"], 1)

            def mb_start(g):
                U = unit[g % 2]
                if g == 0:
                    pe.wait_ge(S["ml_lo"], 2 * ML_HEADS)
                    pe.wait_ge(S["ml_hi"], 2 * ML_HEADS)
                    pe.wait_ge(S["g_acc"], KT)
                pe.wait_ge(S["mb_silu"], 6 * g + 4)
                wait(pe, S["mb_y"], 6 * g - 3)
                for i in range(2):
                    for b in range(2):
                        for v in range(2):
                            ins = pe.transpose(blk((b6, b7)[i], 2 * b + v), blk(U[:, 2 + v, :], 2 * i + b), ident)
                    ins.then_inc(S["mb_tr"], 1)
                wait(pe, S["mb_pt"], 12 * g)
                bm, cm = U[:, 0, :], U[:, 1, :]
                for b in range(NB):
                    mm(blk(b2, b), blk(bm, b), blk(cm, b), start=True, stop=True)
                mm(b3[:, 0:384], blk(bm, 0), blk(cm, 1, 3), start=True, stop=True)
                mm(b3[:, 384:512], blk(bm, 2), blk(cm, 3), start=True, stop=True)
                mm(b4[:, 0:256], blk(bm, 1), blk(cm, 2, 2), start=True, stop=True).then_inc(S["mb_cb"], 1)
                mb_bcast(g, 0)

            def mb_finish(g):
                pe.wait_ge(S["mb_dx"], 16 * (g + 1))
                pe.wait_ge(S["mb_ex"], 28 * (g + 1))
                for v in range(2):
                    pe.wait_ge(S["mb_sq"], 2 * g + v + 1)
                    ins = mm(b5[:, :], ones, s_sq[:, v, :], start=v == 0, stop=v == 1)
                ins.then_inc(S["mb_ss"], 1)

            def hg_pair(it):
                for p in range(2):
                    for part in range(4):
                        project(J_HG + 4 + 4 * p + part, it, 8)
                        if it is None and p == 0 and part == 0:
                            pe.wait_ge(S["row_done"], 8)
                        hg_part(part, lin(p, it, 2), p, J_HG + 4 * p, it)

            hg_pair(None)
            with pe.Fori(1, HG_HEADS // 2 - 1) as it:
                hg_pair(it)
            for u in (HG_HEADS - 2, HG_HEADS - 1):
                for part in range(4):
                    for i in tiles_before(part, 4 if u == HG_HEADS - 2 else 6):
                        project((J_HG + 4 * (u + 1) if u == HG_HEADS - 2 else J_ML0) + i)
                    hg_part(part, u, u % 2, J_HG + 4 * u, None)

            def gates(j0, lo_sem, n):
                pe.wait_ge(lo_sem, n)
                project(j0 + 1, src=(yh, yl))
                project(j0 + 2)
                project(j0 + 3, src=(yh, yl))
                with pe.Fori(1, KT // 2) as it:
                    for f in range(2):
                        project(j0 + 2 * f, it, 4)
                        project(j0 + 2 * f + 1, it, 4, src=(yh, yl))

            project(J_G0)
            hg_finish(HG_HEADS - 1)
            gates(J_G0, S["hg_lo"], HG_HEADS)
            for u in range(ML_HEADS):
                nxt = ml_slab(u + 1) if u + 1 < ML_HEADS else J_MB0
                for part in range(4):
                    for i in tiles_before(part, 6):
                        project(nxt + i)
                    if part == 0 and u:
                        ml_finish(u - 1)
                    ml_part(part, u)
            project(J_G1)
            ml_finish(ML_HEADS - 1)
            gates(J_G1, S["ml_lo"], 2 * ML_HEADS)
            for g in range(MB_GROUPS):
                nxt = mb_slab(g + 1) if g + 1 < MB_GROUPS else J_G2
                mb_start(g)
                for h in range(4):
                    project(nxt + h)
                    if h < 3:
                        mb_bcast(g, h + 1)
                    mb_values(g, h)
                project(nxt + 4)
                project(nxt + 5)
                mb_finish(g)
            project(J_G2 + 6)
            project(J_G2 + 7)
            pe.wait_ge(S["mb_lo"], 2 * MB_GROUPS)
            with pe.Fori(0, KT // 4) as it:
                for f in range(4):
                    project(J_G2 + KT + f, it, 4, src=(yh, yl))

            for f in range(KT):
                project(J_O + f, ready=(S["o_lo"], 1) if f == 0 else None)
                if f:
                    norm_sum(1, f - 1)
            norm_sum(1, KT - 1)
            project(J_UP, ready=(S["nrm_lo"], KT + 1))
            project(J_UP + 1)
            project(J_UP + 2)
            project(J_UP + 3)
            with pe.Fori(1, NF // 2) as it:
                for j in range(2):
                    project(J_UP + 2 * j, it, 4)
                    project(J_UP + 2 * j + 1, it, 4)
            pe.wait_ge(S["up_lo"], NF)
            for f in range(KT):
                for c, n in enumerate(DN_CHUNKS):
                    project(J_DN + 3 * f + c, src=(fh, fl), n=n, base=8 * c, t0=J_DN + f, first=c == 0, last=c == 2)
                if f:
                    norm_sum(2, f - 1)
            norm_sum(2, KT - 1)
            norm(3)
            for i in range(4):
                project(J_CV + i, t0=J_CV - DN_SHIFT + i, ready=(S["nrm_lo"], 2 * KT + 1) if i == 0 else None)
            with pe.Fori(1, 4) as it:
                for i in range(4):
                    project(J_CV + i, it, 4, t0=J_CV - DN_SHIFT + i)

            def at_scores(i, t):
                n = 8 * t + i
                wait(pe, S["at_l"], n - 1)
                mm((b5, b6)[i % 2][:, :], blk(a_q, i % 4), a_k[i // 4][:, :], start=True, stop=True
                   ).then_inc(S["at_s"], 1)

            def at_values(i, t):
                n = 8 * t + i
                pe.wait_ge(S["at_p"], n + 1)
                wait(pe, S["at_pt"], n - 1)
                if i < 2:
                    pe.wait_ge(S["at_n"], 3 * t + 3)
                bank = (b2, b3)[i % 2]
                for b in range(NB):
                    ins = pe.transpose(blk(bank, b), blk(a_l[i % 4], b), ident)
                ins.then_inc(S["at_tr"], 1)
                pe.wait_ge(S["at_pt"], n + 1)
                if i == 0:
                    wait(pe, S["at_y"], t)
                hd = i // 4
                rows = slice(64 * hd, 64 * hd + 64)
                for b in range(NB):
                    ins = mm(b7[rows, (i % 4) * P:(i % 4 + 1) * P], a_v[:, b, rows], blk(a_pt[i % 2], b),
                             start=b == 0, stop=b == NB - 1)
                ins.then_inc(S["at_o"], 1)

            def at_part(part, t):
                U, j = au[t % 2], J_AT - DN_SHIFT + 4 * t
                if part == 0:
                    for i in range(2):
                        pe.wait_ge(S["at_sq"], 2 * t + i + 1)
                        wait(pe, S["at_tr"], 8 * t)
                        wait(pe, S["at_pt"], 8 * t)
                        mm((b2, b3)[i][:, :], cc(K_BD), a_sq[:, i, :], start=True, stop=True
                           ).then_inc(S["at_ss"], 1)
                    filled(pe, j + 2)
                    wait(pe, S["at_v"], t)
                    for b in range(NB):
                        ins = pe.transpose(blk(b4, b), blk(U[:, 2, :], b), ident)
                    ins.then_inc(S["at_ss"], 1)
                    pe.wait_ge(S["at_n"], 3 * t + 3)
                at_scores(2 * part, t)
                at_scores(2 * part + 1, t)
                if part:
                    if part == 1:
                        pe.wait_ge(S["at_v"], t + 1)
                    at_values(2 * part - 2, t)
                    at_values(2 * part - 1, t)

            for i in range(4):
                project(J_AT + i, t0=J_AT - DN_SHIFT + i)
            for t in range(4):
                for part in range(4):
                    if t < 3:
                        j = J_AT + 4 * (t + 1) + part
                        project(j, t0=j - DN_SHIFT)
                    at_part(part, t)
                at_values(6, t)
                at_values(7, t)
            pe.wait_ge(S["at_lo"], 4)
            pe.wait_ge(S["cv_lo"], 4)
            with pe.Fori(0, KT // 4) as it:
                for f in range(4):
                    project(J_O2 + f, it, 4, src=(yh, yl), t0=J_O2 - DN_SHIFT + f)
            for f in range(KT):
                filled(pe, J_O2 - DN_SHIFT + f)
                wait(pe, S["out_ev"], f - 3)
                for b in range(NB):
                    ins = pe.transpose(blk(psum[2 + f % 4], b), blk(xT[:, f, :], b), ident)
                ins.then_inc(S["out_tr"], 1)

        @block.scalar
        def _(act):
            A = act.activation

            def silu_tables():
                act.preload_act_table_set("silu_and_others")

            def exp_tables():
                act.preload_act_table_set("natural_log_exp_and_others")

            act.dma_start(con[:, :], const_d).then_inc(S["params_in"], 16)
            act.dma_start(par[:, :], par_d).then_inc(S["params_in"], 16)
            act.dma_start(oneh[:, :], onehot_d).then_inc(S["onehot_in"], 16)
            exp_tables()

            def norm_squares(k, j0):
                for f in range(KT):
                    n = 8 * k + f
                    if j0 is not None:
                        filled(act, j0 + f)
                    elif k == 3:
                        act.wait_ge(S["nrm_h"], 16 + f + 1)
                    wait(act, S["nrm_ss"], n - 1)
                    A(sqn[f % 2][:, :], xT[:, f, :], ACT.Square).then_inc(S["nrm_sq"], 1)

            def norm_rms(k):
                act.wait_ge(S["nrm_ss"], 8 * k + 8)
                if k:
                    act.wait_ge(S["nrm_h"], 8 * k)
                A(rsn[:, :], b6[:, :], ACT.Ln, scale=1.0 / D, bias=EPS).then_inc(S["nrm_rs"], 1)
                act.wait_ge(S["nrm_rs"], 2 * k + 1)
                A(rsn[:, :], rsn[:, :], ACT.Exp, scale=-0.5).then_inc(S["nrm_rs"], 1)

            def norm(k, j0):
                norm_squares(k, j0)
                norm_rms(k)

            def norm_hi(k, m):
                for f in range(KT):
                    act.wait_ge(S["nrm_h"], 8 * k + f + 1)
                    A(hh[:, f, :], htn[f % 2][:, :], ACT.Copy).then_inc(S["nrm_hi"], 1)

            for f in range(KT):
                act.wait_ge(S["pro_tr"], f + 1)
                A(xT[:, f, :], psum[2 + f % 4][:, :], ACT.Copy).then_inc(S["pro_xT"], 1)
            act.wait_ge(S["pro_xT"], 8)
            norm(0, None)
            norm_hi(0, 0)
            act.wait_ge(S["lb_step"], 1)
            A(lbt[:, 1, :], lbt[:, 0, :], ACT.Exp).then_inc(S["lb_step"], 1)
            for c, bank in ((0, b7), (1, b5)):
                act.wait_ge(S["wb_mm"], c + 1)
                A(wrow[:, c * T:(c + 1) * T], bank[0:AT_HEADS, :], ACT.Copy).then_inc(S["wb_ev"], 1)
            act.wait_ge(S["wb_ev"], 2)
            act.dma_start(bias_scratch, wrow[:, :].unsqueeze(1).broadcast_to([AT_HEADS, P, W_LINE])
                          ).then_inc(S["wb_out"], 16)
            act.wait_ge(S["row_step"], 2)
            A(r2[:, :], r1[:, :], ACT.Exp).then_inc(S["row_act"], 1)
            A(rac[:, :], pc("alog"), ACT.Exp).then_inc(S["row_act"], 1)

            def copy_out(j0, dst, it=None, k=0, bank=None):
                act.wait_ge(S["slab_used"], lin(j0 + 1, it, k))
                A(dst, acc[j0 % 2][:, :], ACT.Copy).then_inc(acc_free[j0 % 2], 1)

            def hg_exps(l, u):
                n, half = P >> (l - 1), P >> l
                d, e = dd[l % 2], ex[l % 2]
                act.wait_ge(S["hg_d"], u * 8 + (l + 1))
                if l == 1:
                    wait(act, S["hg_z"], u * 14)
                elif l == 2:
                    act.wait_ge(S["hg_x"], u * 2 + 1)
                else:
                    act.wait_ge(S["hg_z"], u * 14 + 2 * (l - 2))
                dv = d[:, :].rearrange("p (c n) -> p c n", n=n)
                ev = e[:, :].rearrange("p (c n) -> p c n", n=n)
                A(ev[:, :, half:], dv[:, :, half:], ACT.Exp).then_inc(S["hg_ex"], 1)
                A(ev[:, :, :half], dv[:, :, :half], ACT.Exp, scale=-1.0).then_inc(S["hg_ex"], 1)

            def hg_prep(u, U, j0, it):
                silu_tables()
                filled(act, j0 + HG_Q, it, 8)
                A(U[:, HG_Q, :], U[:, HG_Q, :], ACT.Silu).then_inc(S["hg_silu"], 1)
                filled(act, j0 + HG_G, it, 8)
                A(U[:, HG_G, :], U[:, HG_G, :], ACT.Silu).then_inc(S["hg_silu"], 1)
                exp_tables()
                filled(act, j0 + HG_F, it, 8)
                wait(act, S["hg_lf"], u)
                wait(act, S["hg_k"], u)
                A(e0[:, :], U[:, HG_F, :], ACT.Exp, scale=-1.0).then_inc(S["hg_e"], 1)
                act.wait_ge(S["hg_e"], u + 1)
                lb = lbc[:, u:u + 1] if isinstance(u, int) else lbc[:, bass.ds(u, 1)]
                A(e1[:, :], e0[:, :], ACT.Ln, scale=lb, bias=1.0).then_inc(S["hg_l"], 1)
                act.wait_ge(S["hg_l"], u * 2 + 1)
                A(e0[:, :], e0[:, :], ACT.Ln, bias=1.0).then_inc(S["hg_l"], 1)
                copy_out(j0 + HG_I, U[:, HG_I, :], it, 8)
                act.wait_ge(S["hg_lf"], u + 1)
                A(e1[:, :], lf[:, :], ACT.Exp).then_inc(S["hg_f"], 1)

            def hg_square(u):
                act.wait_ge(S["hg_o"], u + 1)
                wait(act, S["hg_ss"], u)
                A(sqh[:, :], b6[:, :], ACT.Square).then_inc(S["hg_sq"], 1)

            def hg_rms(u):
                act.wait_ge(S["hg_ss"], u + 1)
                wait(act, S["hg_y"], u * 2)
                A(rsh[:, :], b7[:, :], ACT.Ln, scale=1.0 / P, bias=EPS).then_inc(S["hg_rs"], 1)
                act.wait_ge(S["hg_rs"], u * 2 + 1)
                A(rsh[:, :], rsh[:, :], ACT.Exp, scale=-0.5).then_inc(S["hg_rs"], 1)

            def hg_hi(u):
                act.wait_ge(S["hg_y"], u * 2 + 2)
                A(tile_of(yh, u), yth[:, :], ACT.Copy).then_inc(S["hg_hi"], 1)

            def hg_part(part, u, nxt, it):
                U2, j2 = nxt
                before = not isinstance(u, int) or u > 0
                more = not isinstance(u, int) or u + 1 < HG_HEADS
                if part == 0:
                    if before:
                        hg_square(u - 1)
                    act.wait_ge(S["hg_d"], u * 8 + 1)
                    wait(act, S["hg_z"], u * 14)
                    A(ex[0][:, :], dd[0][:, :], ACT.Exp).then_inc(S["hg_ex"], 1)
                    act.wait_ge(S["hg_b"], u + 1)
                    wait(act, S["hg_s"], u * 3)
                    wait(act, S["hg_x"], u * 2)
                    A(eb[:, :], bb[:, :], ACT.Exp).then_inc(S["hg_eb"], 1)
                    act.wait_ge(S["hg_tr"], u * 2 + 1)
                    wait(act, S["hg_o"], u)
                    A(vt[:, :], b4[:, :], ACT.Copy).then_inc(S["hg_v"], 1)
                    act.wait_ge(S["hg_tr"], u * 2 + 2)
                    A(kt_[:, :], b4[:, 0:3 * P], ACT.Copy).then_inc(S["hg_kt"], 1)
                    hg_exps(1, u)
                elif part == 1:
                    if before:
                        hg_rms(u - 1)
                    hg_exps(2, u)
                    hg_exps(3, u)
                    if more:
                        copy_out(j2 + HG_Q, U2[:, HG_Q, :], it, 8)
                elif part == 2:
                    if before:
                        hg_hi(u - 1)
                    hg_exps(4, u)
                    hg_exps(5, u)
                    hg_exps(6, u)
                    if more:
                        copy_out(j2 + HG_G, U2[:, HG_G, :], it, 8)
                else:
                    hg_exps(7, u)
                    if more:
                        hg_prep(u + 1, U2, j2, it)

            def fill_ml(i, j0, dst):
                if i >= 2:
                    copy_out(j0 + i, dst[:, i, :])

            def fill_mb(i, j0, dst):
                if i >= 4:
                    copy_out(j0 + i, dst[:, i, :])

            def ml_part(part, u):
                p = u % 2
                U, j = unit[p], ml_slab(u)
                if part == 0:
                    silu_tables()
                    for i in range(2):
                        filled(act, j + i)
                        A(U[:, i, :], U[:, i, :], ACT.Silu).then_inc(S["ml_silu"], 1)
                    for i in range(2):
                        filled(act, j + 4 + i)
                        A(U[:, 4 + i, :], U[:, 4 + i, :], ACT.Tanh, scale=0.5).then_inc(S["ml_tanh"], 1)
                    exp_tables()
                    if u:
                        ml_rms(u - 1)
                    else:
                        act.wait_ge(S["hg_lo"], HG_HEADS)
                        act.wait_ge(S["hg_hi"], HG_HEADS)
                        filled(act, J_G0 + 15)
                    act.wait_ge(S["ml_dx"], 4 * u + 4)
                    wait(act, S["ml_pt"], 3 * u)
                    for b in (0, 2, 1):
                        o, n = OFF[b]
                        A(m_e[:, o:o + n], b5[:, (b + 1) * P:T], ACT.Exp, bias=acol[:, b, u:u + 1]
                          ).then_inc(S["ml_ex"], 1)
                    for v in range(2):
                        act.wait_ge(S["ml_tr"], 2 * u + v + 1)
                        wait(act, S["ml_num"], 3 * u)
                        A(m_v[:, :, v * P:(v + 1) * P], (b6, b7)[v][:, :].rearrange("p (b d) -> p b d", b=NB),
                          ACT.Copy).then_inc(S["ml_v"], 1)
                    A(m_e[:, 0:T], m_e[:, 0:T], ACT.Exp).then_inc(S["ml_ex"], 1)
                elif part == 2:
                    act.wait_ge(S["ml_nm2"], u + 1)
                    wait(act, S["ml_dn"], 3 * u)
                    A(m_em[:, :], b2[:, :], ACT.Exp).then_inc(S["ml_em"], 1)
                elif part == 3:
                    for v in range(2):
                        act.wait_ge(S["ml_h"], 2 * u + v + 1)
                        wait(act, S["ml_ss"], u)
                        A(m_sq[:, v, :], m_h[:, v, :], ACT.Square).then_inc(S["ml_sq"], 1)

            def ml_rms(u):
                act.wait_ge(S["ml_ss"], u + 1)
                wait(act, S["ml_y"], 4 * u)
                A(m_rs[:, :], b3[:, :], ACT.Ln, scale=1.0 / 256, bias=EPS).then_inc(S["ml_rs"], 1)
                act.wait_ge(S["ml_rs"], 2 * u + 1)
                A(m_rs[:, :], m_rs[:, :], ACT.Exp, scale=-0.5).then_inc(S["ml_rs"], 1)

            def ml_hi(u):
                for v in range(2):
                    act.wait_ge(S["ml_y"], 4 * u + 2 * v + 2)
                    if u == 0:
                        act.wait_ge(S["slab_used"], J_ML1)
                    A(yh[:, 2 * u + v, :], m_h[:, v, :], ACT.Copy, scale=0.5).then_inc(S["ml_hi"], 1)

            def mb_head(g, h):
                n = 4 * g + h
                act.wait_ge(S["mb_dx"], 4 * n + 4)
                wait(act, S["mb_pt"], 3 * n)
                if n == 0:
                    act.wait_ge(S["ml_lo"], 2 * ML_HEADS)
                    act.wait_ge(S["g_acc"], KT)
                for k, (b, i) in enumerate(((0, 1), (0, 2), (0, 3), (2, 3), (1, 2), (1, 3))):
                    o = OFF[b][0] + (i - b - 1) * P
                    A(s_e[:, o:o + P], blk(b5, i), ACT.Exp, bias=dend[:, k, n:n + 1]).then_inc(S["mb_ex"], 1)
                A(s_e[:, 0:T], s_e[:, 0:T], ACT.Exp).then_inc(S["mb_ex"], 1)

            def mb_silus(g, tiles):
                for i in tiles:
                    filled(act, mb_slab(g) + i)
                    A(unit[g % 2][:, i, :], unit[g % 2][:, i, :], ACT.Silu).then_inc(S["mb_silu"], 1)

            def mb_tail(g):
                for v in range(2):
                    act.wait_ge(S["mb_y"], 6 * g + 2 * v + 2)
                    wait(act, S["mb_ss"], g)
                    A(s_sq[:, v, :], s_y[:, v, :], ACT.Square).then_inc(S["mb_sq"], 1)

            def mb_rms(g):
                act.wait_ge(S["mb_ss"], g + 1)
                wait(act, S["mb_y"], 6 * g)
                A(s_rs[:, :], b5[:, :], ACT.Ln, scale=1.0 / 256, bias=EPS).then_inc(S["mb_rs"], 1)
                act.wait_ge(S["mb_rs"], 2 * g + 1)
                A(s_rs[:, :], s_rs[:, :], ACT.Exp, scale=-0.5).then_inc(S["mb_rs"], 1)

            def mb_hi(g):
                for v in range(2):
                    act.wait_ge(S["mb_y"], 6 * g + 4 + v + 1)
                    if g == 0:
                        act.wait_ge(S["slab_used"], J_MB1)
                    A(yh[:, 2 * g + v, :], s_y[:, v, :], ACT.Copy).then_inc(S["mb_hi"], 1)

            for i in (HG_Q, HG_G):
                copy_out(J_HG + i, unit[0][:, i, :])
            hg_prep(0, unit[0], J_HG, None)
            act.wait_ge(S["row_mm"], 1)
            A(ra[:, :], b4[:, :], ACT.Copy).then_inc(S["row_ev"], 1)
            act.wait_ge(S["wb_out"], 16)

            def hg_pair(it):
                for p in range(2):
                    for part in range(4):
                        hg_part(part, lin(p, it, 2), (unit[1 - p], J_HG + 4 + 4 * p), it)

            hg_pair(None)
            with act.Fori(1, HG_HEADS // 2 - 1) as it:
                hg_pair(it)
            for u in (HG_HEADS - 2, HG_HEADS - 1):
                for part in range(4):
                    hg_part(part, u, (unit[1 - u % 2], J_HG + 4 * (u + 1)), None)
                    if u == HG_HEADS - 1:
                        for i in tiles_before(part, 6):
                            if i == HG_G:
                                act.wait_ge(S["hg_y"], 2 * u)
                            fill_ml(i, J_ML0, unit[0])
            hg_square(HG_HEADS - 1)
            hg_rms(HG_HEADS - 1)
            hg_hi(HG_HEADS - 1)

            def gates(b, j0):
                silu_tables()
                if b == 0:
                    act.wait_ge(S["hg_lo"], HG_HEADS)
                else:
                    act.wait_ge(S["ml_lo"], 2 * ML_HEADS)
                with act.Fori(0, KT // 2) as it:
                    for f in range(2):
                        act.wait_ge(S["slab_used"], it * 4 + (j0 + 2 * f + 1))
                        filled(act, j0 + 2 * f - 3, it, 4)
                        A(tg[f][:, :], acc[j0 % 2][:, :], ACT.Tanh, scale=0.5).then_inc(acc_free[j0 % 2], 1)

            gates(0, J_G0)
            for u in range(ML_HEADS):
                last = u + 1 == ML_HEADS
                for part in range(4):
                    ml_part(part, u)
                    if part == 0 and u:
                        ml_hi(u - 1)
                    for i in tiles_before(part, 6):
                        if i == 4:
                            wait(act, S["ml_lo"], 2 * u)
                        if last:
                            fill_mb(i, J_MB0, unit[0])
                        else:
                            fill_ml(i, ml_slab(u + 1), unit[1 - u % 2])
            ml_rms(ML_HEADS - 1)
            ml_hi(ML_HEADS - 1)
            gates(1, J_G1)
            silu_tables()
            mb_silus(0, range(6))
            exp_tables()
            for g in range(MB_GROUPS):
                last = g + 1 == MB_GROUPS
                nxt = J_G2 if last else mb_slab(g + 1)
                for h in range(4):
                    mb_head(g, h)
                    if last:
                        copy_out(nxt + h, gbuf[:, h, :])
                if not last:
                    silu_tables()
                    mb_silus(g + 1, range(4))
                for i in (4, 5):
                    wait(act, S["mb_y"], 6 * g - 2)
                    copy_out(nxt + i, gbuf[:, i, :] if last else unit[1 - g % 2][:, i, :])
                mb_tail(g)
                if not last:
                    mb_silus(g + 1, (4, 5))
                    exp_tables()
                mb_rms(g)
                if last:
                    for i in (6, 7):
                        copy_out(nxt + i, gbuf[:, i, :])
                mb_hi(g)
            silu_tables()
            for f in range(KT):
                filled(act, J_G2 + f)
                A(gbuf[:, f, :], gbuf[:, f, :], ACT.Tanh, scale=0.5).then_inc(S["g_tanh"], 1)
            for f in range(KT):
                act.wait_ge(S["g_acc"], KT + f + 1)
                A(hh[:, f, :], mixed[:, f, :], ACT.Copy, scale=0.5).then_inc(S["o_hi"], 1)

            exp_tables()
            norm(1, J_O)
            norm_hi(1, 1)
            silu_tables()
            with act.Fori(0, NF // 2) as it:
                for p in range(2):
                    j = it * 2 + p
                    act.wait_ge(S["slab_used"], it * 4 + (J_UP + 2 * p + 1))
                    A(f_g[p][:, :], acc[J_UP % 2][:, :], ACT.Identity, scale=pc("fcw", it * 6 + (3 * p + 2)),
                      bias=pc("fcb", j)).then_inc(S["up_c"], 1)
                    act.wait_ge(S["slab_used"], it * 4 + (J_UP + 2 * p + 2))
                    A(f_v[p][:, :], acc[1 - J_UP % 2][:, :], ACT.Identity,
                      scale=pc("fcw", it * 6 + (3 * NF + 3 * p + 2)), bias=pc("fcb", j + NF)
                      ).then_inc(S["up_c"], 1)
                    filled(act, J_UP + 2 * p, it, 4)
                    A(f_s[p][:, :], f_g[p][:, :], ACT.Silu).then_inc(S["up_sg"], 1)
                    act.wait_ge(S["up_a"], j + 1)
                    A(tile_of(fh, j), f_s[p][:, :], ACT.Copy).then_inc(S["up_hi"], 1)
            exp_tables()
            norm_squares(2, J_DN)
            skew = bass.AP(tensor=bias_scratch.tensor, offset=P - 1,
                           ap=[[W_LINE - 1, P], [P * W_LINE, AT_HEADS], [1, W_BIAS]])
            act.dma_start(wb[:, :, :], skew).then_inc(S["wb_in"], 16)
            norm_rms(2)
            norm(3, None)
            norm_hi(3, 2)
            silu_tables()
            def conv_tile(it):
                j = J_CV
                t0 = J_CV - DN_SHIFT
                wait(act, S["cv_y"], it * 5)
                for i, dst in ((0, c_u), (1, c_b)):
                    act.wait_ge(S["slab_used"], it * 4 + (j + i + 1))
                    A(dst[:, :], acc[(t0 + i) % 2][:, :], ACT.Copy).then_inc(acc_free[(t0 + i) % 2], 1)
                act.wait_ge(S["slab_used"], it * 4 + (j + 4))
                A(c_z[:, :], acc[(t0 + 3) % 2][:, :], ACT.Silu).then_inc(acc_free[(t0 + 3) % 2], 1)
                act.wait_ge(S["cv_y"], it * 5 + 5)
                A(tile_of(yh, it), c_y[:, :], ACT.Copy).then_inc(S["cv_hi"], 1)

            conv_tile(0)
            with act.Fori(1, 4) as it:
                conv_tile(it)

            def fill_at(i, t):
                j = J_AT + 4 * t + i
                act.wait_ge(S["slab_used"], j + 1)
                A(au[t % 2][:, i, :], acc[(j - DN_SHIFT) % 2][:, :], ACT.Copy
                  ).then_inc(acc_free[(j - DN_SHIFT) % 2], 1)

            for i in range(4):
                fill_at(i, 0)

            def at_part(part, t):
                U, j = au[t % 2], J_AT - DN_SHIFT + 4 * t
                if part == 0:
                    silu_tables()
                    filled(act, j + 3)
                    A(U[:, 3, :], U[:, 3, :], ACT.Silu).then_inc(S["at_silu"], 1)
                    exp_tables()
                    for i in range(2):
                        wait(act, S["at_ss"], 3 * t)
                        A(a_sq[:, i, :], U[:, i, :], ACT.Square).then_inc(S["at_sq"], 1)
                    for i in range(2):
                        act.wait_ge(S["at_ss"], 3 * t + i + 1)
                        wait(act, S["at_n"], 3 * t)
                        A(a_rs[:, i, :], (b2, b3)[i][:, :], ACT.Ln, scale=1.0 / AT_DH, bias=EPS
                          ).then_inc(S["at_rs"], 1)
                        act.wait_ge(S["at_rs"], 4 * t + 2 * i + 1)
                        A(a_rs[:, i, :], a_rs[:, i, :], ACT.Exp, scale=-0.5).then_inc(S["at_rs"], 1)
                    act.wait_ge(S["at_ss"], 3 * t + 3)
                    wait(act, S["at_o"], 8 * t)
                    A(a_v[:, :, :].rearrange("p b d -> p (b d)"), b4[:, :], ACT.Copy).then_inc(S["at_v"], 1)
                for i in (2 * part, 2 * part + 1):
                    n = 8 * t + i
                    act.wait_ge(S["at_mx"], n + 1)
                    A(a_l[i % 4][:, :], a_l[i % 4][:, :], ACT.Exp, bias=a_st[:, i, 0:1],
                      accum_out=a_st[:, i, 1:2]).then_inc(S["at_ex"], 1)
                if part:
                    at_copy(2 * part - 2, t)
                    at_copy(2 * part - 1, t)

            def at_copy(i, t):
                n = 8 * t + i
                act.wait_ge(S["at_tr"], n + 1)
                wait(act, S["at_o"], n - 1)
                A(a_pt[i % 2][:, :], (b2, b3)[i % 2][:, :], ACT.Copy).then_inc(S["at_pt"], 1)

            for t in range(4):
                for part in range(4):
                    at_part(part, t)
                    if t < 3:
                        if part == 0:
                            wait(act, S["at_lo"], t)
                        fill_at(part, t + 1)
                at_copy(6, t)
                at_copy(7, t)
                act.wait_ge(S["at_y"], t + 1)
                A(yh[:, 4 + t, :], a_y[:, :], ACT.Copy).then_inc(S["at_hi"], 1)
            for f in range(KT):
                act.wait_ge(S["out_tr"], f + 1)
                if f >= 2:
                    act.wait_ge(S[f"out_dma{f % 2}"], 16 * (f // 2))
                A(os_[f % 2][:, :], psum[2 + f % 4][:, :], ACT.Copy).then_inc(S["out_ev"], 1)

        @block.vector
        def _(dve):
            TT, TS, STT = dve.tensor_tensor, dve.tensor_scalar, dve.scalar_tensor_tensor

            def norm_scale(k, m, gain, keep=False):
                dve.wait_ge(S["nrm_rs"], 2 * k + 2)
                for f in range(KT):
                    if keep:
                        STT(xT[:, f, :], xT[:, f, :], pc(gain, f), rsn[:, :], ALU.mult, ALU.mult
                            ).then_inc(S["nrm_h"], 1)
                        continue
                    if f >= 2:
                        dve.wait_ge(S["nrm_hi"], 8 * m + f - 1)
                        dve.wait_ge(S["nrm_lo"], 8 * m + f - 1)
                    STT(htn[f % 2][:, :], xT[:, f, :], pc(gain, f), rsn[:, :], ALU.mult, ALU.mult
                        ).then_inc(S["nrm_h"], 1)
                    if f:
                        lo(k, m, f - 1)
                if not keep:
                    lo(k, m, KT - 1)

            def lo(k, m, f):
                dve.wait_ge(S["nrm_h"], 8 * k + f + 1)
                dve.wait_ge(S["nrm_hi"], 8 * m + f + 1)
                TT(hl[:, f, :], htn[f % 2][:, :], hh[:, f, :].bitcast(F32), ALU.subtract).then_inc(S["nrm_lo"], 1)

            dve.wait_ge(S["zero_set"], 1)
            dve.wait_ge(S["params_in"], 32)
            lg = par[:, PAR["lb"]:PAR["lb"] + 8]
            TT(lbt[:, 0, :], lg, lg, ALU.subtract).then_inc(S["lb_step"], 1)
            norm_scale(0, 0, "norm1")
            dve.wait_ge(S["lb_step"], 2)
            dve.reciprocal(lbt[:, 2, :], lbt[:, 1, :]).then_inc(S["lb_step"], 1)
            dve.wait_ge(S["lb_step"], 3)
            TT(lbt[:, 0, :], lbt[:, 1, :], lbt[:, 2, :], ALU.mult).then_inc(S["lb_step"], 1)
            dve.wait_ge(S["lb_step"], 4)
            TT(lbc[:, :], lbt[:, 0, :], lbt[:, 0, :], ALU.subtract).then_inc(S["lb_step"], 1)

            step = [0]

            def row(ins):
                step[0] += 1
                ins.then_inc(S["row_step"], 1)
                dve.wait_ge(S["row_step"], step[0])

            def clamp_f(j0, dst, it=None):
                dve.wait_ge(S["slab_used"], lin(j0 + 1, it, 8))
                TS(dst, acc[j0 % 2][:, :], -40.0, None, ALU.max).then_inc(acc_free[j0 % 2], 1)

            def hg_prep(u):
                dve.wait_ge(S["hg_l"], u * 2 + 2)
                wait(dve, S["hg_f"], u)
                wait(dve, S["hg_b"], u)
                TT(lf[:, :], e1[:, :], e0[:, :], ALU.subtract).then_inc(S["hg_lf"], 1)
                dve.wait_ge(S["hg_lf"], u + 1)
                wait(dve, S["hg_eb"], u)
                wait(dve, S["hg_d"], u * 8)
                dve.tensor_tensor_scan(bb[:, :], cc(K_HGMASK, T), lf[:, :], 0.0, ALU.mult, ALU.add
                                       ).then_inc(S["hg_b"], 1)
                dve.wait_ge(S["hg_f"], u + 1)
                wait(dve, S["hg_lv"], u * 8)
                wait(dve, S["hg_z"], u * 14)
                TS(kk[:, :], e1[:, :], -1.0, 1.0, ALU.mult, ALU.add).then_inc(S["hg_k"], 1)

            sign = cc(K_SIGN, 1)
            dve.wait_ge(S["slab_used"], 1)
            STT(rz[:, :], acc[0][:, :], pc("rowb"), sign.broadcast_to([P, T]), ALU.add, ALU.mult
                ).then_inc(acc_free[0], 1)
            dve.wait_ge(acc_free[0], 1)
            row(TS(r3[:, :], rz[:, :], 0.0, None, ALU.max))
            row(STT(r1[:, :], rz[:, :], -1.0, rz[:, :], ALU.mult, ALU.min))
            dve.wait_ge(S["row_act"], 2)
            row(TS(r4[:, :], r2[:, :], 2.0, None, ALU.add))
            row(dve.reciprocal(r5[:, :], r4[:, :]))
            clamp_f(J_HG + HG_F, unit[0][:, HG_F, :])
            row(TT(r4[:, :], r2[:, :], r5[:, :], ALU.mult))
            row(TT(r2[:, :], r4[:, :], r4[:, :], ALU.mult))
            row(TS(r1[:, :], r2[:, :], 1.0 / 17, None, ALU.mult))
            for k in (15, 13, 11, 9, 7, 5, 3):
                row(STT(r1[:, :], r1[:, :], 1.0 / k, r2[:, :], ALU.add, ALU.mult))
            row(STT(r1[:, :], r1[:, :], 1.0, r4[:, :], ALU.add, ALU.mult))
            row(STT(r5[:, :], r1[:, :], 2.0, r3[:, :], ALU.mult, ALU.add))
            row(TS(rac[:, :], rac[:, :], -1.0, None, ALU.mult))
            row(TS(r4[:, :], r5[:, :], rac[:, 0:1], None, ALU.mult))
            dve.tensor_tensor_scan(cum[:, :], cc(K_RMASK, T), r4[:, :], 0.0, ALU.mult, ALU.add
                                   ).then_inc(S["row_a"], 1)
            dve.wait_ge(S["row_a"], 1)
            for b in range(NB):
                TS(rdg[:, b, :], ident[:, 0:MB_HEADS], cum[:, b * P + P - 1:b * P + P], None, ALU.mult
                   ).then_inc(S["row_done"], 1)
            hg_prep(0)
            dve.wait_ge(S["row_ev"], 1)
            dve.tensor_tensor_scan(rnm[:, :], ra[:, :], ra[:, :], 0.0, ALU.max, ALU.max).then_inc(S["rnm_done"], 1)
            dve.wait_ge(S["rnm_done"], 1)
            TS(rnm[:, :], rnm[:, :], -1.0, None, ALU.mult).then_inc(S["rnm_done"], 1)
            def cols(bank, n):
                return bank[:, :].rearrange("p (b r) -> p b r", b=NB)[:, :, 0:n]

            dve.wait_ge(S["row_mm"], 2)
            TS(ncc[:, :, :], cols(b6, MB_HEADS), -1.0, None, ALU.mult).then_inc(S["row_done"], 1)
            dve.tensor_copy(dtc[:, :, :], cols(b7, MB_HEADS)).then_inc(S["row_done"], 1)
            dve.wait_ge(S["row_mm"], 3)
            dve.tensor_copy(totb[:, :, :], b5[:, 0:NB * MB_HEADS].rearrange("p (b h) -> p b h", b=NB)
                            ).then_inc(S["row_done"], 1)
            dve.wait_ge(S["row_mm"], 4)
            dve.tensor_copy(acol[:, :, :], cols(b3, ML_HEADS)).then_inc(S["row_done"], 1)
            dve.wait_ge(S["row_done"], 8)
            TT(dend[:, 0, :], totb[:, 0, :], ncc[:, 0, :], ALU.add).then_inc(S["row_step"], 1)
            TT(dend[:, 3, :], totb[:, 2, :], ncc[:, 2, :], ALU.add).then_inc(S["row_step"], 1)
            TT(dend[:, 4, :], totb[:, 1, :], ncc[:, 1, :], ALU.add).then_inc(S["row_step"], 1)
            dve.wait_ge(S["row_step"], step[0] + 3)
            TT(dend[:, 1, :], dend[:, 0, :], totb[:, 1, :], ALU.add).then_inc(S["row_done"], 1)
            TT(dend[:, 5, :], dend[:, 4, :], totb[:, 2, :], ALU.add).then_inc(S["row_done"], 1)
            dve.wait_ge(S["row_done"], 10)
            TT(dend[:, 2, :], dend[:, 1, :], totb[:, 2, :], ALU.add).then_inc(S["row_done"], 1)
            dve.wait_ge(S["row_done"], 11)

            convs = [0]

            def conv4(j0, dst, w, b, i):
                bank = acc[j0 % 2]
                dve.wait_ge(S["slab_used"], j0 + 1)
                TS(dst, bank[:, :], pc(w, 4 * i + 3), pc(b, i), ALU.mult, ALU.add).then_inc(S["conv_step"], 1)
                for k in (2, 1, 0):
                    convs[0] += 1
                    dve.wait_ge(S["conv_step"], convs[0])
                    s = 3 - k
                    ins = STT(dst[:, s:], bank[:, 0:T - s], pc(w, 4 * i + k), dst[:, s:], ALU.mult, ALU.add)
                    ins.then_inc(S["conv_step"] if k else acc_free[j0 % 2], 1)

            def hg_diff(l, u):
                dve.wait_ge(S["hg_b"], u + 1)
                if l == 0:
                    wait(dve, S["hg_ex"], u * 15)
                    v = bb[:, :].rearrange("p (c n) -> p c n", n=P)
                    o = dd[0][:, :].rearrange("p (c n) -> p c n", n=P)
                    TT(o, v[:, :, P - 1:P].broadcast_to([P, NB, P]), v, ALU.subtract).then_inc(S["hg_d"], 1)
                    return
                n, half = P >> (l - 1), P >> l
                wait(dve, S["hg_ex"], u * 15 if l == 1 else u * 15 + (1 + 2 * (l - 2)))
                v = bb[:, :].rearrange("p (c n) -> p c n", n=n)
                o = dd[l % 2][:, :].rearrange("p (c n) -> p c n", n=n)
                TT(o, v, v[:, :, half - 1:half].broadcast_to([P, T // n, n]), ALU.subtract).then_inc(S["hg_d"], 1)

            def hg_scale(l, u, p):
                n, half = P >> (l - 1), P >> l
                dve.wait_ge(S["hg_ex"], u * 15 + (1 + 2 * l))
                wait(dve, S["hg_lv"], u * 8 + (l - 1))
                def v(ap):
                    return ap.rearrange("p (c n) -> p c n", n=n)
                q, k, e, z = v(unit[p][:, HG_Q, :]), v(kk[:, :]), v(ex[l % 2][:, :]), v(zz[l % 2][:, :])
                TT(z[:, :, half:], q[:, :, half:], e[:, :, half:], ALU.mult).then_inc(S["hg_z"], 1)
                TT(z[:, :, :half], k[:, :, :half], e[:, :, :half], ALU.mult).then_inc(S["hg_z"], 1)

            def hg_merge(l, u):
                dve.wait_ge(S["hg_lv"], u * 8 + (l + 1))
                dve.wait_ge(S["hg_at"], u * 8 + l)
                dve.tensor_copy(tick[:, :], zero[:, :])
                mask = cc(K_LMASK + (l - 1) * P).bitcast(U32).unsqueeze(1).broadcast_to([P, NB, P])
                dve.copy_predicated(at_[:, :].rearrange("p (b t) -> p b t", b=NB), mask,
                                    (b2, b3)[l % 2][:, :].rearrange("p (b t) -> p b t", b=NB)
                                    ).then_inc(S["hg_at"], 1)

            def hg_y(u, U):
                dve.wait_ge(S["hg_rs"], u * 2 + 2)
                wait(dve, S["hg_hi"], u)
                wait(dve, S["hg_lo"], u)
                STT(yth[:, :], b6[:, :], pc("hgg"), rsh[:, :], ALU.mult, ALU.mult).then_inc(S["hg_y"], 1)
                dve.wait_ge(S["hg_y"], u * 2 + 1)
                dve.wait_ge(S["hg_silu"], u * 2 + 2)
                TT(yth[:, :], yth[:, :], U[:, HG_G, :], ALU.mult).then_inc(S["hg_y"], 1)

            def hg_lo(u):
                dve.wait_ge(S["hg_hi"], u + 1)
                dve.wait_ge(S["hg_y"], u * 2 + 2)
                TT(tile_of(yl, u), yth[:, :], tile_of(yh, u).bitcast(F32), ALU.subtract).then_inc(S["hg_lo"], 1)

            def hg_part(part, u, p, it):
                U = unit[p]
                before = not isinstance(u, int) or u > 0
                more = not isinstance(u, int) or u + 1 < HG_HEADS
                if part == 0:
                    hg_diff(0, u)
                    hg_diff(1, u)
                    dve.wait_ge(S["hg_k"], u + 1)
                    dve.wait_ge(S["hg_ex"], u * 15 + 1)
                    wait(dve, S["hg_tr"], u * 2)
                    TT(k1[:, :], kk[:, :], ex[0][:, :], ALU.mult).then_inc(S["hg_x"], 1)
                    dve.wait_ge(S["hg_eb"], u + 1)
                    dve.wait_ge(S["hg_silu"], u * 2 + 1)
                    wait(dve, S["hg_o"], u)
                    TT(q1[:, :], U[:, HG_Q, :], eb[:, :], ALU.mult).then_inc(S["hg_x"], 1)
                    dve.wait_ge(S["hg_lv"], u * 8 + 1)
                    TT(at_[:, :].rearrange("p (b t) -> p b t", b=NB), b2[:, :].rearrange("p (b t) -> p b t", b=NB),
                       ident.unsqueeze(1).broadcast_to([P, NB, P]), ALU.mult).then_inc(S["hg_at"], 1)
                    hg_scale(1, u, p)
                    if more:
                        clamp_f(J_HG + 4 * ((u if it is None else p) + 1) + HG_F, unit[1 - p][:, HG_F, :], it)
                elif part == 1:
                    hg_diff(2, u)
                    hg_scale(2, u, p)
                    hg_diff(3, u)
                    hg_merge(1, u)
                    hg_scale(3, u, p)
                    dve.wait_ge(S["hg_stp"], u + 1)
                    wait(dve, S["hg_o"], u)
                    dve.tensor_copy(blk(st_, 0), blk(b5, 0)).then_inc(S["hg_s"], 1)
                    for b in (1, 2):
                        dve.wait_ge(S["hg_s"], u * 3 + b)
                        STT(blk(st_, b), blk(st_, b - 1), eb[:, b * P + P - 1:b * P + P], blk(b5, b),
                            ALU.mult, ALU.add).then_inc(S["hg_s"], 1)
                    hg_merge(2, u)
                    if before:
                        hg_y(u - 1, unit[1 - p])
                elif part == 2:
                    hg_diff(4, u)
                    hg_scale(4, u, p)
                    hg_diff(5, u)
                    hg_merge(3, u)
                    hg_scale(5, u, p)
                    if before:
                        hg_lo(u - 1)
                    hg_diff(6, u)
                    hg_merge(4, u)
                    hg_scale(6, u, p)
                    hg_merge(5, u)
                else:
                    hg_diff(7, u)
                    hg_scale(7, u, p)
                    hg_merge(6, u)
                    hg_merge(7, u)
                    if more:
                        hg_prep(u + 1)

            def hg_pair(it):
                for p in range(2):
                    for part in range(4):
                        hg_part(part, lin(p, it, 2), p, it)

            hg_pair(None)
            with dve.Fori(1, HG_HEADS // 2 - 1) as it:
                hg_pair(it)
            for u in (HG_HEADS - 2, HG_HEADS - 1):
                for part in range(4):
                    hg_part(part, u, u % 2, None)
                    if u == HG_HEADS - 1:
                        for i in tiles_before(part, 6):
                            if i < 2:
                                conv4(J_ML0 + i, unit[0][:, i, :], "mlcw", "mlcb", 4 * i)
            hg_y(HG_HEADS - 1, unit[(HG_HEADS - 1) % 2])
            hg_lo(HG_HEADS - 1)

            def gates(b, j0):
                with dve.Fori(0, KT // 2) as it:
                    for f in range(2):
                        dve.wait_ge(S["slab_used"], it * 4 + (j0 + 2 * f + 2))
                        filled(dve, j0 + 2 * f, it, 4)
                        fo = it * 2 + f
                        dst = tile_of(mixed, fo) if b == 0 else tm[:, :]
                        if b:
                            wait(dve, S["g_acc"], it * 2 + (KT * (b - 1) + f))
                        STT(dst, tg[f][:, :], 1.0, acc[1 - j0 % 2][:, :], ALU.add, ALU.mult
                            ).then_inc(acc_free[1 - j0 % 2], 1)
                        if b:
                            filled(dve, j0 + 2 * f + 1, it, 4)
                            TT(tile_of(mixed, fo), tile_of(mixed, fo), tm[:, :], ALU.add).then_inc(S["g_acc"], 1)

            def ml_part(part, u):
                p = u % 2
                U = unit[p]
                if part == 0:
                    dve.wait_ge(S["ml_nm"], u + 1)
                    wait(dve, S["ml_pt"], 3 * u)
                    for b in range(NB):
                        STT(m_e[:, b * P:(b + 1) * P], blk(b5, b), acol[:, b, u:u + 1], clampm, ALU.add, ALU.min
                            ).then_inc(S["ml_dx"], 1)
                elif part == 1:
                    dve.wait_ge(S["ml_ex"], 4 * u + 4)
                    wait(dve, S["ml_num"], 3 * u)
                    for i, (bank, a, n) in enumerate(((b2, 0, 512), (b3, 512, 512), (b4, 1024, 256))):
                        dve.wait_ge(S["ml_qk"], 3 * u + i + 1)
                        STT(m_p[:, a:a + n], bank[:, 0:n], P ** -0.5, m_e[:, a:a + n], ALU.mult, ALU.mult
                            ).then_inc(S["ml_pt"], 1)
                elif part == 2:
                    dve.wait_ge(S["ml_num"], 3 * u + 3)
                    dve.wait_ge(S["ml_em"], u + 1)
                    wait(dve, S["ml_dn"], 3 * u)
                    STT(m_dn[:, :], b5[:, :], -1.0, m_em[:, :], ALU.mult, ALU.max).then_inc(S["ml_dn"], 1)
                    dve.wait_ge(S["ml_dn"], 3 * u + 1)
                    TT(m_dn[:, :], m_dn[:, :], b5[:, :], ALU.max).then_inc(S["ml_dn"], 1)
                    dve.wait_ge(S["ml_dn"], 3 * u + 2)
                    wait(dve, S["ml_h"], 2 * u)
                    dve.reciprocal(m_rd[:, :], m_dn[:, :]).then_inc(S["ml_dn"], 1)
                    dve.wait_ge(S["ml_dn"], 3 * u + 3)
                    wait(dve, S["ml_hi"], 2 * u)
                    wait(dve, S["ml_lo"], 2 * u)
                    for v in range(2):
                        TT(m_h[:, v, :], (b6, b7)[v][:, :], m_rd[:, :], ALU.mult).then_inc(S["ml_h"], 1)

            def ml_end(u):
                U = unit[u % 2]
                dve.wait_ge(S["ml_rs"], 2 * u + 2)
                dve.wait_ge(S["ml_sq"], 2 * u + 2)
                dve.wait_ge(S["ml_tanh"], 2 * u + 2)
                for v in range(2):
                    STT(m_h[:, v, :], m_h[:, v, :], pc("mlg", v), m_rs[:, :], ALU.mult, ALU.mult
                        ).then_inc(S["ml_y"], 1)
                    dve.wait_ge(S["ml_y"], 4 * u + 2 * v + 1)
                    STT(m_h[:, v, :], U[:, 4 + v, :], 1.0, m_h[:, v, :], ALU.add, ALU.mult
                        ).then_inc(S["ml_y"], 1)
                for v in range(2):
                    dve.wait_ge(S["ml_hi"], 2 * u + v + 1)
                    dve.wait_ge(S["ml_y"], 4 * u + 4)
                    STT(yl[:, 2 * u + v, :], m_h[:, v, :], 0.5, yh[:, 2 * u + v, :].bitcast(F32),
                        ALU.mult, ALU.subtract).then_inc(S["ml_lo"], 1)

            def mb_head(g, h):
                n = 4 * g + h
                dve.wait_ge(S["mb_nm"], n + 1)
                wait(dve, S["mb_pt"], 3 * n)
                for b in range(NB):
                    STT(s_e[:, b * P:(b + 1) * P], blk(b5, b), ncc[:, b, n:n + 1], clampm, ALU.add, ALU.min
                        ).then_inc(S["mb_dx"], 1)
                dve.wait_ge(S["mb_ex"], 7 * n + 7)
                wait(dve, S["mb_ym"], n - 1)
                if h == 0:
                    dve.wait_ge(S["mb_cb"], g + 1)
                for bank, a, m in ((b2, 0, 512), (b3, 512, 512), (b4, 1024, 256)):
                    TT(s_p[n % 2][:, a:a + m], s_e[:, a:a + m], bank[:, 0:m], ALU.mult).then_inc(S["mb_pt"], 1)

            def mb_xdt(g):
                wait(dve, S["mb_ym"], 4 * g)
                for i in range(2):
                    dve.wait_ge(S["mb_tr"], 2 * g + i + 1)
                    TT(s_x[:, 2 * i:2 * i + 2], (b6, b7)[i][:, :].rearrange("p (b h d) -> p b h d", b=2, h=4),
                       dtc[:, 2 * i:2 * i + 2, 4 * g:4 * g + 4].unsqueeze(3).broadcast_to([P, 2, 4, 64]), ALU.mult
                       ).then_inc(S["mb_xd"], 1)

            def mb_y(g):
                U = unit[g % 2]
                wait(dve, S["mb_hi"], 2 * g)
                wait(dve, S["mb_lo"], 2 * g)
                dve.wait_ge(S["mb_ym"], 4 * g + 4)
                dve.wait_ge(S["mb_silu"], 6 * g + 6)
                for v in range(2):
                    STT(s_y[:, v, :], U[:, 2 + v, :], pc("mbd", 2 * g + v), (b6, b7)[v][:, :],
                        ALU.mult, ALU.add).then_inc(S["mb_y"], 1)
                    dve.wait_ge(S["mb_y"], 6 * g + 2 * v + 1)
                    TT(s_y[:, v, :], s_y[:, v, :], U[:, 4 + v, :], ALU.mult).then_inc(S["mb_y"], 1)

            def mb_norm(g):
                dve.wait_ge(S["mb_rs"], 2 * g + 2)
                dve.wait_ge(S["mb_sq"], 2 * g + 2)
                for v in range(2):
                    STT(s_y[:, v, :], s_y[:, v, :], pc("mbg", 2 * g + v), s_rs[:, :], ALU.mult, ALU.mult
                        ).then_inc(S["mb_y"], 1)

            def mb_lo(g):
                for v in range(2):
                    dve.wait_ge(S["mb_hi"], 2 * g + v + 1)
                    dve.wait_ge(S["mb_y"], 6 * g + 4 + v + 1)
                    TT(yl[:, 2 * g + v, :], s_y[:, v, :], yh[:, 2 * g + v, :].bitcast(F32), ALU.subtract
                       ).then_inc(S["mb_lo"], 1)

            gates(0, J_G0)
            for u in range(ML_HEADS):
                last = u + 1 == ML_HEADS
                for part in range(4):
                    ml_part(part, u)
                    for i in tiles_before(part, 6):
                        if last and i < 4:
                            conv4(J_MB0 + i, unit[0][:, i, :], "mbcw", "mbcb", (8, 12, 0, 1)[i])
                        elif not last and i < 2:
                            conv4(ml_slab(u + 1) + i, unit[1 - u % 2][:, i, :], "mlcw", "mlcb", 4 * i + u + 1)
                    if part == 0 and u:
                        ml_end(u - 1)
            ml_end(ML_HEADS - 1)
            gates(1, J_G1)
            for g in range(MB_GROUPS):
                mb_xdt(g)
                for h in range(4):
                    mb_head(g, h)
                    if h == 0 and g:
                        mb_lo(g - 1)
                    if g + 1 < MB_GROUPS:
                        conv4(mb_slab(g + 1) + h, unit[1 - g % 2][:, h, :], "mbcw", "mbcb",
                              (8 + g + 1, 12 + g + 1, 2 * g + 2, 2 * g + 3)[h])
                mb_y(g)
                mb_norm(g)
            mb_lo(MB_GROUPS - 1)
            with dve.Fori(0, KT // 4) as it:
                for f in range(4):
                    t = J_G2 + KT + f
                    fo = it * 4 + f
                    dve.wait_ge(S["slab_used"], it * 4 + (t + 1))
                    dve.wait_ge(S["g_tanh"], it * 4 + (f + 1))
                    dve.wait_ge(S["g_acc"], it * 4 + (f + KT))
                    STT(tm[:, :], tile_of(gbuf, fo), 1.0, acc[t % 2][:, :], ALU.add, ALU.mult
                        ).then_inc(acc_free[t % 2], 1)
                    filled(dve, t, it, 4)
                    TT(tile_of(mixed, fo), tile_of(mixed, fo), tm[:, :], ALU.add).then_inc(S["g_acc"], 1)
                    dve.wait_ge(S["o_hi"], it * 4 + (f + 1))
                    STT(tile_of(hl, fo), tile_of(mixed, fo), 0.5, tile_of(hh, fo).bitcast(F32),
                        ALU.mult, ALU.subtract).then_inc(S["o_lo"], 1)

            def add_residual(j0, used, it, per):
                for f in range(4):
                    t = j0 + f
                    dve.wait_ge(S["slab_used"], it * per + used(f))
                    fo = it * 4 + f
                    TT(tile_of(xT, fo), tile_of(xT, fo), acc[t % 2][:, :], ALU.add).then_inc(acc_free[t % 2], 1)

            with dve.Fori(0, KT // 4) as it:
                add_residual(J_O, lambda f: J_O + f + 1, it, 4)
            norm_scale(1, 1, "norm2")
            with dve.Fori(0, NF // 2) as it:
                for p in range(2):
                    j = it * 2 + p
                    for v, buf in ((0, f_g), (1, f_v)):
                        bank = acc[(J_UP + v) % 2]
                        w0 = it * 6 + (3 * NF * v + 3 * p)
                        d = buf[p]
                        dve.wait_ge(S["up_c"], it * 4 + (2 * p + v + 1))
                        STT(d[:, 1:], bank[:, 0:T - 1], pc("fcw", w0 + 1), d[:, 1:], ALU.mult, ALU.add
                            ).then_inc(S["up_s1"], 1)
                        dve.wait_ge(S["up_s1"], it * 4 + (2 * p + v + 1))
                        STT(d[:, 2:], bank[:, 0:T - 2], pc("fcw", w0), d[:, 2:], ALU.mult, ALU.add
                            ).then_inc(acc_free[(J_UP + v) % 2], 1)
                    dve.wait_ge(S["up_sg"], j + 1)
                    filled(dve, J_UP + 2 * p + 1, it, 4)
                    TT(f_s[p][:, :], f_s[p][:, :], f_v[p][:, :], ALU.mult).then_inc(S["up_a"], 1)
                    dve.wait_ge(S["up_hi"], j + 1)
                    TT(tile_of(fl, j), f_s[p][:, :], tile_of(fh, j).bitcast(F32), ALU.subtract
                       ).then_inc(S["up_lo"], 1)
            with dve.Fori(0, KT // 4) as it:
                add_residual(J_DN, lambda f: J_DN + 3 * f + 3, it, 12)
            norm_scale(2, None, "final", keep=True)
            norm_scale(3, 2, "normw2")
            def conv_tile(it):
                t0 = J_CV - DN_SHIFT
                filled(dve, t0, it, 4)
                dve.wait_ge(S["slab_used"], it * 4 + (J_CV + 3))
                TT(c_p[:, :], c_u[:, :], acc[(t0 + 2) % 2][:, :], ALU.mult).then_inc(acc_free[(t0 + 2) % 2], 1)
                filled(dve, t0 + 2, it, 4)
                wait(dve, S["cv_hi"], it * 1)
                wait(dve, S["cv_lo"], it * 1)
                n = it * 5
                TS(c_y[:, :], c_p[:, :], pc("cw2", it * 3 + 1), pc("cb2", it * 1), ALU.mult, ALU.add
                   ).then_inc(S["cv_y"], 1)
                dve.wait_ge(S["cv_y"], n + 1)
                STT(c_y[:, 1:], c_p[:, 0:T - 1], pc("cw2", it * 3), c_y[:, 1:], ALU.mult, ALU.add
                    ).then_inc(S["cv_y"], 1)
                dve.wait_ge(S["cv_y"], n + 2)
                STT(c_y[:, 0:T - 1], c_p[:, 1:], pc("cw2", it * 3 + 2), c_y[:, 0:T - 1], ALU.mult, ALU.add
                    ).then_inc(S["cv_y"], 1)
                filled(dve, t0 + 1, it, 4)
                dve.wait_ge(S["cv_y"], n + 3)
                TT(c_y[:, :], c_y[:, :], c_b[:, :], ALU.mult).then_inc(S["cv_y"], 1)
                filled(dve, t0 + 3, it, 4)
                dve.wait_ge(S["cv_y"], n + 4)
                TT(c_y[:, :], c_y[:, :], c_z[:, :], ALU.mult).then_inc(S["cv_y"], 1)
                dve.wait_ge(S["cv_hi"], it + 1)
                TT(tile_of(yl, it), c_y[:, :], tile_of(yh, it).bitcast(F32), ALU.subtract).then_inc(S["cv_lo"], 1)

            conv_tile(0)
            with dve.Fori(1, 4) as it:
                conv_tile(it)

            dve.memset(a_k[0][64:P, :], 0.0).then_inc(S["kz_set"], 1)
            dve.memset(a_k[1][0:64, :], 0.0).then_inc(S["kz_set"], 1)
            dve.wait_ge(S["kz_set"], 2)
            dve.wait_ge(S["wb_in"], 16)
            dve.wait_ge(S["cv_lo"], 4)

            def at_part(part, t):
                U, j = au[t % 2], J_AT - DN_SHIFT + 4 * t
                if part == 0:
                    wait(dve, S["at_s"], 8 * t)
                    dve.wait_ge(S["at_rs"], 4 * t + 2)
                    STT(a_q[:, :], U[:, 0, :], pc("qn"), a_rs[:, 0, :], ALU.mult, ALU.mult).then_inc(S["at_n"], 1)
                    dve.wait_ge(S["at_rs"], 4 * t + 4)
                    for h in range(2):
                        r = slice(64 * h, 64 * h + 64)
                        STT(a_k[h][r, :], U[r, 1, :], par[r, PAR["kn"]:PAR["kn"] + 1], a_rs[r, 1, :],
                            ALU.mult, ALU.mult).then_inc(S["at_n"], 1)
                for i in (2 * part, 2 * part + 1):
                    n = 8 * t + i
                    head, qb = 2 * t + i // 4, i % 4
                    lg_ = a_l[i % 4]
                    dve.wait_ge(S["at_s"], n + 1)
                    wait(dve, S["at_tr"], n - 3)
                    STT(lg_[:, :], (b5, b6)[i % 2][:, :], AT_DH ** -0.5,
                        wb[:, head, (3 - qb) * P:(3 - qb) * P + T], ALU.mult, ALU.add).then_inc(S["at_l"], 1)
                    dve.wait_ge(S["at_l"], n + 1)
                    dve.tensor_reduce(a_st[:, i, 0:1], lg_[:, :], AX_X, ALU.max, negate=True
                                      ).then_inc(S["at_mx"], 1)
                for i in (2 * part, 2 * part + 1):
                    n = 8 * t + i
                    dve.wait_ge(S["at_ex"], n + 1)
                    dve.reciprocal(a_st[:, i, 2:3], a_st[:, i, 1:2]).then_inc(S["at_sum"], 1)
                    dve.wait_ge(S["at_sum"], n + 1)
                    TS(a_l[i % 4][:, :], a_l[i % 4][:, :], a_st[:, i, 2:3], None, ALU.mult).then_inc(S["at_p"], 1)

            for t in range(4):
                for part in range(4):
                    at_part(part, t)
                dve.wait_ge(S["at_o"], 8 * t + 8)
                dve.wait_ge(S["at_silu"], t + 1)
                wait(dve, S["at_hi"], t)
                wait(dve, S["at_lo"], t)
                TT(a_y[:, :], b7[:, :], au[t % 2][:, 3, :], ALU.mult).then_inc(S["at_y"], 1)
                dve.wait_ge(S["at_hi"], t + 1)
                dve.wait_ge(S["at_y"], t + 1)
                TT(yl[:, 4 + t, :], a_y[:, :], yh[:, 4 + t, :].bitcast(F32), ALU.subtract).then_inc(S["at_lo"], 1)
            with dve.Fori(0, KT // 4) as it:
                for f in range(4):
                    t = J_O2 - DN_SHIFT + f
                    dve.wait_ge(S["slab_used"], it * 4 + (J_O2 + f + 1))
                    fo = it * 4 + f
                    TT(tile_of(xT, fo), tile_of(xT, fo), acc[t % 2][:, :], ALU.add).then_inc(acc_free[t % 2], 1)


def bucket(rel):
    n = np.abs(rel)
    nf = np.maximum(n, 1).astype(np.float32)
    large = 8 + (np.log(nf / np.float32(8)) / np.float32(np.log(128.0)) * np.float32(8)).astype(np.int32)
    return np.where(rel > 0, 16, 0) + np.where(n < 8, n, np.minimum(large, 15))


def constants():
    c = np.zeros((P, N_CONST), np.float32)
    i = np.arange(P)
    eye = np.eye(P, dtype=np.float32)
    c[:, K_ID:K_ID + P] = eye
    c[:, K_NID:K_NID + P] = -eye
    c[:, K_ONES:K_ONES + P] = 1
    c[:, K_BD:K_BD + P] = (i[:, None] // AT_DH) == (i[None] // AT_DH)
    for h in range(ML_HEADS):
        c[ROW_I + h, K_SELI + h] = 1
        c[ROW_F + h, K_NSELF + h] = -1
    c[:, K_CLAMP:K_CLAMP + P] = np.where(i[:, None] <= i[None], 0.0, NEG)
    for l in range(1, 8):
        n, half = P >> (l - 1), P >> l
        s, t = i[:, None], i[None]
        c[:, K_LMASK + (l - 1) * P:K_LMASK + l * P] = (s // n == t // n) & (s % n < half) & (t % n >= half)
    start = np.where(np.arange(T) % P == 0, 0.0, 1.0)
    c[:, K_HGMASK:K_HGMASK + T] = start
    c[:, K_RMASK:K_RMASK + T] = 1
    c[:ROW_I, K_RMASK:K_RMASK + T] = start
    c[:, K_SIGN] = 1
    c[ROW_F:ROW_F + 32, K_SIGN] = -1
    hot = np.zeros((P, W_LINE), np.float32)
    d = np.arange(1 - T, T)
    hot[bucket(d), np.arange(2 * T - 1)] = 1
    count = (np.abs(d) <= 64) * 1 + ((d % 4 == 0) & (np.abs(d) <= 256)) + (d % 16 == 0)
    hot[32, :2 * T - 1] = np.where(count > 0, np.log(np.maximum(count, 1)), NEG)
    return c, hot


def slabs_of(i):
    w_in, w_up, w_dn, w2 = i["w_in"][0], i["w_up"][0], i["w_down"][0], i["w_in_2"]
    br = (i["w_br_hg"][0], i["w_br_ml"][0], i["w_br_mb"][0])
    a = np.zeros((N_SLABS, P, KT * P), np.float32)

    def put(j, w, c, k0=0, n=KT):
        a[j].reshape(P, KT, P)[:, :n] = w[k0 * P:(k0 + n) * P, c:c + P].reshape(n, P, P).transpose(1, 0, 2)

    small = a[J_SMALL].reshape(P, KT, P)
    for row, c, n in ((ROW_DT, C_MBDT, MB_HEADS), (ROW_I, C_MLIF, ML_HEADS), (ROW_F, C_MLIF + ML_HEADS, ML_HEADS)):
        small[:, :, row:row + n] = w_in[:, c:c + n].reshape(KT, P, n).transpose(1, 0, 2)
    for u in range(HG_HEADS):
        for k, c in enumerate((C_HGF, C_HGQ, C_HGG, C_HGI)):
            put(J_HG + 4 * u + k, w_in, c + P * u)
    for u in range(ML_HEADS):
        for k, c in enumerate((C_MLQ + P * u, C_MLK + P * u, C_MLV + 2 * P * u, C_MLV + 2 * P * u + P,
                               C_MLO + 2 * P * u, C_MLO + 2 * P * u + P)):
            put(ml_slab(u) + k, w_in, c)
    for g in range(MB_GROUPS):
        for k, c in enumerate((C_MBX + 1024 + P * g, C_MBX + 1536 + P * g, C_MBX + 2 * P * g, C_MBX + 2 * P * g + P,
                               C_MBZ + 2 * P * g, C_MBZ + 2 * P * g + P)):
            put(mb_slab(g) + k, w_in, c)
    for b, j in enumerate((J_G0, J_G1, J_G2)):
        for f in range(KT):
            put(j + (2 * f if b < 2 else f), w_in, C_GATE + D * b + P * f)
            put(j + (2 * f + 1 if b < 2 else KT + f), br[b], P * f)
    for f in range(KT):
        put(J_O + f, i["w_out"][0], P * f)
        put(J_O2 + f, i["w_out_2"], P * f)
        for c, n in enumerate(DN_CHUNKS):
            put(J_DN + 3 * f + c, w_dn, P * f, 8 * c, n)
    for j in range(NF):
        put(J_UP + 2 * j, w_up, P * j)
        put(J_UP + 2 * j + 1, w_up, D_FF + P * j)
    for t in range(4):
        for k in range(4):
            put(J_CV + 4 * t + k, w2, 512 * k + P * t)
            put(J_AT + 4 * t + k, w2, 2048 + 512 * k + P * t)
    return a


def params_of(i):
    a = np.zeros((P, N_PAR), np.float32)

    def put(name, v):
        a[:, PAR[name]:PAR[name] + v.shape[1]] = v

    def cols(v):
        return v.reshape(-1, P).T

    def taps(w):
        return w.reshape(w.shape[0], -1, P).transpose(2, 1, 0).reshape(P, -1)

    put("norm1", cols(i["norm1_g"]))
    put("norm2", cols(i["norm2_g"]))
    put("final", cols(i["final_g"]))
    put("normw2", cols(i["norm_w_2"]))
    put("lb", cols(i["hg_lb_logits"]))
    put("hgg", cols(i["hg_norm_g"]))
    put("mlcw", taps(i["ml_conv_w"][0]))
    put("mlcb", cols(i["ml_conv_b"]))
    put("mlg", cols(i["ml_norm_g"]))
    put("mbcw", taps(i["mb_conv_w"][0]))
    put("mbcb", cols(i["mb_conv_b"]))
    put("mbg", cols(i["mb_norm_g"]))
    put("mbd", cols(np.repeat(i["mb_d"].reshape(-1), 64)))
    put("fcw", taps(i["ffn_conv_w"][0]))
    put("fcb", cols(i["ffn_conv_b"]))
    put("cw2", taps(i["conv_w_2"]))
    put("cb2", cols(i["conv_b_2"]))
    put("qn", cols(np.tile(i["q_norm_w_2"], 2)))
    put("kn", cols(np.tile(i["k_norm_w_2"], 2)))
    a[ROW_DT:ROW_DT + MB_HEADS, PAR["rowb"]] = i["mb_dt_bias"][0]
    a[ROW_I:ROW_I + ML_HEADS, PAR["rowb"]] = i["ml_gate_b"][0, :ML_HEADS]
    a[ROW_F:ROW_F + ML_HEADS, PAR["rowb"]] = i["ml_gate_b"][0, ML_HEADS:]
    a[ROW_DT:ROW_DT + MB_HEADS, PAR["alog"]] = i["mb_a_log"][0]
    a[:32, PAR["rel"]:PAR["rel"] + AT_HEADS] = i["rel_bias_2"]
    a[32, PAR["rel"]:PAR["rel"] + AT_HEADS] = 1
    return a


def kernel(**inputs):
    import concourse.bacc as bacc
    from concourse.bass_utils import run_bass_kernel_spmd

    i = {k: np.asarray(v) for k, v in inputs.items()}
    con, hot = constants()
    arrays = {"slabs": slabs_of(i), "x": np.ascontiguousarray(i["x"]), "params": params_of(i), "consts": con,
              "onehot": hot}
    nc = bacc.Bacc("TRN2", target_bir_lowering=False, num_devices=1)
    ins = [nc.dram_tensor(n, a.shape, F32, kind="ExternalInput").ap() for n, a in arrays.items()]
    bias_scratch = nc.dram_tensor("bias_scratch", (AT_HEADS, P, W_LINE), F32).ap()
    out = nc.dram_tensor("out", (1, T, D), F32, kind="ExternalOutput").ap()
    build(nc, *ins, bias_scratch, out)
    r = run_bass_kernel_spmd(nc, [arrays], core_ids=[0])
    return r.results[0]["out"]
```

```python
from contextlib import ExitStack

import numpy as np

import concourse.bass as bass
from concourse import mybir

P = 128
T = 512
NB = T // P
D = 1024
KT = D // P
F32 = mybir.dt.float32
F32R = mybir.dt.float32r
U32 = mybir.dt.uint32
ALU = mybir.AluOpType
ACT = mybir.ActivationFunctionType
AX_X = mybir.AxisListType.X
EPS = 1e-6
NEG = -1e30

HG_HEADS, ML_HEADS, MB_GROUPS, MB_HEADS = 8, 4, 4, 16
D_FF = 2816
NF = D_FF // P
AT_HEADS, AT_DH = 8, 64

C_HGQ, C_HGF, C_HGI, C_HGG = 0, 1024, 2048, 3072
C_MLQ, C_MLK, C_MLV, C_MLIF, C_MLO = 4096, 4608, 5120, 6144, 6152
C_MBZ, C_MBX, C_MBDT, C_GATE = 7176, 8200, 10248, 10264

HG_F, HG_Q, HG_G, HG_I = range(4)

J_SMALL = 0
J_HG = 1
J_ML0 = J_HG + 4 * HG_HEADS
J_G0 = J_ML0 + 6
J_ML1 = J_G0 + 16
J_MB0 = J_ML1 + 18
J_G1 = J_MB0 + 6
J_MB1 = J_G1 + 16
J_G2 = J_MB1 + 18
J_O = J_G2 + 16
J_UP = J_O + 8
J_DN = J_UP + 2 * NF
DN_CHUNKS = (8, 8, 6)
J_AT = J_DN + 24
J_O2 = J_AT + 32
N_SLABS = J_O2 + 8
DN_SHIFT = 16

K_ID, K_ONES, K_SEL2, K_BD, K_SELI, K_NSELF, K_CLAMP = (P * i for i in range(7))
K_LMASK = 7 * P
K_HGMASK = K_LMASK + 7 * P // 2
K_RMASK = K_HGMASK + T
K_SIGN = K_RMASK + T
N_CONST = K_SIGN + 1

_PAR = [("norm1", 8), ("norm2", 8), ("final", 8), ("normw2", 8), ("lb", 8), ("hgg", 1), ("mlcw", 32), ("mlcb", 8),
        ("mlg", 2), ("mbcw", 64), ("mbcb", 16), ("mbg", 8), ("mbd", 8), ("fcw", 132), ("fcb", 44), ("cw2", 12),
        ("cb2", 4), ("qn", 1), ("kn", 1), ("rowb", 1), ("alog", 1), ("rel", 8)]
PAR = {}
N_PAR = 0
for _n, _w in _PAR:
    PAR[_n] = N_PAR
    N_PAR += _w

ROW_DT, ROW_I, ROW_F = 0, 32, 64
W_BIAS = 896
W_LINE = 1024


def ml_slab(u):
    return J_ML0 if u == 0 else J_ML1 + 6 * (u - 1)


def mb_slab(g):
    return J_MB0 if g == 0 else J_MB1 + 6 * (g - 1)


def at_slab(t, i):
    return J_AT + i if t == 0 else J_AT + 4 + 8 * (t - 1) + 2 * i


def cv_slab(t, i):
    return J_AT + 4 + 8 * t + 2 * i + 1 if t < 3 else J_AT + 28 + i


def lin(c, it, k):
    return c if it is None else it * k + c


def wait(eng, sem, n):
    if not isinstance(n, int) or n > 0:
        eng.wait_ge(sem, n)


def tiles_before(part, n):
    return {0: [[], [], [], []], 4: [[0], [1], [2], [3]], 6: [[0], [1, 2], [3], [4, 5]]}[n][part]


def build(nc, slabs, x, par_d, const_d, onehot_d, bias_scratch, out):
    with ExitStack() as ctx:
        start = -(-nc.sbuf_base // 64) * 64

        def arena(at):
            pos = [at]

            def take(name, shape, dt=F32):
                n = 4
                for s in shape[1:]:
                    n *= s
                pos[0] = -(-pos[0] // 64) * 64
                t = nc.alloc_sbuf_tensor_at(name, shape, dt, offset=pos[0])
                pos[0] += n
                assert pos[0] <= nc.sbuf_usable_end, (name, pos[0])
                return t
            return take, pos

        sb, sb_pos = arena(start)
        raw = sb("raw", [P, 4, KT, P])
        wh = sb("wh", [P, 2, KT, P], F32R)
        wl = sb("wl", [P, 2, KT, P], F32R)
        xT = sb("xT", [P, KT, T])
        hh = sb("hh", [P, KT, T], F32R)
        hl = sb("hl", [P, KT, T], F32R)
        con_at = -(-sb_pos[0] // 64) * 64
        con = sb("con", [P, N_CONST])
        par = sb("par", [P, N_PAR])
        zero = sb("zero", [P, 1])
        tick = sb("tick", [P, 1])
        gg = sb("gg", [P, KT])
        lbc = sb("lbc", [P, 8])
        lbt = sb("lbt", [P, 3, 8])
        sb_pos[0] = -(-sb_pos[0] // 64) * 64
        y_at = sb_pos[0]
        yh = sb("yh", [P, KT, T], F32R)
        yl = sb("yl", [P, KT, T], F32R)
        area = sb_pos[0]

        mx, mx_pos = arena(area)
        mixed = mx("mixed", [P, KT, T])
        unit_at = mx_pos[0]
        unit = [mx(f"unit{i}", [P, 6, T]) for i in range(2)]
        gbuf = arena(unit_at)[0]("gbuf", [P, KT, T])
        csh = mx("csh", [P, T], F32R)
        csl = mx("csl", [P, T], F32R)
        selr = mx("selr", [P, 2 * P], F32R)
        acol = mx("acol", [P, NB, ML_HEADS])
        dtc = mx("dtc", [P, NB, MB_HEADS])
        ncc = mx("ncc", [P, NB, MB_HEADS])
        totb = mx("totb", [P, NB, MB_HEADS])
        dend = mx("dend", [P, 6, MB_HEADS])
        scratch = mx_pos[0]

        psum = [ctx.enter_context(nc.psum_tensor(f"bank{i}", [P, T], F32)) for i in range(8)]
        acc = psum[:2]
        b2, b3, b4, b5, b6, b7 = psum[2:]

        names = """params_in ident_in x_in0 x_in1 onehot_in slab_hi slab_split slab_used acc_free0 acc_free1 zero_set
            pro_tr pro_xT nrm_sq nrm_ss nrm_rs nrm_h nrm_hi nrm_lo lt_sq lt_add lt_ss lt_step x2_done lb_step
            wb_mm wb_ev wb_out wb_in row_step row_act row_mm row_ev row_a row_done rnm_done
            conv_step
            hg_silu hg_e hg_l hg_lf hg_b hg_f hg_k hg_d hg_ex hg_eb hg_x hg_tr hg_v hg_kt hg_lv hg_z hg_at hg_stp
            hg_s hg_o hg_sq hg_ss hg_rs hg_y hg_hi hg_lo
            ml_silu ml_tanh ml_nm ml_tr ml_v ml_dx ml_ex ml_qk ml_pt ml_num ml_nm2 ml_ps ml_em ml_h ml_dn ml_sq ml_ss
            ml_rs ml_y ml_hi ml_lo
            mb_silu mb_tr mb_xd mb_cb mb_nm mb_dx mb_ex mb_pt mb_ym mb_y mb_sq mb_ss mb_rs mb_hi mb_lo
            g_tanh g_acc o_hi o_lo up_c up_s1 up_sg up_a up_hi up_lo
            cv_z cv_y cv_hi cv_lo
            at_silu at_sq at_ss at_tr at_rs at_v at_n at_s at_l at_mx at_ex at_sum at_p at_pt at_pe at_o at_y
            at_hi at_lo kz_set out_tr out_ev out_dma0 out_dma1""".split()
        S = {n: ctx.enter_context(nc.semaphore(n)) for n in names}
        slab_in = [ctx.enter_context(nc.semaphore(f"slab_in{i}")) for i in range(4)]
        acc_free = [S["acc_free0"], S["acc_free1"]]

        def cc(k, n=P):
            return con[:, k:k + n]

        ident, ones, clampm = cc(K_ID), cc(K_ONES), cc(K_CLAMP)

        def pc(name, i=0):
            if isinstance(i, int):
                return par[:, PAR[name] + i:PAR[name] + i + 1]
            return par[:, bass.ds(i + PAR[name], 1)]

        def tile_of(buf, f):
            if isinstance(f, int):
                return buf[:, f, :]
            return buf[:, bass.ds(f, 1), :].rearrange("p a t -> p (a t)")

        def blk(ap, b, n=1):
            return ap[:, b * P:(b + n) * P]

        def stage(at=scratch):
            return arena(at)[0]

        pr = stage()
        xs = pr("xs", [P, NB, D])
        nr_at = y_at + NF * 4 * T
        nr, nr_pos = arena(nr_at)
        sqn = [nr(f"sqn{i}", [P, T]) for i in range(2)]
        rsn = nr("rsn", [P, T])
        htn = [nr(f"htn{i}", [P, T]) for i in range(2)]
        ro = stage(y_at)
        rz, r1, r2, r3, r4, r5, ra = (ro(f"row{i}", [P, T]) for i in range(7))
        cum = ro("cum", [P, T])
        rdg = ro("rdg", [P, NB, MB_HEADS])
        rac = ro("rac", [P, 1])
        oneh = ro("oneh", [P, W_LINE])
        wrow = ro("wrow", [AT_HEADS, W_LINE])

        hg = stage()
        e0, e1, lf, bb, kk, eb, k1, q1, at_ = (hg(f"hg{i}", [P, T]) for i in range(9))
        dd = [hg(f"hgd{i}", [P, T]) for i in range(3)]
        ex = [hg(f"hgx{i}", [P, T]) for i in range(3)]
        zz = [hg(f"hgz{i}", [P, T]) for i in range(3)]
        hm = stage(area)
        sqh, rsh, yth, vt = (hm(f"hgm{i}", [P, T]) for i in range(4))
        kt_ = hm("hgkt", [P, 3 * P])
        st_ = hm("hgst", [P, 3 * P])

        ml = stage()
        m_e = ml("m_e", [P, 1280])
        m_p = ml("m_p", [P, 1280])
        m_ps = ml("m_ps", [P, T])
        m_v = ml("m_v", [P, NB, 2 * P])
        m_em, m_dn, m_rd, m_rs = (ml(f"m_{i}", [P, T]) for i in range(4))
        m_h = ml("m_h", [P, 2, T])
        m_sq = ml("m_sq", [P, 2, T])
        mb = stage()
        s_e = mb("s_e", [P, 1280])
        s_p = [mb(f"s_p{i}", [P, 1280]) for i in range(2)]
        s_x = mb("s_x", [P, NB, 4, 64])
        s_y = mb("s_y", [P, 2, T])
        s_sq = mb("s_sq", [P, 2, T])
        s_rs = mb("s_rs", [P, T])
        gs = stage()
        tg = [gs(f"tg{i}", [P, T]) for i in range(2)]
        tm = gs("tm", [P, T])

        nr_end = nr_pos[0]
        fl = stage(y_at)("fl", [P, NF, T], F32R)
        ff = stage(nr_end)
        fh = ff("fh", [P, NF, T], F32R)
        f_g = [ff(f"f_g{i}", [P, T]) for i in range(2)]
        f_v = [ff(f"f_v{i}", [P, T]) for i in range(2)]
        f_s = [ff(f"f_s{i}", [P, T]) for i in range(2)]

        lt_sum = {1: [htn[0]], 2: f_g}
        lt_new = {1: [sqn], 2: [f_v, f_s]}

        sec = stage(nr_end)
        wb = sec("wb", [P, AT_HEADS, W_BIAS])
        au = [sec(f"au{i}", [P, 4, T]) for i in range(2)]
        cv = stage(con_at + 4 * K_SELI)
        c_u, c_b, c_y, c_z = (cv(f"c_{i}", [P, T]) for i in range(4))
        a_l = [sec(f"a_l{i}", [P, T]) for i in range(4)]
        a_q = sec("a_q", [P, T])
        an = stage(area)
        a_rs = an("a_rs", [P, 2, T])
        a_pt = [an(f"a_pt{i}", [P, T]) for i in range(2)]
        a_sq = an("a_sq", [P, 2, T])
        a_k = [sec(f"a_k{i}", [P, T]) for i in range(2)]
        a_v = sec("a_v", [P, NB, P])
        a_st = sec("a_st", [P, 8, 3])
        a_y = sqn[0]
        os_ = htn

        OFF = {0: (512, 384), 2: (896, 128), 1: (1024, 256)}

        block = ctx.enter_context(nc.Block())

        def filled(eng, j0, it=None, k=0):
            eng.wait_ge(acc_free[j0 % 2], lin(j0 // 2 + 1, it, k // 2))

        @block.sync
        def _(sp):
            def load(slot, j, use):
                wait(sp, S["slab_split"], use)
                src = slabs[bass.ds(j, 1)] if not isinstance(j, int) else slabs[j:j + 1]
                sp.dma_start(raw[:, slot:slot + 1].rearrange("p a k f -> p a (k f)"),
                             src.rearrange("a p n -> p a n")).then_inc(slab_in[slot], 16)

            for i in range(2):
                c = slice(i * D // 2, (i + 1) * D // 2)
                sp.dma_start(xs[:, :, c], x.rearrange("a (b p) d -> p (a b) d", p=P)[:, :, c]
                             ).then_inc(S[f"x_in{i}"], 16)
            for j in range(4):
                load(j, j, 0)
            with sp.Fori(1, N_SLABS // 4) as it:
                for i in range(4):
                    load(i, it * 4 + i, it * 4 + (i - 3))
            for j in range(N_SLABS // 4 * 4, N_SLABS):
                load(j % 4, j, j - 3)
            for f in range(KT):
                sp.wait_ge(S["out_ev"], f + 1)
                sp.dma_start(out.rearrange("a (b p) d -> p (a b) d", p=P)[:, :, f * P:(f + 1) * P],
                             os_[f % 2][:, :].rearrange("p (b d) -> p b d", b=NB)
                             ).then_inc(S[f"out_dma{f % 2}"], 16)
            sp.wait_ge(S["out_dma0"], 16 * KT // 2)
            sp.wait_ge(S["out_dma1"], 16 * KT // 2)

        @block.gpsimd
        def _(pool):
            nc.gpsimd.memset(zero[:, :], 0.0).then_inc(S["zero_set"], 1)
            pool.wait_ge(S["zero_set"], 1)

            def split(i, j, nth):
                r = raw[:, i].rearrange("p k f -> p (k f)")
                h = wh[:, i % 2].rearrange("p k f -> p (k f)")
                lo = wl[:, i % 2].rearrange("p k f -> p (k f)")
                pool.wait_ge(slab_in[i], nth)
                wait(pool, S["slab_used"], j - 1)
                pool.tensor_tensor(h, r, zero[:, 0:1].broadcast_to([P, KT * P]), ALU.add).then_inc(S["slab_hi"], 1)
                pool.wait_ge(S["slab_hi"], j + 1)
                pool.tensor_tensor(lo, r, h.bitcast(F32), ALU.subtract).then_inc(S["slab_split"], 1)

            for j in range(4):
                split(j, j, 16)
            with pool.Fori(1, N_SLABS // 4) as it:
                for i in range(4):
                    split(i, it * 4 + i, it * 16 + 16)
            for j in range(N_SLABS // 4 * 4, N_SLABS):
                split(j % 4, j, 16 * (j // 4 + 1))

        @block.tensor
        def _(pe):
            mm = pe.matmul

            def project(j0, it=None, k=0, src=(hh, hl), n=KT, base=0, t0=None, first=True, last=True,
                        ready=(), order=()):
                t0 = j0 if t0 is None else t0
                bank, s = acc[t0 % 2], j0 % 2
                pe.wait_ge(S["slab_split"], lin(j0 + 1, it, k))
                if first:
                    wait(pe, acc_free[t0 % 2], lin(t0 // 2, it, k // 2))
                for i, b in enumerate(order or range(n)):
                    if ready:
                        pe.wait_ge(*ready[i])
                    xh, xl = src[0][:, base + b, :], src[1][:, base + b, :]
                    mm(bank[:, :], wh[:, s, b, :], xh, start=first and i == 0, stop=False)
                    mm(bank[:, :], wh[:, s, b, :], xl, start=False, stop=False)
                    ins = mm(bank[:, :], wl[:, s, b, :], xh, start=False, stop=last and i == n - 1)
                ins.then_inc(S["slab_used"], 1)

            def on_all(bank, c, sem):
                w = selr[:, c:c + 1].broadcast_to([P, P])
                mm(bank[:, :], w, csh[:, :], start=True, stop=False)
                mm(bank[:, :], w, csl[:, :], start=False, stop=True).then_inc(sem, 1)

            def norm_sum(k, f):
                pe.wait_ge(S["nrm_sq"], 8 * k + f + 1)
                if f == 0:
                    wait(pe, S["nrm_rs"], 2 * k)
                mm(b6[:, :], ones, sqn[f % 2][:, :], start=f == 0, stop=f == KT - 1).then_inc(S["nrm_ss"], 1)

            def norm(k):
                for f in range(KT):
                    norm_sum(k, f)

            def late_sums(m):
                for q in range(m):
                    pe.wait_ge(S["lt_add"], 6 * (m - 1) + 5 * m + q + 1)
                    mm((b6, b7)[q][:, :], ones, lt_sum[m][q][:, :], start=True, stop=False)
                for q in range(m):
                    pe.wait_ge(S["lt_sq"], 8 * (m - 1) + 7 * m + q + 1)
                    mm((b6, b7)[q][:, :], ones, lt_new[m][q][1][:, :], start=False, stop=True
                       ).then_inc(S["lt_ss"], 1)

            pe.wait_ge(S["ident_in"], 16)
            for f in range(KT):
                pe.wait_ge(S[f"x_in{f // 4}"], 16)
                wait(pe, S["pro_xT"], f - 3)
                for b in range(NB):
                    ins = pe.transpose(blk(psum[2 + f % 4], b), xs[:, b, f * P:(f + 1) * P], ident)
                ins.then_inc(S["pro_tr"], 1)
            norm(0)
            pe.wait_ge(S["params_in"], 32)
            pe.wait_ge(S["onehot_in"], 16)
            pe.wait_ge(S["pro_xT"], 8)
            for c, bank in ((0, b7), (1, b5)):
                mm(bank[0:AT_HEADS, :], par[:, PAR["rel"]:PAR["rel"] + AT_HEADS], oneh[:, c * T:(c + 1) * T],
                   start=True, stop=True).then_inc(S["wb_mm"], 1)
            project(J_SMALL, ready=[(S["nrm_lo"], b + 1) for b in range(KT)])
            for i in range(4):
                project(J_HG + i)
            pe.wait_ge(S["row_a"], 1)
            mm(b4[:, :], cc(K_SELI), rz[:, :], start=True, stop=False)
            mm(b4[:, :], cc(K_NSELF), cum[:, :], start=False, stop=True).then_inc(S["row_mm"], 1)
            pe.wait_ge(S["wb_ev"], 2)
            for b in range(NB):
                pe.transpose(blk(b6, b), blk(cum, b), ident)
            for b in range(NB):
                ins = pe.transpose(blk(b7, b), blk(r5, b), ident)
            ins.then_inc(S["row_mm"], 1)
            pe.wait_ge(S["row_done"], 4)
            mm(b5[:, 0:NB * MB_HEADS], ones, rdg[:, :, :].rearrange("p b h -> p (b h)"),
               start=True, stop=True).then_inc(S["row_mm"], 1)
            pe.wait_ge(S["row_ev"], 1)
            for b in range(NB):
                ins = pe.transpose(blk(b3, b), blk(ra, b), ident)
            ins.then_inc(S["row_mm"], 1)

            def blk_nodes(z, l):
                n, half = P >> (l - 1), P >> l
                return z[:, :].rearrange("p (b c n) -> p b c n", b=NB, n=n)[:, :, :, half:]

            def hg_level(l, u, p):
                pe.wait_ge(S["hg_z"], u * 14 + 2 * l)
                pe.wait_ge(S["hg_at"], u * 8 + (l - 1))
                z, bank = zz[l % 3], (b2, b3)[l % 2]
                right = blk_nodes(z, l)
                for b in range(NB):
                    ins = mm(bank[:, b * P // 2:(b + 1) * P // 2], blk(z, b), right[:, b, :, :], start=True, stop=True)
                ins.then_inc(S["hg_lv"], 1)

            def hg_part(part, u, p, j0, it):
                U = unit[p]
                if part == 0:
                    if not isinstance(u, int) or u:
                        hg_out(u - 1)
                    filled(pe, j0 + 3, it, 8)
                    wait(pe, S["hg_kt"], u * 1)
                    for b in range(NB):
                        ins = pe.transpose(blk(b4, b), blk(U[:, HG_I, :], b), ident)
                    ins.then_inc(S["hg_tr"], 1)
                    pe.wait_ge(S["hg_k"], u + 1)
                    pe.wait_ge(S["hg_silu"], u * 2 + 1)
                    wait(pe, S["hg_at"], u * 8)
                    for b in range(NB):
                        ins = mm(blk(b2, b), blk(kk, b), blk(U[:, HG_Q, :], b), start=True, stop=True)
                    ins.then_inc(S["hg_lv"], 1)
                    pe.wait_ge(S["hg_x"], u * 2 + 1)
                    pe.wait_ge(S["hg_v"], u + 1)
                    for b in range(3):
                        ins = pe.transpose(blk(b4, b), blk(k1, b), ident)
                    ins.then_inc(S["hg_tr"], 1)
                elif part == 1:
                    if not isinstance(u, int) or u:
                        hg_sum(u - 1)
                    pe.wait_ge(S["hg_kt"], u + 1)
                    wait(pe, S["hg_s"], u * 3)
                    for b in range(3):
                        ins = mm(blk(b5, b), blk(kt_, b), blk(vt, b), start=True, stop=True)
                    ins.then_inc(S["hg_stp"], 1)
                    hg_level(1, u, p)
                    hg_level(2, u, p)
                elif part == 2:
                    for l in (3, 4, 5):
                        hg_level(l, u, p)
                else:
                    hg_level(6, u, p)
                    hg_level(7, u, p)

            def hg_out(u):
                pe.wait_ge(S["hg_at"], u * 8 + 8)
                pe.wait_ge(S["hg_s"], u * 3 + 3)
                pe.wait_ge(S["hg_x"], u * 2 + 2)
                wait(pe, S["hg_y"], u * 2)
                for b in range(NB):
                    ins = mm(blk(b6, b), blk(vt, b), blk(at_, b), start=True, stop=b == 0)
                    if b:
                        ins = mm(blk(b6, b), blk(st_, b - 1), blk(q1, b), start=False, stop=True)
                ins.then_inc(S["hg_o"], 1)

            def hg_sum(u):
                pe.wait_ge(S["hg_sq"], u + 1)
                wait(pe, S["hg_rs"], u * 2)
                mm(b7[:, :], ones, sqh[:, :], start=True, stop=True).then_inc(S["hg_ss"], 1)


            def ml_part(part, u):
                p = u % 2
                U, j = unit[p], ml_slab(u)
                if part == 0:
                    if u == 0:
                        pe.wait_ge(S["hg_lo"], HG_HEADS)
                        pe.wait_ge(S["hg_hi"], HG_HEADS)
                        filled(pe, J_G0 + 15)
                    wait(pe, S["ml_h"], 2 * u)
                    on_all(b5, ROW_I + u, S["ml_nm"])
                    for v in range(2):
                        filled(pe, j + 2 + v)
                        for b in range(NB):
                            ins = pe.transpose(blk((b6, b7)[v], b), blk(U[:, 2 + v, :], b), ident)
                        ins.then_inc(S["ml_tr"], 1)
                elif part == 1:
                    pe.wait_ge(S["ml_silu"], 2 * u + 2)
                    wait(pe, S["ml_em"], u)
                    wait(pe, S["ml_rs"], 2 * u)
                    q, k = U[:, 0, :], U[:, 1, :]
                    for b in range(NB):
                        ins = mm(blk(b2, b), blk(k, b), blk(q, b), start=True, stop=True)
                    ins.then_inc(S["ml_qk"], 1)
                    mm(b3[:, 0:384], blk(k, 0), blk(q, 1, 3), start=True, stop=True)
                    mm(b3[:, 384:512], blk(k, 2), blk(q, 3), start=True, stop=True).then_inc(S["ml_qk"], 1)
                    mm(b4[:, 0:256], blk(k, 1), blk(q, 2, 2), start=True, stop=True).then_inc(S["ml_qk"], 1)
                elif part == 2:
                    pe.wait_ge(S["ml_pt"], 3 * u + 3)
                    pe.wait_ge(S["ml_v"], 2 * u + 2)
                    pe.wait_ge(S["ml_dx"], 4 * u + 4)
                    pe.wait_ge(S["ml_ex"], 4 * u + 4)
                    for bank, w in ((b6, lambda b: m_v[:, b, 0:P]), (b7, lambda b: m_v[:, b, P:2 * P])):
                        mm(bank[:, P:T], w(0), m_p[:, 512:896], start=True, stop=False)
                        mm(bank[:, 2 * P:T], w(1), m_p[:, 1024:1280], start=False, stop=False)
                        mm(bank[:, 3 * P:T], w(2), m_p[:, 896:1024], start=False, stop=False)
                        for b in range(NB):
                            ins = mm(blk(bank, b), w(b), m_p[:, b * P:(b + 1) * P], start=False, stop=b == NB - 1)
                        ins.then_inc(S["ml_num"], 1)
                    pe.wait_ge(S["ml_ps"], 4 * u + 4)
                    mm(b5[:, :], ones, m_ps[:, :], start=True, stop=True).then_inc(S["ml_num"], 1)
                    on_all(b2, P + u, S["ml_nm2"])

            def ml_finish(u):
                for v in range(2):
                    pe.wait_ge(S["ml_sq"], 2 * u + v + 1)
                    ins = mm(b3[:, :], ones, m_sq[:, v, :], start=v == 0, stop=v == 1)
                ins.then_inc(S["ml_ss"], 1)

            def mb_bcast(g, h):
                n = 4 * g + h
                if h == 0:
                    wait(pe, S["mb_rs"], 2 * g)
                if n:
                    pe.wait_ge(S["mb_dx"], 4 * n)
                    pe.wait_ge(S["mb_ex"], 7 * n)
                on_all(b5, n, S["mb_nm"])

            def mb_values(g, h):
                n = 4 * g + h
                pe.wait_ge(S["mb_pt"], 3 * n + 3)
                if h == 0:
                    pe.wait_ge(S["mb_xd"], 2 * g + 2)
                pt = s_p[n % 2]
                rows = slice(64 * (h % 2), 64 * (h % 2) + 64)
                bank = (b6, b7)[h // 2]
                mm(bank[rows, P:T], s_x[:, 0, h, :], pt[:, 512:896], start=True, stop=False)
                mm(bank[rows, 2 * P:T], s_x[:, 1, h, :], pt[:, 1024:1280], start=False, stop=False)
                mm(bank[rows, 3 * P:T], s_x[:, 2, h, :], pt[:, 896:1024], start=False, stop=False)
                for b in range(NB):
                    ins = mm(bank[rows, b * P:(b + 1) * P], s_x[:, b, h, :], pt[:, b * P:(b + 1) * P],
                             start=False, stop=b == NB - 1)
                ins.then_inc(S["mb_ym"], 1)

            def mb_start(g):
                U = unit[g % 2]
                if g == 0:
                    pe.wait_ge(S["ml_lo"], 2 * ML_HEADS)
                    pe.wait_ge(S["ml_hi"], 2 * ML_HEADS)
                    pe.wait_ge(S["g_acc"], KT)
                pe.wait_ge(S["mb_silu"], 6 * g + 4)
                wait(pe, S["mb_y"], 6 * g - 3)
                for i in range(2):
                    for b in range(2):
                        for v in range(2):
                            ins = pe.transpose(blk((b6, b7)[i], 2 * b + v), blk(U[:, 2 + v, :], 2 * i + b), ident)
                    ins.then_inc(S["mb_tr"], 1)
                wait(pe, S["mb_pt"], 12 * g)
                bm, cm = U[:, 0, :], U[:, 1, :]
                for b in range(NB):
                    mm(blk(b2, b), blk(bm, b), blk(cm, b), start=True, stop=True)
                mm(b3[:, 0:384], blk(bm, 0), blk(cm, 1, 3), start=True, stop=True)
                mm(b3[:, 384:512], blk(bm, 2), blk(cm, 3), start=True, stop=True)
                mm(b4[:, 0:256], blk(bm, 1), blk(cm, 2, 2), start=True, stop=True).then_inc(S["mb_cb"], 1)
                mb_bcast(g, 0)

            def mb_finish(g):
                pe.wait_ge(S["mb_dx"], 16 * (g + 1))
                pe.wait_ge(S["mb_ex"], 28 * (g + 1))
                for v in range(2):
                    pe.wait_ge(S["mb_sq"], 2 * g + v + 1)
                    ins = mm(b5[:, :], ones, s_sq[:, v, :], start=v == 0, stop=v == 1)
                ins.then_inc(S["mb_ss"], 1)

            def hg_pair(it):
                for p in range(2):
                    for part in range(4):
                        project(J_HG + 4 + 4 * p + part, it, 8)
                        if it is None and p == 0 and part == 0:
                            pe.wait_ge(S["row_done"], 8)
                        hg_part(part, lin(p, it, 2), p, J_HG + 4 * p, it)

            hg_pair(None)
            with pe.Fori(1, HG_HEADS // 2 - 1) as it:
                hg_pair(it)
            u = HG_HEADS - 2
            for part in range(4):
                project(J_HG + 4 * (u + 1) + part)
                hg_part(part, u, u % 2, J_HG + 4 * u, None)
            u = HG_HEADS - 1
            for part in range(3):
                for i in tiles_before(part, 6):
                    project(J_ML0 + i)
                hg_part(part, u, u % 2, J_HG + 4 * u, None)
            project(J_ML0 + 4)
            hg_part(3, u, u % 2, J_HG + 4 * u, None)
            project(J_ML0 + 5)
            hg_out(u)
            project(J_G0)
            hg_sum(u)

            def gates(j0, lo_sem):
                project(j0 + 1, src=(yh, yl), ready=[(lo_sem, b + 1) for b in range(KT)])
                project(j0 + 2)
                project(j0 + 3, src=(yh, yl))
                with pe.Fori(1, KT // 2) as it:
                    for f in range(2):
                        project(j0 + 2 * f, it, 4)
                        project(j0 + 2 * f + 1, it, 4, src=(yh, yl))

            gates(J_G0, S["hg_lo"])
            for u in range(ML_HEADS):
                last = u + 1 == ML_HEADS
                nxt = J_MB0 if last else ml_slab(u + 1)
                for part in range(4):
                    for i in tiles_before(part, 6):
                        project(nxt + i)
                        if last and i == 4:
                            ml_finish(u)
                    if part == 0 and u:
                        ml_finish(u - 1)
                    ml_part(part, u)
            project(J_G1)
            gates(J_G1, S["ml_lo"])
            for g in range(MB_GROUPS):
                nxt = mb_slab(g + 1) if g + 1 < MB_GROUPS else J_G2
                mb_start(g)
                for h in range(4):
                    project(nxt + h)
                    if h < 3:
                        mb_bcast(g, h + 1)
                    mb_values(g, h)
                project(nxt + 4)
                project(nxt + 5)
                mb_finish(g)
            project(J_G2 + 6)
            project(J_G2 + 7)
            for f in range(4):
                project(J_G2 + KT + f, src=(yh, yl), ready=() if f else [(S["mb_lo"], b + 1) for b in range(KT)])
            with pe.Fori(1, KT // 4) as it:
                for f in range(4):
                    project(J_G2 + KT + f, it, 4, src=(yh, yl))

            for f in range(KT):
                project(J_O + f, ready=[(S["o_lo"], b + 1) for b in range(KT)] if f == 0 else ())
            late_sums(1)
            project(J_UP, ready=[(S["nrm_lo"], KT + 1 + b) for b in range(KT)])
            project(J_UP + 1)
            project(J_UP + 2)
            project(J_UP + 3)
            with pe.Fori(1, NF // 2) as it:
                for j in range(2):
                    project(J_UP + 2 * j, it, 4)
                    project(J_UP + 2 * j + 1, it, 4)
            for f in range(KT):
                for c, n in enumerate(DN_CHUNKS):
                    project(J_DN + 3 * f + c, src=(fh, fl), n=n, base=8 * c, t0=J_DN + f, first=c == 0, last=c == 2,
                            ready=() if f else [(S["up_lo"], 8 * c + b + 1) for b in range(n)])
            late_sums(2)
            for i in range(4):
                project(J_AT + i, t0=J_AT - DN_SHIFT + i,
                        ready=[(S["nrm_lo"], 2 * KT + 1 + b) for b in range(KT)] if i == 0 else ())
            def at_scores(i, t):
                n = 8 * t + i
                wait(pe, S["at_l"], n - 1)
                mm((b5, b6)[i % 2][:, :], blk(a_q, i % 4), a_k[i // 4][:, :], start=True, stop=True
                   ).then_inc(S["at_s"], 1)

            def at_turn(i, t):
                n = 8 * t + i
                pe.wait_ge(S["at_p"], n + 1)
                wait(pe, S["at_pt"], n - 1)
                for b in range(NB):
                    ins = pe.transpose(blk((b2, b3)[i % 2], b), blk(a_l[i % 4], b), ident)
                ins.then_inc(S["at_tr"], 1)

            def at_values(i, t):
                pe.wait_ge(S["at_pt"], 8 * t + i + 1)
                if i == 0:
                    pe.wait_ge(S["at_v"], t + 1)
                    wait(pe, S["at_y"], t)
                hd = i // 4
                rows = slice(64 * hd, 64 * hd + 64)
                for b in range(NB):
                    ins = mm(b7[rows, (i % 4) * P:(i % 4 + 1) * P], a_v[:, b, rows], blk(a_pt[i % 2], b),
                             start=b == 0, stop=b == NB - 1)
                ins.then_inc(S["at_o"], 1)

            def at_sums(t):
                for i in range(2):
                    pe.wait_ge(S["at_sq"], 2 * t + i + 1)
                    wait(pe, S["at_l"], 8 * t)
                    mm((b5, b6)[i][:, :], cc(K_BD), a_sq[:, i, :], start=True, stop=True).then_inc(S["at_ss"], 1)
                filled(pe, at_slab(t, 2) - DN_SHIFT)
                wait(pe, S["at_v"], t)
                for b in range(NB):
                    ins = pe.transpose(blk(b4, b), blk(au[t % 2][:, 2, :], b), ident)
                ins.then_inc(S["at_ss"], 1)

            for n in range(2 * AT_HEADS):
                t, part = n // 4, n % 4
                before = [(2 * (n - 1) + i) for i in range(2)] if n else []
                if t < 3:
                    project(at_slab(t + 1, part), t0=at_slab(t + 1, part) - DN_SHIFT)
                else:
                    project(cv_slab(t, part), t0=cv_slab(t, part) - DN_SHIFT)
                if part == 0:
                    at_sums(t)
                for m in before:
                    at_turn(m % 8, m // 8)
                if t < 3:
                    project(cv_slab(t, part), t0=cv_slab(t, part) - DN_SHIFT)
                for m in before:
                    at_values(m % 8, m // 8)
                if part == 0:
                    pe.wait_ge(S["at_n"], 3 * t + 3)
                    pe.wait_ge(S["at_rs"], 4 * t + 4)
                at_scores(2 * part, t)
                at_scores(2 * part + 1, t)
            at_turn(6, 3)
            at_turn(7, 3)
            at_values(6, 3)
            at_values(7, 3)
            order = (0, 1, 2, 4, 5, 6, 3, 7)
            project(J_O2, src=(yh, yl), t0=J_O2 - DN_SHIFT, order=order,
                    ready=[(S["at_lo"], f - 3) if f >= 4 else (S["cv_lo"], f + 1) for f in order])

            def turn_out(f):
                filled(pe, J_O2 - DN_SHIFT + f)
                wait(pe, S["out_ev"], f - 3)
                for b in range(NB):
                    ins = pe.transpose(blk(psum[2 + f % 4], b), blk(xT[:, f, :], b), ident)
                ins.then_inc(S["out_tr"], 1)

            for f in range(1, KT):
                project(J_O2 + f, src=(yh, yl), t0=J_O2 - DN_SHIFT + f)
                turn_out(f - 1)
            turn_out(KT - 1)
        @block.scalar
        def _(act):
            A = act.activation

            def silu_tables():
                act.preload_act_table_set("silu_and_others")

            def exp_tables():
                act.preload_act_table_set("natural_log_exp_and_others")

            act.dma_start(con[:, 0:K_BD], const_d[:, 0:K_BD]).then_inc(S["ident_in"], 16)
            act.dma_start(par[:, :], par_d).then_inc(S["params_in"], 16)
            act.dma_start(con[:, K_BD:], const_d[:, K_BD:]).then_inc(S["params_in"], 16)
            act.dma_start(oneh[:, :], onehot_d).then_inc(S["onehot_in"], 16)
            exp_tables()

            def norm_squares():
                for f in range(KT):
                    act.wait_ge(S["pro_xT"], f + 1)
                    wait(act, S["nrm_ss"], f - 1)
                    A(sqn[f % 2][:, :], xT[:, f, :], ACT.Square).then_inc(S["nrm_sq"], 1)
                act.wait_ge(S["nrm_ss"], 8)
                A(rsn[:, :], b6[:, :], ACT.Ln, scale=1.0 / D, bias=EPS).then_inc(S["nrm_rs"], 1)
                act.wait_ge(S["nrm_rs"], 1)
                A(rsn[:, :], rsn[:, :], ACT.Exp, scale=-0.5).then_inc(S["nrm_rs"], 1)

            def late_squares(m, j0):
                for f in range(KT):
                    filled(act, j0 + f)
                    for q in range(m):
                        if f >= 3:
                            act.wait_ge(S["lt_add"], 6 * (m - 1) + (f - 3) * m + q + 1)
                        dst = lt_new[m][q][f % 2] if f else lt_sum[m][q]
                        A(dst[:, :], xT[:, f, :], ACT.Square, scale=pc("final", f) if q else 1.0
                          ).then_inc(S["lt_sq"], 1)

            def late_rms(m):
                act.wait_ge(S["lt_ss"], m)
                act.wait_ge(S["nrm_h"], 8 * m)
                A(rsn[:, :], b6[:, :], ACT.Ln, scale=1.0 / D, bias=EPS).then_inc(S["nrm_rs"], 1)
                act.wait_ge(S["nrm_rs"], 2 * m + 1)
                A(rsn[:, :], rsn[:, :], ACT.Exp, scale=-0.5).then_inc(S["nrm_rs"], 1)

            def norm_hi(k, m):
                for f in range(KT):
                    act.wait_ge(S["nrm_h"], 8 * k + f + 1)
                    A(hh[:, f, :], htn[f % 2][:, :], ACT.Copy).then_inc(S["nrm_hi"], 1)

            norm_squares()
            norm_hi(0, 0)
            act.wait_ge(S["lb_step"], 1)
            A(lbt[:, 1, :], lbt[:, 0, :], ACT.Exp).then_inc(S["lb_step"], 1)
            for c, bank in ((0, b7), (1, b5)):
                act.wait_ge(S["wb_mm"], c + 1)
                A(wrow[:, c * T:(c + 1) * T], bank[0:AT_HEADS, :], ACT.Copy).then_inc(S["wb_ev"], 1)
            act.wait_ge(S["wb_ev"], 2)
            act.dma_start(bias_scratch, wrow[:, :].unsqueeze(1).broadcast_to([AT_HEADS, P, W_LINE])
                          ).then_inc(S["wb_out"], 16)
            act.wait_ge(S["row_step"], 2)
            A(r2[:, :], r1[:, :], ACT.Exp).then_inc(S["row_act"], 1)
            A(rac[:, :], pc("alog"), ACT.Exp).then_inc(S["row_act"], 1)

            def copy_out(j0, dst, it=None, k=0, bank=None):
                act.wait_ge(S["slab_used"], lin(j0 + 1, it, k))
                A(dst, acc[j0 % 2][:, :], ACT.Copy).then_inc(acc_free[j0 % 2], 1)

            def hg_exps(l, u):
                n, half = P >> (l - 1), P >> l
                d, e = dd[l % 3], ex[l % 3]
                act.wait_ge(S["hg_d"], u * 8 + (l + 1))
                if l < 3:
                    wait(act, S["hg_z"], u * 14)
                elif l == 3:
                    act.wait_ge(S["hg_x"], u * 2 + 1)
                else:
                    act.wait_ge(S["hg_z"], u * 14 + 2 * (l - 3))
                dv = d[:, :].rearrange("p (c n) -> p c n", n=n)
                ev = e[:, :].rearrange("p (c n) -> p c n", n=n)
                A(ev[:, :, half:], dv[:, :, half:], ACT.Exp).then_inc(S["hg_ex"], 1)
                A(ev[:, :, :half], dv[:, :, :half], ACT.Exp, scale=-1.0).then_inc(S["hg_ex"], 1)

            def hg_prep(u, U, j0, it):
                silu_tables()
                filled(act, j0 + HG_Q, it, 8)
                A(U[:, HG_Q, :], U[:, HG_Q, :], ACT.Silu).then_inc(S["hg_silu"], 1)
                filled(act, j0 + HG_G, it, 8)
                A(U[:, HG_G, :], U[:, HG_G, :], ACT.Silu).then_inc(S["hg_silu"], 1)
                exp_tables()
                filled(act, j0 + HG_F, it, 8)
                wait(act, S["hg_lf"], u)
                wait(act, S["hg_k"], u)
                A(e0[:, :], U[:, HG_F, :], ACT.Exp, scale=-1.0).then_inc(S["hg_e"], 1)
                act.wait_ge(S["hg_e"], u + 1)
                lb = lbc[:, u:u + 1] if isinstance(u, int) else lbc[:, bass.ds(u, 1)]
                A(e1[:, :], e0[:, :], ACT.Ln, scale=lb, bias=1.0).then_inc(S["hg_l"], 1)
                act.wait_ge(S["hg_l"], u * 2 + 1)
                A(e0[:, :], e0[:, :], ACT.Ln, bias=1.0).then_inc(S["hg_l"], 1)
                copy_out(j0 + HG_I, U[:, HG_I, :], it, 8)
                act.wait_ge(S["hg_lf"], u + 1)
                A(e1[:, :], lf[:, :], ACT.Exp).then_inc(S["hg_f"], 1)

            def hg_square(u):
                act.wait_ge(S["hg_o"], u + 1)
                wait(act, S["hg_ss"], u)
                A(sqh[:, :], b6[:, :], ACT.Square).then_inc(S["hg_sq"], 1)

            def hg_rms(u):
                act.wait_ge(S["hg_ss"], u + 1)
                wait(act, S["hg_y"], u * 2)
                A(rsh[:, :], b7[:, :], ACT.Ln, scale=1.0 / P, bias=EPS).then_inc(S["hg_rs"], 1)
                act.wait_ge(S["hg_rs"], u * 2 + 1)
                A(rsh[:, :], rsh[:, :], ACT.Exp, scale=-0.5).then_inc(S["hg_rs"], 1)

            def hg_hi(u):
                act.wait_ge(S["hg_y"], u * 2 + 2)
                A(tile_of(yh, u), yth[:, :], ACT.Copy).then_inc(S["hg_hi"], 1)

            def hg_part(part, u, nxt, it):
                U2, j2 = nxt
                before = not isinstance(u, int) or u > 0
                more = not isinstance(u, int) or u + 1 < HG_HEADS
                if part == 0:
                    act.wait_ge(S["hg_d"], u * 8 + 1)
                    wait(act, S["hg_z"], u * 14)
                    A(ex[0][:, :], dd[0][:, :], ACT.Exp).then_inc(S["hg_ex"], 1)
                    act.wait_ge(S["hg_b"], u + 1)
                    wait(act, S["hg_s"], u * 3)
                    wait(act, S["hg_x"], u * 2)
                    A(eb[:, :], bb[:, :], ACT.Exp).then_inc(S["hg_eb"], 1)
                    if before:
                        hg_square(u - 1)
                    act.wait_ge(S["hg_tr"], u * 2 + 1)
                    wait(act, S["hg_o"], u)
                    A(vt[:, :], b4[:, :], ACT.Copy).then_inc(S["hg_v"], 1)
                    act.wait_ge(S["hg_tr"], u * 2 + 2)
                    A(kt_[:, :], b4[:, 0:3 * P], ACT.Copy).then_inc(S["hg_kt"], 1)
                    hg_exps(1, u)
                elif part == 1:
                    hg_exps(2, u)
                    hg_exps(3, u)
                    if before:
                        hg_rms(u - 1)
                    hg_exps(4, u)
                    if more:
                        copy_out(j2 + HG_Q, U2[:, HG_Q, :], it, 8)
                elif part == 2:
                    if before:
                        hg_hi(u - 1)
                    hg_exps(5, u)
                    hg_exps(6, u)
                    if more:
                        copy_out(j2 + HG_G, U2[:, HG_G, :], it, 8)
                else:
                    hg_exps(7, u)
                    if more:
                        hg_prep(u + 1, U2, j2, it)

            def fill_ml(i, j0, dst):
                if i >= 2:
                    copy_out(j0 + i, dst[:, i, :])

            def fill_mb(i, j0, dst):
                if i >= 4:
                    copy_out(j0 + i, dst[:, i, :])

            def ml_part(part, u):
                p = u % 2
                U, j = unit[p], ml_slab(u)
                if part == 0:
                    silu_tables()
                    for i in range(2):
                        filled(act, j + i)
                        A(U[:, i, :], U[:, i, :], ACT.Silu).then_inc(S["ml_silu"], 1)
                    for i in range(2):
                        filled(act, j + 4 + i)
                        A(U[:, 4 + i, :], U[:, 4 + i, :], ACT.Tanh, scale=0.5).then_inc(S["ml_tanh"], 1)
                    exp_tables()
                    if u:
                        ml_rms(u - 1)
                    else:
                        act.wait_ge(S["hg_lo"], HG_HEADS)
                        act.wait_ge(S["hg_hi"], HG_HEADS)
                        filled(act, J_G0 + 15)
                    act.wait_ge(S["ml_dx"], 4 * u + 4)
                    wait(act, S["ml_pt"], 3 * u)
                    for b in (0, 2, 1):
                        o, n = OFF[b]
                        A(m_e[:, o:o + n], b5[:, (b + 1) * P:T], ACT.Exp, bias=acol[:, b, u:u + 1]
                          ).then_inc(S["ml_ex"], 1)
                    for v in range(2):
                        act.wait_ge(S["ml_tr"], 2 * u + v + 1)
                        wait(act, S["ml_num"], 3 * u)
                        A(m_v[:, :, v * P:(v + 1) * P], (b6, b7)[v][:, :].rearrange("p (b d) -> p b d", b=NB),
                          ACT.Copy).then_inc(S["ml_v"], 1)
                    A(m_e[:, 0:T], m_e[:, 0:T], ACT.Exp).then_inc(S["ml_ex"], 1)
                elif part == 2:
                    act.wait_ge(S["ml_nm2"], u + 1)
                    wait(act, S["ml_dn"], 3 * u)
                    A(m_em[:, :], b2[:, :], ACT.Exp).then_inc(S["ml_em"], 1)
                elif part == 3:
                    for v in range(2):
                        act.wait_ge(S["ml_h"], 2 * u + v + 1)
                        wait(act, S["ml_ss"], u)
                        A(m_sq[:, v, :], m_h[:, v, :], ACT.Square).then_inc(S["ml_sq"], 1)

            def ml_rms(u):
                act.wait_ge(S["ml_ss"], u + 1)
                wait(act, S["ml_y"], 4 * u)
                A(m_rs[:, :], b3[:, :], ACT.Ln, scale=1.0 / 256, bias=EPS).then_inc(S["ml_rs"], 1)
                act.wait_ge(S["ml_rs"], 2 * u + 1)
                A(m_rs[:, :], m_rs[:, :], ACT.Exp, scale=-0.5).then_inc(S["ml_rs"], 1)

            def ml_hi(u):
                for v in range(2):
                    act.wait_ge(S["ml_y"], 4 * u + 2 * v + 2)
                    if u == 0:
                        act.wait_ge(S["slab_used"], J_ML1)
                    A(yh[:, 2 * u + v, :], m_h[:, v, :], ACT.Copy, scale=0.5).then_inc(S["ml_hi"], 1)

            def mb_head(g, h):
                n = 4 * g + h
                act.wait_ge(S["mb_dx"], 4 * n + 4)
                wait(act, S["mb_pt"], 3 * n)
                if n == 0:
                    act.wait_ge(S["ml_lo"], 2 * ML_HEADS)
                    act.wait_ge(S["g_acc"], KT)
                for k, (b, i) in enumerate(((0, 1), (0, 2), (0, 3), (2, 3), (1, 2), (1, 3))):
                    o = OFF[b][0] + (i - b - 1) * P
                    A(s_e[:, o:o + P], blk(b5, i), ACT.Exp, bias=dend[:, k, n:n + 1]).then_inc(S["mb_ex"], 1)
                A(s_e[:, 0:T], s_e[:, 0:T], ACT.Exp).then_inc(S["mb_ex"], 1)

            def mb_silus(g, tiles):
                for i in tiles:
                    filled(act, mb_slab(g) + i)
                    A(unit[g % 2][:, i, :], unit[g % 2][:, i, :], ACT.Silu).then_inc(S["mb_silu"], 1)

            def mb_tail(g):
                for v in range(2):
                    act.wait_ge(S["mb_y"], 6 * g + 2 * v + 2)
                    wait(act, S["mb_ss"], g)
                    A(s_sq[:, v, :], s_y[:, v, :], ACT.Square).then_inc(S["mb_sq"], 1)

            def mb_rms(g):
                act.wait_ge(S["mb_ss"], g + 1)
                wait(act, S["mb_y"], 6 * g)
                A(s_rs[:, :], b5[:, :], ACT.Ln, scale=1.0 / 256, bias=EPS).then_inc(S["mb_rs"], 1)
                act.wait_ge(S["mb_rs"], 2 * g + 1)
                A(s_rs[:, :], s_rs[:, :], ACT.Exp, scale=-0.5).then_inc(S["mb_rs"], 1)

            def mb_hi(g):
                for v in range(2):
                    act.wait_ge(S["mb_y"], 6 * g + 4 + v + 1)
                    if g == 0:
                        act.wait_ge(S["slab_used"], J_MB1)
                    A(yh[:, 2 * g + v, :], s_y[:, v, :], ACT.Copy).then_inc(S["mb_hi"], 1)

            for i in (HG_Q, HG_G):
                copy_out(J_HG + i, unit[0][:, i, :])
            hg_prep(0, unit[0], J_HG, None)
            act.wait_ge(S["row_mm"], 1)
            A(ra[:, :], b4[:, :], ACT.Copy).then_inc(S["row_ev"], 1)
            act.wait_ge(S["wb_out"], 16)

            def hg_pair(it):
                for p in range(2):
                    for part in range(4):
                        hg_part(part, lin(p, it, 2), (unit[1 - p], J_HG + 4 + 4 * p), it)

            hg_pair(None)
            with act.Fori(1, HG_HEADS // 2 - 1) as it:
                hg_pair(it)
            for u in (HG_HEADS - 2, HG_HEADS - 1):
                for part in range(4):
                    hg_part(part, u, (unit[1 - u % 2], J_HG + 4 * (u + 1)), None)
                    if u == HG_HEADS - 1:
                        for i in tiles_before(part, 6):
                            if i == HG_G:
                                act.wait_ge(S["hg_y"], 2 * u)
                            fill_ml(i, J_ML0, unit[0])
            hg_square(HG_HEADS - 1)
            hg_rms(HG_HEADS - 1)
            hg_hi(HG_HEADS - 1)

            def gates(b, j0):
                silu_tables()
                if b == 0:
                    act.wait_ge(S["hg_lo"], HG_HEADS)
                else:
                    act.wait_ge(S["ml_lo"], 2 * ML_HEADS)
                with act.Fori(0, KT // 2) as it:
                    for f in range(2):
                        act.wait_ge(S["slab_used"], it * 4 + (j0 + 2 * f + 1))
                        filled(act, j0 + 2 * f - 3, it, 4)
                        A(tg[f][:, :], acc[j0 % 2][:, :], ACT.Tanh, scale=0.5).then_inc(acc_free[j0 % 2], 1)

            gates(0, J_G0)
            for u in range(ML_HEADS):
                last = u + 1 == ML_HEADS
                for part in range(4):
                    ml_part(part, u)
                    if part == 0 and u:
                        ml_hi(u - 1)
                    for i in tiles_before(part, 6):
                        if i == 4:
                            wait(act, S["ml_lo"], 2 * u)
                        if last and i == 5:
                            ml_rms(u)
                        if last:
                            fill_mb(i, J_MB0, unit[0])
                        else:
                            fill_ml(i, ml_slab(u + 1), unit[1 - u % 2])
            ml_hi(ML_HEADS - 1)
            gates(1, J_G1)
            silu_tables()
            mb_silus(0, range(6))
            exp_tables()
            for g in range(MB_GROUPS):
                last = g + 1 == MB_GROUPS
                nxt = J_G2 if last else mb_slab(g + 1)
                for h in range(4):
                    mb_head(g, h)
                    if last:
                        copy_out(nxt + h, gbuf[:, h, :])
                if not last:
                    silu_tables()
                    mb_silus(g + 1, range(4))
                for i in (4, 5):
                    wait(act, S["mb_y"], 6 * g - 2)
                    copy_out(nxt + i, gbuf[:, i, :] if last else unit[1 - g % 2][:, i, :])
                    if i == 4:
                        mb_tail(g)
                if not last:
                    mb_silus(g + 1, (4, 5))
                    exp_tables()
                mb_rms(g)
                if last:
                    for i in (6, 7):
                        copy_out(nxt + i, gbuf[:, i, :])
                mb_hi(g)
            silu_tables()
            for f in range(KT):
                filled(act, J_G2 + f)
                A(gbuf[:, f, :], gbuf[:, f, :], ACT.Tanh, scale=0.5).then_inc(S["g_tanh"], 1)
            for f in range(KT):
                act.wait_ge(S["g_acc"], KT + f + 1)
                A(hh[:, f, :], mixed[:, f, :], ACT.Copy, scale=0.5).then_inc(S["o_hi"], 1)

            exp_tables()
            late_squares(1, J_O)
            late_rms(1)
            norm_hi(1, 1)
            silu_tables()
            with act.Fori(0, NF // 2) as it:
                for p in range(2):
                    j = it * 2 + p
                    act.wait_ge(S["slab_used"], it * 4 + (J_UP + 2 * p + 1))
                    A(f_g[p][:, :], acc[J_UP % 2][:, :], ACT.Identity, scale=pc("fcw", it * 6 + (3 * p + 2)),
                      bias=pc("fcb", j)).then_inc(S["up_c"], 1)
                    act.wait_ge(S["slab_used"], it * 4 + (J_UP + 2 * p + 2))
                    A(f_v[p][:, :], acc[1 - J_UP % 2][:, :], ACT.Identity,
                      scale=pc("fcw", it * 6 + (3 * NF + 3 * p + 2)), bias=pc("fcb", j + NF)
                      ).then_inc(S["up_c"], 1)
                    filled(act, J_UP + 2 * p, it, 4)
                    A(f_s[p][:, :], f_g[p][:, :], ACT.Silu).then_inc(S["up_sg"], 1)
                    act.wait_ge(S["up_a"], j + 1)
                    A(tile_of(fh, j), f_s[p][:, :], ACT.Copy).then_inc(S["up_hi"], 1)
            exp_tables()
            late_squares(2, J_DN)
            skew = bass.AP(tensor=bias_scratch.tensor, offset=P - 1,
                           ap=[[W_LINE - 1, P], [P * W_LINE, AT_HEADS], [1, W_BIAS]])
            act.dma_start(wb[:, :, :], skew).then_inc(S["wb_in"], 16)
            late_rms(2)
            act.wait_ge(S["lt_step"], 2)
            A(sqn[0][:, :], sqn[1][:, :], ACT.Ln, scale=1.0 / D, bias=EPS).then_inc(S["nrm_rs"], 1)
            act.wait_ge(S["nrm_rs"], 7)
            A(sqn[0][:, :], sqn[0][:, :], ACT.Exp, scale=-0.5).then_inc(S["nrm_rs"], 1)
            norm_hi(2, 2)
            silu_tables()
            def leave(j, dst):
                act.wait_ge(S["slab_used"], j + 1)
                A(dst, acc[j % 2][:, :], ACT.Copy).then_inc(acc_free[j % 2], 1)

            def at_squares(t):
                for i in range(2):
                    filled(act, at_slab(t, i) - DN_SHIFT)
                    wait(act, S["at_ss"], 3 * t)
                    A(a_sq[:, i, :], au[t % 2][:, i, :], ACT.Square).then_inc(S["at_sq"], 1)

            def at_copy(n):
                act.wait_ge(S["at_tr"], n + 1)
                wait(act, S["at_o"], n - 1)
                A(a_pt[n % 2][:, :], (b2, b3)[n % 2][:, :], ACT.Copy).then_inc(S["at_pt"], 1)

            def at_hi(t):
                act.wait_ge(S["at_y"], t + 1)
                A(yh[:, 4 + t, :], a_y[:, :], ACT.Copy).then_inc(S["at_hi"], 1)

            def cv_silu(t):
                filled(act, cv_slab(t, 3) - DN_SHIFT)
                A(c_z[:, :], c_z[:, :], ACT.Silu).then_inc(S["cv_z"], 1)

            def cv_hi(t):
                act.wait_ge(S["cv_y"], 5 * t + 5)
                A(yh[:, t, :], c_y[:, :], ACT.Copy).then_inc(S["cv_hi"], 1)

            for i in range(4):
                leave(J_AT + i, au[0][:, i, :])
            at_squares(0)
            for n in range(2 * AT_HEADS):
                t, part = n // 4, n % 4
                if part == 0:
                    filled(act, at_slab(t, 3) - DN_SHIFT)
                    A(au[t % 2][:, 3, :], au[t % 2][:, 3, :], ACT.Silu).then_inc(S["at_silu"], 1)
                    if t:
                        cv_silu(t - 1)
                    exp_tables()
                if t < 3:
                    if part == 3:
                        wait(act, S["at_y"], t)
                    leave(at_slab(t + 1, part), au[1 - t % 2][:, part, :])
                if part == 0:
                    for i in range(2):
                        act.wait_ge(S["at_ss"], 3 * t + i + 1)
                        wait(act, S["at_n"], 3 * t)
                        A(a_rs[:, i, :], (b5, b6)[i][:, :], ACT.Ln, scale=1.0 / AT_DH, bias=EPS
                          ).then_inc(S["at_rs"], 1)
                        act.wait_ge(S["at_rs"], 4 * t + 2 * i + 1)
                        A(a_rs[:, i, :], a_rs[:, i, :], ACT.Exp, scale=-0.5).then_inc(S["at_rs"], 1)
                if n:
                    at_copy(2 * n - 2)
                    at_copy(2 * n - 1)
                if part == 0:
                    act.wait_ge(S["at_ss"], 3 * t + 3)
                    wait(act, S["at_o"], 8 * t)
                    A(a_v[:, :, :].rearrange("p b d -> p (b d)"), b4[:, :], ACT.Copy).then_inc(S["at_v"], 1)
                if part != 2:
                    wait(act, S["cv_y"], 5 * t - (2, 1, 0, 0)[part])
                    leave(cv_slab(t, part), (c_u, c_b, None, c_z)[part][:, :])
                if part == 1 and t:
                    at_hi(t - 1)
                    cv_hi(t - 1)
                for i in (2 * part, 2 * part + 1):
                    act.wait_ge(S["at_mx"], 8 * t + i + 1)
                    A(a_l[i % 4][:, :], a_l[i % 4][:, :], ACT.Exp, bias=a_st[:, i, 0:1],
                      accum_out=a_st[:, i, 1:2]).then_inc(S["at_ex"], 1)
                if part == 3:
                    silu_tables()
                    if t < 3:
                        at_squares(t + 1)
            cv_silu(3)
            at_copy(30)
            at_copy(31)
            cv_hi(3)
            at_hi(3)
            for f in range(KT):
                act.wait_ge(S["out_tr"], f + 1)
                if f >= 2:
                    act.wait_ge(S[f"out_dma{f % 2}"], 16 * (f // 2))
                A(os_[f % 2][:, :], psum[2 + f % 4][:, :], ACT.Copy).then_inc(S["out_ev"], 1)

        @block.vector
        def _(dve):
            TT, TS, STT = dve.tensor_tensor, dve.tensor_scalar, dve.scalar_tensor_tensor

            def norm_scale(k, gain, rs):
                for f in range(KT):
                    if f >= 2:
                        dve.wait_ge(S["nrm_hi"], 8 * k + f - 1)
                        dve.wait_ge(S["nrm_lo"], 8 * k + f - 1)
                    STT(htn[f % 2][:, :], xT[:, f, :], gain(f), rs[:, :], ALU.mult, ALU.mult
                        ).then_inc(S["nrm_h"], 1)
                    if f:
                        lo(k, k, f - 1)
                lo(k, k, KT - 1)

            def lo(k, m, f):
                dve.wait_ge(S["nrm_h"], 8 * k + f + 1)
                dve.wait_ge(S["nrm_hi"], 8 * m + f + 1)
                TT(hl[:, f, :], htn[f % 2][:, :], hh[:, f, :].bitcast(F32), ALU.subtract).then_inc(S["nrm_lo"], 1)

            for f in range(KT):
                dve.wait_ge(S["pro_tr"], f + 1)
                dve.tensor_copy(xT[:, f, :], psum[2 + f % 4][:, :]).then_inc(S["pro_xT"], 1)
            dve.wait_ge(S["pro_xT"], 8)
            dve.wait_ge(S["zero_set"], 1)
            dve.wait_ge(S["params_in"], 32)
            lg = par[:, PAR["lb"]:PAR["lb"] + 8]
            TT(lbt[:, 0, :], lg, lg, ALU.subtract).then_inc(S["lb_step"], 1)
            dve.wait_ge(S["nrm_rs"], 2)
            norm_scale(0, lambda f: pc("norm1", f), rsn)
            TT(gg[:, :], par[:, PAR["final"]:PAR["final"] + KT], par[:, PAR["normw2"]:PAR["normw2"] + KT], ALU.mult
               ).then_inc(S["x2_done"], 1)
            dve.wait_ge(S["lb_step"], 2)
            dve.reciprocal(lbt[:, 2, :], lbt[:, 1, :]).then_inc(S["lb_step"], 1)
            dve.wait_ge(S["lb_step"], 3)
            TT(lbt[:, 0, :], lbt[:, 1, :], lbt[:, 2, :], ALU.mult).then_inc(S["lb_step"], 1)
            dve.wait_ge(S["lb_step"], 4)
            TT(lbc[:, :], lbt[:, 0, :], lbt[:, 0, :], ALU.subtract).then_inc(S["lb_step"], 1)

            step = [0]

            def row(ins):
                step[0] += 1
                ins.then_inc(S["row_step"], 1)
                dve.wait_ge(S["row_step"], step[0])

            def clamp_f(j0, dst, it=None):
                dve.wait_ge(S["slab_used"], lin(j0 + 1, it, 8))
                TS(dst, acc[j0 % 2][:, :], -40.0, None, ALU.max).then_inc(acc_free[j0 % 2], 1)

            def hg_prep(u):
                dve.wait_ge(S["hg_l"], u * 2 + 2)
                wait(dve, S["hg_f"], u)
                wait(dve, S["hg_b"], u)
                TT(lf[:, :], e1[:, :], e0[:, :], ALU.subtract).then_inc(S["hg_lf"], 1)
                dve.wait_ge(S["hg_lf"], u + 1)
                wait(dve, S["hg_eb"], u)
                wait(dve, S["hg_d"], u * 8)
                dve.tensor_tensor_scan(bb[:, :], cc(K_HGMASK, T), lf[:, :], 0.0, ALU.mult, ALU.add
                                       ).then_inc(S["hg_b"], 1)
                dve.wait_ge(S["hg_f"], u + 1)
                wait(dve, S["hg_lv"], u * 8)
                wait(dve, S["hg_z"], u * 14)
                TS(kk[:, :], e1[:, :], -1.0, 1.0, ALU.mult, ALU.add).then_inc(S["hg_k"], 1)

            sign = cc(K_SIGN, 1)
            dve.wait_ge(S["slab_used"], 1)
            STT(rz[:, :], acc[0][:, :], pc("rowb"), sign.broadcast_to([P, T]), ALU.add, ALU.mult
                ).then_inc(acc_free[0], 1)
            dve.wait_ge(acc_free[0], 1)
            row(TS(r3[:, :], rz[:, :], 0.0, None, ALU.max))
            row(STT(r1[:, :], rz[:, :], -1.0, rz[:, :], ALU.mult, ALU.min))
            dve.wait_ge(S["row_act"], 2)
            row(TS(r4[:, :], r2[:, :], 2.0, None, ALU.add))
            row(dve.reciprocal(r5[:, :], r4[:, :]))
            clamp_f(J_HG + HG_F, unit[0][:, HG_F, :])
            row(TT(r4[:, :], r2[:, :], r5[:, :], ALU.mult))
            row(TT(r2[:, :], r4[:, :], r4[:, :], ALU.mult))
            row(TS(r1[:, :], r2[:, :], 1.0 / 17, None, ALU.mult))
            for k in (15, 13, 11, 9, 7, 5, 3):
                row(STT(r1[:, :], r1[:, :], 1.0 / k, r2[:, :], ALU.add, ALU.mult))
            row(STT(r1[:, :], r1[:, :], 1.0, r4[:, :], ALU.add, ALU.mult))
            row(STT(r5[:, :], r1[:, :], 2.0, r3[:, :], ALU.mult, ALU.add))
            row(TS(rac[:, :], rac[:, :], -1.0, None, ALU.mult))
            row(TS(r4[:, :], r5[:, :], rac[:, 0:1], None, ALU.mult))
            dve.tensor_tensor_scan(cum[:, :], cc(K_RMASK, T), r4[:, :], 0.0, ALU.mult, ALU.add
                                   ).then_inc(S["row_a"], 1)
            dve.wait_ge(S["row_a"], 1)
            for b in range(NB):
                TS(rdg[:, b, :], ident[:, 0:MB_HEADS], cum[:, b * P + P - 1:b * P + P], None, ALU.mult
                   ).then_inc(S["row_done"], 1)
            hg_prep(0)
            dve.wait_ge(S["row_ev"], 1)
            i_rows = slice(ROW_I, ROW_I + 32)
            dve.tensor_tensor_scan(r1[i_rows, :], ra[i_rows, :], ra[i_rows, :], 0.0, ALU.max, ALU.max
                                   ).then_inc(S["rnm_done"], 1)
            TS(r3[:, :], cum[:, :], sign, None, ALU.mult).then_inc(S["rnm_done"], 1)
            dve.wait_ge(S["rnm_done"], 2)
            TS(r3[i_rows, :], r1[i_rows, :], -1.0, None, ALU.mult).then_inc(S["rnm_done"], 1)
            dve.tensor_copy(selr[:, 0:P], ident).then_inc(S["rnm_done"], 1)
            dve.tensor_copy(selr[:, P:2 * P], cc(K_SEL2)).then_inc(S["rnm_done"], 1)
            dve.wait_ge(S["rnm_done"], 3)
            dve.tensor_copy(csh[:, :], r3[:, :]).then_inc(S["rnm_done"], 1)
            dve.wait_ge(S["rnm_done"], 6)
            TT(csl[:, :], r3[:, :], csh[:, :].bitcast(F32), ALU.subtract).then_inc(S["rnm_done"], 1)
            def cols(bank, n, c=0):
                return bank[:, :].rearrange("p (b r) -> p b r", b=NB)[:, :, c:c + n]

            dve.wait_ge(S["row_mm"], 2)
            TS(ncc[:, :, :], cols(b6, MB_HEADS), -1.0, None, ALU.mult).then_inc(S["row_done"], 1)
            dve.tensor_copy(dtc[:, :, :], cols(b7, MB_HEADS)).then_inc(S["row_done"], 1)
            dve.wait_ge(S["row_mm"], 3)
            dve.tensor_copy(totb[:, :, :], b5[:, 0:NB * MB_HEADS].rearrange("p (b h) -> p b h", b=NB)
                            ).then_inc(S["row_done"], 1)
            dve.wait_ge(S["row_mm"], 4)
            dve.tensor_copy(acol[:, :, :], cols(b3, ML_HEADS, ROW_I)).then_inc(S["row_done"], 1)
            dve.wait_ge(S["row_done"], 8)
            TT(dend[:, 0, :], totb[:, 0, :], ncc[:, 0, :], ALU.add).then_inc(S["row_step"], 1)
            TT(dend[:, 3, :], totb[:, 2, :], ncc[:, 2, :], ALU.add).then_inc(S["row_step"], 1)
            TT(dend[:, 4, :], totb[:, 1, :], ncc[:, 1, :], ALU.add).then_inc(S["row_step"], 1)
            dve.wait_ge(S["row_step"], step[0] + 3)
            TT(dend[:, 1, :], dend[:, 0, :], totb[:, 1, :], ALU.add).then_inc(S["row_done"], 1)
            TT(dend[:, 5, :], dend[:, 4, :], totb[:, 2, :], ALU.add).then_inc(S["row_done"], 1)
            dve.wait_ge(S["row_done"], 10)
            TT(dend[:, 2, :], dend[:, 1, :], totb[:, 2, :], ALU.add).then_inc(S["row_done"], 1)
            dve.wait_ge(S["row_done"], 11)

            convs = [0]

            def conv4(j0, dst, w, b, i):
                bank = acc[j0 % 2]
                dve.wait_ge(S["slab_used"], j0 + 1)
                TS(dst, bank[:, :], pc(w, 4 * i + 3), pc(b, i), ALU.mult, ALU.add).then_inc(S["conv_step"], 1)
                for k in (2, 1, 0):
                    convs[0] += 1
                    dve.wait_ge(S["conv_step"], convs[0])
                    s = 3 - k
                    ins = STT(dst[:, s:], bank[:, 0:T - s], pc(w, 4 * i + k), dst[:, s:], ALU.mult, ALU.add)
                    ins.then_inc(S["conv_step"] if k else acc_free[j0 % 2], 1)

            def hg_diff(l, u):
                dve.wait_ge(S["hg_b"], u + 1)
                if l == 0:
                    wait(dve, S["hg_ex"], u * 15)
                    v = bb[:, :].rearrange("p (c n) -> p c n", n=P)
                    o = dd[0][:, :].rearrange("p (c n) -> p c n", n=P)
                    TT(o, v[:, :, P - 1:P].broadcast_to([P, NB, P]), v, ALU.subtract).then_inc(S["hg_d"], 1)
                    return
                n, half = P >> (l - 1), P >> l
                wait(dve, S["hg_ex"], u * 15 if l < 3 else u * 15 + (1 + 2 * (l - 3)))
                v = bb[:, :].rearrange("p (c n) -> p c n", n=n)
                o = dd[l % 3][:, :].rearrange("p (c n) -> p c n", n=n)
                TT(o, v, v[:, :, half - 1:half].broadcast_to([P, T // n, n]), ALU.subtract).then_inc(S["hg_d"], 1)

            def hg_scale(l, u, p):
                n, half = P >> (l - 1), P >> l
                dve.wait_ge(S["hg_ex"], u * 15 + (1 + 2 * l))
                wait(dve, S["hg_lv"], u * 8 + (l - 2 if l > 3 else 0))
                def v(ap):
                    return ap.rearrange("p (c n) -> p c n", n=n)
                q, k, e, z = v(unit[p][:, HG_Q, :]), v(kk[:, :]), v(ex[l % 3][:, :]), v(zz[l % 3][:, :])
                TT(z[:, :, half:], q[:, :, half:], e[:, :, half:], ALU.mult).then_inc(S["hg_z"], 1)
                TT(z[:, :, :half], k[:, :, :half], e[:, :, :half], ALU.mult).then_inc(S["hg_z"], 1)

            def hg_merge(l, u):
                dve.wait_ge(S["hg_lv"], u * 8 + (l + 1))
                dve.wait_ge(S["hg_at"], u * 8 + l)
                dve.tensor_copy(tick[:, :], zero[:, :])
                n, half = P >> (l - 1), P >> l
                k = K_LMASK + (l - 1) * P // 2
                mask = con[:, k:k + P // 2].bitcast(U32).rearrange("p (c h) -> p c h", h=half)
                dve.copy_predicated(
                    at_[:, :].rearrange("p (b c n) -> p b c n", b=NB, n=n)[:, :, :, half:],
                    mask.unsqueeze(1).broadcast_to([P, NB, P // n, half]),
                    (b2, b3)[l % 2][:, 0:T // 2].rearrange("p (b c h) -> p b c h", b=NB, h=half)
                    ).then_inc(S["hg_at"], 1)

            def hg_y(u, U):
                dve.wait_ge(S["hg_rs"], u * 2 + 2)
                wait(dve, S["hg_hi"], u)
                wait(dve, S["hg_lo"], u)
                STT(yth[:, :], b6[:, :], pc("hgg"), rsh[:, :], ALU.mult, ALU.mult).then_inc(S["hg_y"], 1)
                dve.wait_ge(S["hg_y"], u * 2 + 1)
                dve.wait_ge(S["hg_silu"], u * 2 + 2)
                TT(yth[:, :], yth[:, :], U[:, HG_G, :], ALU.mult).then_inc(S["hg_y"], 1)

            def hg_lo(u):
                dve.wait_ge(S["hg_hi"], u + 1)
                dve.wait_ge(S["hg_y"], u * 2 + 2)
                TT(tile_of(yl, u), yth[:, :], tile_of(yh, u).bitcast(F32), ALU.subtract).then_inc(S["hg_lo"], 1)

            def hg_part(part, u, p, it):
                U = unit[p]
                before = not isinstance(u, int) or u > 0
                more = not isinstance(u, int) or u + 1 < HG_HEADS
                if part == 0:
                    hg_diff(0, u)
                    hg_diff(1, u)
                    dve.wait_ge(S["hg_k"], u + 1)
                    dve.wait_ge(S["hg_ex"], u * 15 + 1)
                    wait(dve, S["hg_tr"], u * 2)
                    TT(k1[:, :], kk[:, :], ex[0][:, :], ALU.mult).then_inc(S["hg_x"], 1)
                    dve.wait_ge(S["hg_eb"], u + 1)
                    dve.wait_ge(S["hg_silu"], u * 2 + 1)
                    wait(dve, S["hg_o"], u)
                    TT(q1[:, :], U[:, HG_Q, :], eb[:, :], ALU.mult).then_inc(S["hg_x"], 1)
                    dve.wait_ge(S["hg_lv"], u * 8 + 1)
                    TT(at_[:, :].rearrange("p (b t) -> p b t", b=NB), b2[:, :].rearrange("p (b t) -> p b t", b=NB),
                       ident.unsqueeze(1).broadcast_to([P, NB, P]), ALU.mult).then_inc(S["hg_at"], 1)
                    hg_scale(1, u, p)
                    hg_diff(2, u)
                    if more:
                        clamp_f(J_HG + 4 * ((u if it is None else p) + 1) + HG_F, unit[1 - p][:, HG_F, :], it)
                elif part == 1:
                    hg_diff(3, u)
                    hg_scale(2, u, p)
                    hg_scale(3, u, p)
                    hg_diff(4, u)
                    hg_merge(1, u)
                    dve.wait_ge(S["hg_stp"], u + 1)
                    wait(dve, S["hg_o"], u)
                    dve.tensor_copy(blk(st_, 0), blk(b5, 0)).then_inc(S["hg_s"], 1)
                    for b in (1, 2):
                        dve.wait_ge(S["hg_s"], u * 3 + b)
                        STT(blk(st_, b), blk(st_, b - 1), eb[:, b * P + P - 1:b * P + P], blk(b5, b),
                            ALU.mult, ALU.add).then_inc(S["hg_s"], 1)
                    hg_merge(2, u)
                    if before:
                        hg_y(u - 1, unit[1 - p])
                elif part == 2:
                    hg_diff(5, u)
                    hg_scale(4, u, p)
                    hg_scale(5, u, p)
                    if before:
                        hg_lo(u - 1)
                    hg_diff(6, u)
                    hg_merge(3, u)
                    hg_scale(6, u, p)
                    hg_merge(4, u)
                    hg_diff(7, u)
                    hg_merge(5, u)
                else:
                    hg_scale(7, u, p)
                    hg_merge(6, u)
                    hg_merge(7, u)
                    if more:
                        hg_prep(u + 1)

            def hg_pair(it):
                for p in range(2):
                    for part in range(4):
                        hg_part(part, lin(p, it, 2), p, it)

            hg_pair(None)
            with dve.Fori(1, HG_HEADS // 2 - 1) as it:
                hg_pair(it)
            for u in (HG_HEADS - 2, HG_HEADS - 1):
                for part in range(4):
                    if u == HG_HEADS - 1 and part == 1:
                        conv4(J_ML0 + 1, unit[0][:, 1, :], "mlcw", "mlcb", 4)
                    hg_part(part, u, u % 2, None)
                    if u == HG_HEADS - 1 and part == 0:
                        conv4(J_ML0, unit[0][:, 0, :], "mlcw", "mlcb", 0)
            hg_y(HG_HEADS - 1, unit[(HG_HEADS - 1) % 2])
            hg_lo(HG_HEADS - 1)

            def gates(b, j0):
                with dve.Fori(0, KT // 2) as it:
                    for f in range(2):
                        dve.wait_ge(S["slab_used"], it * 4 + (j0 + 2 * f + 2))
                        filled(dve, j0 + 2 * f, it, 4)
                        fo = it * 2 + f
                        dst = tile_of(mixed, fo) if b == 0 else tm[:, :]
                        if b:
                            wait(dve, S["g_acc"], it * 2 + (KT * (b - 1) + f))
                        STT(dst, tg[f][:, :], 1.0, acc[1 - j0 % 2][:, :], ALU.add, ALU.mult
                            ).then_inc(acc_free[1 - j0 % 2], 1)
                        if b:
                            filled(dve, j0 + 2 * f + 1, it, 4)
                            TT(tile_of(mixed, fo), tile_of(mixed, fo), tm[:, :], ALU.add).then_inc(S["g_acc"], 1)

            def ml_part(part, u):
                p = u % 2
                U = unit[p]
                if part == 0:
                    dve.wait_ge(S["ml_nm"], u + 1)
                    wait(dve, S["ml_pt"], 3 * u)
                    for b in range(NB):
                        STT(m_e[:, b * P:(b + 1) * P], blk(b5, b), acol[:, b, u:u + 1], clampm, ALU.add, ALU.min
                            ).then_inc(S["ml_dx"], 1)
                elif part == 1:
                    dve.wait_ge(S["ml_ex"], 4 * u + 4)
                    wait(dve, S["ml_num"], 3 * u)
                    for i, (bank, a, n) in enumerate(((b2, 0, 512), (b3, 512, 512), (b4, 1024, 256))):
                        dve.wait_ge(S["ml_qk"], 3 * u + i + 1)
                        STT(m_p[:, a:a + n], bank[:, 0:n], P ** -0.5, m_e[:, a:a + n], ALU.mult, ALU.mult
                            ).then_inc(S["ml_pt"], 1)
                    dve.wait_ge(S["ml_pt"], 3 * u + 3)
                    dve.tensor_copy(m_ps[:, 0:P], m_p[:, 0:P]).then_inc(S["ml_ps"], 1)
                    TT(m_ps[:, P:T], m_p[:, P:T], m_p[:, 512:896], ALU.add).then_inc(S["ml_ps"], 1)
                    dve.wait_ge(S["ml_ps"], 4 * u + 2)
                    TT(m_ps[:, 2 * P:T], m_ps[:, 2 * P:T], m_p[:, 1024:1280], ALU.add).then_inc(S["ml_ps"], 1)
                    dve.wait_ge(S["ml_ps"], 4 * u + 3)
                    TT(m_ps[:, 3 * P:T], m_ps[:, 3 * P:T], m_p[:, 896:1024], ALU.add).then_inc(S["ml_ps"], 1)
                elif part == 2:
                    dve.wait_ge(S["ml_num"], 3 * u + 3)
                    dve.wait_ge(S["ml_em"], u + 1)
                    wait(dve, S["ml_dn"], 3 * u)
                    STT(m_dn[:, :], b5[:, :], -1.0, m_em[:, :], ALU.mult, ALU.max).then_inc(S["ml_dn"], 1)
                    dve.wait_ge(S["ml_dn"], 3 * u + 1)
                    TT(m_dn[:, :], m_dn[:, :], b5[:, :], ALU.max).then_inc(S["ml_dn"], 1)
                    dve.wait_ge(S["ml_dn"], 3 * u + 2)
                    wait(dve, S["ml_h"], 2 * u)
                    dve.reciprocal(m_rd[:, :], m_dn[:, :]).then_inc(S["ml_dn"], 1)
                    dve.wait_ge(S["ml_dn"], 3 * u + 3)
                    wait(dve, S["ml_hi"], 2 * u)
                    wait(dve, S["ml_lo"], 2 * u)
                    for v in range(2):
                        TT(m_h[:, v, :], (b6, b7)[v][:, :], m_rd[:, :], ALU.mult).then_inc(S["ml_h"], 1)

            def ml_end(u):
                U = unit[u % 2]
                dve.wait_ge(S["ml_rs"], 2 * u + 2)
                dve.wait_ge(S["ml_sq"], 2 * u + 2)
                dve.wait_ge(S["ml_tanh"], 2 * u + 2)
                for v in range(2):
                    STT(m_h[:, v, :], m_h[:, v, :], pc("mlg", v), m_rs[:, :], ALU.mult, ALU.mult
                        ).then_inc(S["ml_y"], 1)
                    dve.wait_ge(S["ml_y"], 4 * u + 2 * v + 1)
                    STT(m_h[:, v, :], U[:, 4 + v, :], 1.0, m_h[:, v, :], ALU.add, ALU.mult
                        ).then_inc(S["ml_y"], 1)
                for v in range(2):
                    dve.wait_ge(S["ml_hi"], 2 * u + v + 1)
                    dve.wait_ge(S["ml_y"], 4 * u + 4)
                    STT(yl[:, 2 * u + v, :], m_h[:, v, :], 0.5, yh[:, 2 * u + v, :].bitcast(F32),
                        ALU.mult, ALU.subtract).then_inc(S["ml_lo"], 1)

            def mb_head(g, h):
                n = 4 * g + h
                dve.wait_ge(S["mb_nm"], n + 1)
                wait(dve, S["mb_pt"], 3 * n)
                for b in range(NB):
                    STT(s_e[:, b * P:(b + 1) * P], blk(b5, b), ncc[:, b, n:n + 1], clampm, ALU.add, ALU.min
                        ).then_inc(S["mb_dx"], 1)

            def mb_weights(g, h):
                n = 4 * g + h
                dve.wait_ge(S["mb_ex"], 7 * n + 7)
                wait(dve, S["mb_ym"], n - 1)
                if h == 0:
                    dve.wait_ge(S["mb_cb"], g + 1)
                for bank, a, m in ((b2, 0, 512), (b3, 512, 512), (b4, 1024, 256)):
                    TT(s_p[n % 2][:, a:a + m], s_e[:, a:a + m], bank[:, 0:m], ALU.mult).then_inc(S["mb_pt"], 1)

            def mb_xdt(g):
                wait(dve, S["mb_ym"], 4 * g)
                for i in range(2):
                    dve.wait_ge(S["mb_tr"], 2 * g + i + 1)
                    TT(s_x[:, 2 * i:2 * i + 2], (b6, b7)[i][:, :].rearrange("p (b h d) -> p b h d", b=2, h=4),
                       dtc[:, 2 * i:2 * i + 2, 4 * g:4 * g + 4].unsqueeze(3).broadcast_to([P, 2, 4, 64]), ALU.mult
                       ).then_inc(S["mb_xd"], 1)

            def mb_y(g):
                U = unit[g % 2]
                wait(dve, S["mb_hi"], 2 * g)
                wait(dve, S["mb_lo"], 2 * g)
                dve.wait_ge(S["mb_ym"], 4 * g + 4)
                dve.wait_ge(S["mb_silu"], 6 * g + 6)
                for v in range(2):
                    STT(s_y[:, v, :], U[:, 2 + v, :], pc("mbd", 2 * g + v), (b6, b7)[v][:, :],
                        ALU.mult, ALU.add).then_inc(S["mb_y"], 1)
                    dve.wait_ge(S["mb_y"], 6 * g + 2 * v + 1)
                    TT(s_y[:, v, :], s_y[:, v, :], U[:, 4 + v, :], ALU.mult).then_inc(S["mb_y"], 1)

            def mb_norm(g):
                dve.wait_ge(S["mb_rs"], 2 * g + 2)
                dve.wait_ge(S["mb_sq"], 2 * g + 2)
                for v in range(2):
                    STT(s_y[:, v, :], s_y[:, v, :], pc("mbg", 2 * g + v), s_rs[:, :], ALU.mult, ALU.mult
                        ).then_inc(S["mb_y"], 1)

            def mb_lo(g):
                for v in range(2):
                    dve.wait_ge(S["mb_hi"], 2 * g + v + 1)
                    dve.wait_ge(S["mb_y"], 6 * g + 4 + v + 1)
                    TT(yl[:, 2 * g + v, :], s_y[:, v, :], yh[:, 2 * g + v, :].bitcast(F32), ALU.subtract
                       ).then_inc(S["mb_lo"], 1)

            gates(0, J_G0)
            for u in range(ML_HEADS):
                last = u + 1 == ML_HEADS
                for part in range(4):
                    for i in tiles_before(part, 6):
                        if last and i < 4:
                            conv4(J_MB0 + i, unit[0][:, i, :], "mbcw", "mbcb", (8, 12, 0, 1)[i])
                        elif not last and i < 2:
                            conv4(ml_slab(u + 1) + i, unit[1 - u % 2][:, i, :], "mlcw", "mlcb", 4 * i + u + 1)
                    ml_part(part, u)
                    if part == 0 and u:
                        ml_end(u - 1)
            ml_end(ML_HEADS - 1)
            gates(1, J_G1)
            for g in range(MB_GROUPS):
                mb_xdt(g)
                for h in range(5):
                    if h < 4:
                        mb_head(g, h)
                    if h == 0 and g:
                        mb_lo(g - 1)
                    if h and g + 1 < MB_GROUPS:
                        conv4(mb_slab(g + 1) + h - 1, unit[1 - g % 2][:, h - 1, :], "mbcw", "mbcb",
                              (8 + g + 1, 12 + g + 1, 2 * g + 2, 2 * g + 3)[h - 1])
                    if h < 4:
                        mb_weights(g, h)
                mb_y(g)
                mb_norm(g)
            mb_lo(MB_GROUPS - 1)
            with dve.Fori(0, KT // 4) as it:
                for f in range(4):
                    t = J_G2 + KT + f
                    fo = it * 4 + f
                    dve.wait_ge(S["slab_used"], it * 4 + (t + 1))
                    dve.wait_ge(S["g_tanh"], it * 4 + (f + 1))
                    dve.wait_ge(S["g_acc"], it * 4 + (f + KT))
                    STT(tm[:, :], tile_of(gbuf, fo), 1.0, acc[t % 2][:, :], ALU.add, ALU.mult
                        ).then_inc(acc_free[t % 2], 1)
                    filled(dve, t, it, 4)
                    TT(tile_of(mixed, fo), tile_of(mixed, fo), tm[:, :], ALU.add).then_inc(S["g_acc"], 1)
                    dve.wait_ge(S["o_hi"], it * 4 + (f + 1))
                    STT(tile_of(hl, fo), tile_of(mixed, fo), 0.5, tile_of(hh, fo).bitcast(F32),
                        ALU.mult, ALU.subtract).then_inc(S["o_lo"], 1)

            def add_residual(j0, used, m):
                for f in range(KT):
                    t = j0 + f
                    dve.wait_ge(S["slab_used"], used(f))
                    TT(xT[:, f, :], xT[:, f, :], acc[t % 2][:, :], ALU.add).then_inc(acc_free[t % 2], 1)
                    for q in range(m):
                        if f >= 2:
                            add_squares(m, f - 1, q)

            def add_squares(m, f, q):
                dve.wait_ge(S["lt_sq"], 8 * (m - 1) + f * m + q + 1)
                if f > 1:
                    dve.wait_ge(S["lt_add"], 6 * (m - 1) + (f - 2) * m + q + 1)
                TT(lt_sum[m][q][:, :], lt_sum[m][q][:, :], lt_new[m][q][f % 2][:, :], ALU.add
                   ).then_inc(S["lt_add"], 1)

            add_residual(J_O, lambda f: J_O + f + 1, 1)
            dve.wait_ge(S["nrm_rs"], 4)
            norm_scale(1, lambda f: pc("norm2", f), rsn)
            with dve.Fori(0, NF // 2) as it:
                for p in range(2):
                    j = it * 2 + p
                    for v, buf in ((0, f_g), (1, f_v)):
                        bank = acc[(J_UP + v) % 2]
                        w0 = it * 6 + (3 * NF * v + 3 * p)
                        d = buf[p]
                        dve.wait_ge(S["up_c"], it * 4 + (2 * p + v + 1))
                        STT(d[:, 1:], bank[:, 0:T - 1], pc("fcw", w0 + 1), d[:, 1:], ALU.mult, ALU.add
                            ).then_inc(S["up_s1"], 1)
                        dve.wait_ge(S["up_s1"], it * 4 + (2 * p + v + 1))
                        STT(d[:, 2:], bank[:, 0:T - 2], pc("fcw", w0), d[:, 2:], ALU.mult, ALU.add
                            ).then_inc(acc_free[(J_UP + v) % 2], 1)
                    dve.wait_ge(S["up_sg"], j + 1)
                    filled(dve, J_UP + 2 * p + 1, it, 4)
                    TT(f_s[p][:, :], f_s[p][:, :], f_v[p][:, :], ALU.mult).then_inc(S["up_a"], 1)
                    dve.wait_ge(S["up_hi"], j + 1)
                    TT(tile_of(fl, j), f_s[p][:, :], tile_of(fh, j).bitcast(F32), ALU.subtract
                       ).then_inc(S["up_lo"], 1)
            add_residual(J_DN, lambda f: J_DN + 3 * f + 3, 2)
            dve.wait_ge(S["nrm_rs"], 6)
            dve.wait_ge(S["lt_ss"], 3)
            TT(sqn[1][:, :], rsn[:, :], rsn[:, :], ALU.mult).then_inc(S["lt_step"], 1)
            dve.wait_ge(S["lt_step"], 1)
            TT(sqn[1][:, :], sqn[1][:, :], b7[:, :], ALU.mult).then_inc(S["lt_step"], 1)
            dve.wait_ge(S["nrm_rs"], 8)
            TT(sqn[0][:, :], sqn[0][:, :], rsn[:, :], ALU.mult).then_inc(S["lt_step"], 1)
            dve.wait_ge(S["lt_step"], 3)
            norm_scale(2, lambda f: gg[:, f:f + 1], sqn[0])
            for f in range(KT):
                STT(xT[:, f, :], xT[:, f, :], pc("final", f), rsn[:, :], ALU.mult, ALU.mult).then_inc(S["x2_done"], 1)
            dve.memset(a_k[0][64:P, :], 0.0).then_inc(S["kz_set"], 1)
            dve.memset(a_k[1][0:64, :], 0.0).then_inc(S["kz_set"], 1)
            dve.wait_ge(S["kz_set"], 2)
            dve.wait_ge(S["wb_in"], 16)

            def at_norms(t):
                U = au[t % 2]
                wait(dve, S["at_s"], 8 * t)
                dve.wait_ge(S["at_rs"], 4 * t + 2)
                STT(a_q[:, :], U[:, 0, :], pc("qn"), a_rs[:, 0, :], ALU.mult, ALU.mult).then_inc(S["at_n"], 1)
                dve.wait_ge(S["at_rs"], 4 * t + 4)
                for h in range(2):
                    r = slice(64 * h, 64 * h + 64)
                    STT(a_k[h][r, :], U[r, 1, :], par[r, PAR["kn"]:PAR["kn"] + 1], a_rs[r, 1, :],
                        ALU.mult, ALU.mult).then_inc(S["at_n"], 1)

            def at_logits(i, t):
                n = 8 * t + i
                head, qb = 2 * t + i // 4, i % 4
                dve.wait_ge(S["at_s"], n + 1)
                wait(dve, S["at_tr"], n - 3)
                STT(a_l[i % 4][:, :], (b5, b6)[i % 2][:, :], AT_DH ** -0.5,
                    wb[:, head, (3 - qb) * P:(3 - qb) * P + T], ALU.mult, ALU.add).then_inc(S["at_l"], 1)
                dve.wait_ge(S["at_l"], n + 1)
                dve.tensor_reduce(a_st[:, i, 0:1], a_l[i % 4][:, :], AX_X, ALU.max, negate=True
                                  ).then_inc(S["at_mx"], 1)

            def at_normalise(i, t):
                n = 8 * t + i
                dve.wait_ge(S["at_ex"], n + 1)
                dve.reciprocal(a_st[:, i, 2:3], a_st[:, i, 1:2]).then_inc(S["at_sum"], 1)
                dve.wait_ge(S["at_sum"], n + 1)
                TS(a_l[i % 4][:, :], a_l[i % 4][:, :], a_st[:, i, 2:3], None, ALU.mult).then_inc(S["at_p"], 1)

            def at_end(t):
                dve.wait_ge(S["at_o"], 8 * t + 8)
                dve.wait_ge(S["at_silu"], t + 1)
                wait(dve, S["at_hi"], t)
                wait(dve, S["at_lo"], t)
                TT(a_y[:, :], b7[:, :], au[t % 2][:, 3, :], ALU.mult).then_inc(S["at_y"], 1)

            def at_lo(t):
                dve.wait_ge(S["at_hi"], t + 1)
                dve.wait_ge(S["at_y"], t + 1)
                TT(yl[:, 4 + t, :], a_y[:, :], yh[:, 4 + t, :].bitcast(F32), ALU.subtract).then_inc(S["at_lo"], 1)

            def cv_product(t):
                j = cv_slab(t, 2)
                filled(dve, cv_slab(t, 0) - DN_SHIFT)
                dve.wait_ge(S["slab_used"], j + 1)
                TT(c_u[:, :], c_u[:, :], acc[j % 2][:, :], ALU.mult).then_inc(acc_free[j % 2], 1)

            def cv_conv(t):
                n = 5 * t
                filled(dve, cv_slab(t, 2) - DN_SHIFT)
                wait(dve, S["cv_hi"], t)
                wait(dve, S["cv_lo"], t)
                TS(c_y[:, :], c_u[:, :], pc("cw2", 3 * t + 1), pc("cb2", t), ALU.mult, ALU.add
                   ).then_inc(S["cv_y"], 1)
                dve.wait_ge(S["cv_y"], n + 1)
                STT(c_y[:, 1:], c_u[:, 0:T - 1], pc("cw2", 3 * t), c_y[:, 1:], ALU.mult, ALU.add
                    ).then_inc(S["cv_y"], 1)
                dve.wait_ge(S["cv_y"], n + 2)
                STT(c_y[:, 0:T - 1], c_u[:, 1:], pc("cw2", 3 * t + 2), c_y[:, 0:T - 1], ALU.mult, ALU.add
                    ).then_inc(S["cv_y"], 1)
                filled(dve, cv_slab(t, 1) - DN_SHIFT)
                dve.wait_ge(S["cv_y"], n + 3)
                TT(c_y[:, :], c_y[:, :], c_b[:, :], ALU.mult).then_inc(S["cv_y"], 1)

            def cv_end(t):
                dve.wait_ge(S["cv_z"], t + 1)
                dve.wait_ge(S["cv_y"], 5 * t + 4)
                TT(c_y[:, :], c_y[:, :], c_z[:, :], ALU.mult).then_inc(S["cv_y"], 1)

            def cv_lo(t):
                dve.wait_ge(S["cv_hi"], t + 1)
                dve.wait_ge(S["cv_y"], 5 * t + 5)
                TT(yl[:, t, :], c_y[:, :], yh[:, t, :].bitcast(F32), ALU.subtract).then_inc(S["cv_lo"], 1)

            for n in range(2 * AT_HEADS):
                t, part = n // 4, n % 4
                if part == 0:
                    if t:
                        cv_end(t - 1)
                    at_norms(t)
                    if t:
                        at_end(t - 1)
                elif part == 2:
                    cv_product(t)
                items = (2 * part, 2 * part + 1)
                for i in items:
                    at_logits(i, t)
                for i in items:
                    at_normalise(i, t)
                if part == 1 and t:
                    at_lo(t - 1)
                    cv_lo(t - 1)
                elif part == 2:
                    cv_conv(t)
            cv_end(3)
            cv_lo(3)
            at_end(3)
            at_lo(3)
            dve.wait_ge(S["x2_done"], 9)
            with dve.Fori(0, KT // 4) as it:
                for f in range(4):
                    t = J_O2 - DN_SHIFT + f
                    dve.wait_ge(S["slab_used"], it * 4 + (J_O2 + f + 1))
                    fo = it * 4 + f
                    TT(tile_of(xT, fo), tile_of(xT, fo), acc[t % 2][:, :], ALU.add).then_inc(acc_free[t % 2], 1)


def bucket(rel):
    n = np.abs(rel)
    nf = np.maximum(n, 1).astype(np.float32)
    large = 8 + (np.log(nf / np.float32(8)) / np.float32(np.log(128.0)) * np.float32(8)).astype(np.int32)
    return np.where(rel > 0, 16, 0) + np.where(n < 8, n, np.minimum(large, 15))


def constants():
    c = np.zeros((P, N_CONST), np.float32)
    i = np.arange(P)
    eye = np.eye(P, dtype=np.float32)
    c[:, K_ID:K_ID + P] = eye
    c[:, K_ONES:K_ONES + P] = 1
    c[:, K_BD:K_BD + P] = (i[:, None] // AT_DH) == (i[None] // AT_DH)
    for h in range(ML_HEADS):
        c[ROW_I + h, K_SELI + ROW_I + h] = 1
        c[ROW_I + h, K_SEL2 + h] = c[ROW_F + h, K_SEL2 + h] = 1
        c[ROW_F + h, K_NSELF + ROW_I + h] = -1
    c[:, K_CLAMP:K_CLAMP + P] = np.where(i[:, None] <= i[None], 0.0, NEG)
    for l in range(1, 8):
        n, half = P >> (l - 1), P >> l
        s, node = i[:, None], np.arange(P // n).repeat(half)[None]
        k = K_LMASK + (l - 1) * P // 2
        c[:, k:k + P // 2] = (s // n == node) & (s % n < half)
    start = np.where(np.arange(T) % P == 0, 0.0, 1.0)
    c[:, K_HGMASK:K_HGMASK + T] = start
    c[:, K_RMASK:K_RMASK + T] = 1
    c[:ROW_I, K_RMASK:K_RMASK + T] = start
    c[:, K_SIGN] = 1
    c[ROW_F:ROW_F + 32, K_SIGN] = -1
    hot = np.zeros((P, W_LINE), np.float32)
    d = np.arange(1 - T, T)
    hot[bucket(d), np.arange(2 * T - 1)] = 1
    count = (np.abs(d) <= 64) * 1 + ((d % 4 == 0) & (np.abs(d) <= 256)) + (d % 16 == 0)
    hot[32, :2 * T - 1] = np.where(count > 0, np.log(np.maximum(count, 1)), NEG)
    return c, hot


def slabs_of(i):
    w_in, w_up, w_dn, w2 = i["w_in"][0], i["w_up"][0], i["w_down"][0], i["w_in_2"]
    br = (i["w_br_hg"][0], i["w_br_ml"][0], i["w_br_mb"][0])
    a = np.zeros((N_SLABS, P, KT * P), np.float32)

    def put(j, w, c, k0=0, n=KT):
        a[j].reshape(P, KT, P)[:, :n] = w[k0 * P:(k0 + n) * P, c:c + P].reshape(n, P, P).transpose(1, 0, 2)

    small = a[J_SMALL].reshape(P, KT, P)
    for row, c, n in ((ROW_DT, C_MBDT, MB_HEADS), (ROW_I, C_MLIF, ML_HEADS), (ROW_F, C_MLIF + ML_HEADS, ML_HEADS)):
        small[:, :, row:row + n] = w_in[:, c:c + n].reshape(KT, P, n).transpose(1, 0, 2)
    for u in range(HG_HEADS):
        for k, c in enumerate((C_HGF, C_HGQ, C_HGG, C_HGI)):
            put(J_HG + 4 * u + k, w_in, c + P * u)
    for u in range(ML_HEADS):
        for k, c in enumerate((C_MLQ + P * u, C_MLK + P * u, C_MLV + 2 * P * u, C_MLV + 2 * P * u + P,
                               C_MLO + 2 * P * u, C_MLO + 2 * P * u + P)):
            put(ml_slab(u) + k, w_in, c)
    for g in range(MB_GROUPS):
        for k, c in enumerate((C_MBX + 1024 + P * g, C_MBX + 1536 + P * g, C_MBX + 2 * P * g, C_MBX + 2 * P * g + P,
                               C_MBZ + 2 * P * g, C_MBZ + 2 * P * g + P)):
            put(mb_slab(g) + k, w_in, c)
    for b, j in enumerate((J_G0, J_G1, J_G2)):
        for f in range(KT):
            put(j + (2 * f if b < 2 else f), w_in, C_GATE + D * b + P * f)
            put(j + (2 * f + 1 if b < 2 else KT + f), br[b], P * f)
    for f in range(KT):
        put(J_O + f, i["w_out"][0], P * f)
        put(J_O2 + f, i["w_out_2"], P * f)
        for c, n in enumerate(DN_CHUNKS):
            put(J_DN + 3 * f + c, w_dn, P * f, 8 * c, n)
    for j in range(NF):
        put(J_UP + 2 * j, w_up, P * j)
        put(J_UP + 2 * j + 1, w_up, D_FF + P * j)
    for t in range(4):
        for k in range(4):
            put(cv_slab(t, k), w2, 512 * k + P * t)
            put(at_slab(t, k), w2, 2048 + 512 * k + P * t)
    return a


def params_of(i):
    a = np.zeros((P, N_PAR), np.float32)

    def put(name, v):
        a[:, PAR[name]:PAR[name] + v.shape[1]] = v

    def cols(v):
        return v.reshape(-1, P).T

    def taps(w):
        return w.reshape(w.shape[0], -1, P).transpose(2, 1, 0).reshape(P, -1)

    put("norm1", cols(i["norm1_g"]))
    put("norm2", cols(i["norm2_g"]))
    put("final", cols(i["final_g"]))
    put("normw2", cols(i["norm_w_2"]))
    put("lb", cols(i["hg_lb_logits"]))
    put("hgg", cols(i["hg_norm_g"]))
    put("mlcw", taps(i["ml_conv_w"][0]))
    put("mlcb", cols(i["ml_conv_b"]))
    put("mlg", cols(i["ml_norm_g"]))
    put("mbcw", taps(i["mb_conv_w"][0]))
    put("mbcb", cols(i["mb_conv_b"]))
    put("mbg", cols(i["mb_norm_g"]))
    put("mbd", cols(np.repeat(i["mb_d"].reshape(-1), 64)))
    put("fcw", taps(i["ffn_conv_w"][0]))
    put("fcb", cols(i["ffn_conv_b"]))
    put("cw2", taps(i["conv_w_2"]))
    put("cb2", cols(i["conv_b_2"]))
    put("qn", cols(np.tile(i["q_norm_w_2"], 2)))
    put("kn", cols(np.tile(i["k_norm_w_2"], 2)))
    a[ROW_DT:ROW_DT + MB_HEADS, PAR["rowb"]] = i["mb_dt_bias"][0]
    a[ROW_I:ROW_I + ML_HEADS, PAR["rowb"]] = i["ml_gate_b"][0, :ML_HEADS]
    a[ROW_F:ROW_F + ML_HEADS, PAR["rowb"]] = i["ml_gate_b"][0, ML_HEADS:]
    a[ROW_DT:ROW_DT + MB_HEADS, PAR["alog"]] = i["mb_a_log"][0]
    a[:32, PAR["rel"]:PAR["rel"] + AT_HEADS] = i["rel_bias_2"]
    a[32, PAR["rel"]:PAR["rel"] + AT_HEADS] = 1
    return a


def kernel(**inputs):
    import concourse.bacc as bacc
    from concourse.bass_utils import run_bass_kernel_spmd

    i = {k: np.asarray(v) for k, v in inputs.items()}
    con, hot = constants()
    arrays = {"slabs": slabs_of(i), "x": np.ascontiguousarray(i["x"]), "params": params_of(i), "consts": con,
              "onehot": hot}
    nc = bacc.Bacc("TRN2", target_bir_lowering=False, num_devices=1)
    ins = [nc.dram_tensor(n, a.shape, F32, kind="ExternalInput").ap() for n, a in arrays.items()]
    bias_scratch = nc.dram_tensor("bias_scratch", (AT_HEADS, P, W_LINE), F32).ap()
    out = nc.dram_tensor("out", (1, T, D), F32, kind="ExternalOutput").ap()
    build(nc, *ins, bias_scratch, out)
    r = run_bass_kernel_spmd(nc, [arrays], core_ids=[0])
    return r.results[0]["out"]
```
